# Optimizing a Trainium2 kernel written in Bass

```python
import jax, jax.numpy as jnp
from jax import lax
import numpy as np

D_MODEL = 1024
BATCH = 1
SEQ = 256
DEPTH = 2
DEC_BATCH = 8
DEC_SEQ = 1
PAST_LEN = 2048
PAGE_SIZE = 128

N_LAYERS_A = (DEPTH + 1) // 2
N_LAYERS_B = DEPTH // 2
DN_HEADS = 8
DN_DK = 128
DN_DV = 128
DN_QK_W = DN_HEADS * DN_DK
DN_V_W = DN_HEADS * DN_DV
CONV_WIDTH = 4
CONV_CH = 2 * DN_QK_W + DN_V_W
CHUNK = 64
POOL_WINDOWS = (2, 4, 8, 16)
POOL_GROUPS = len(POOL_WINDOWS)
POOL_W = D_MODEL
POOL_GW = POOL_W // POOL_GROUPS
POOL_BUF = max(POOL_WINDOWS) - 1
N_MEM = 256
X_HEADS = 4
X_DH = 128
X_W = X_HEADS * X_DH
D_FF = 2816
N_EXPERTS = 8
TOP_K = 2
D_FF_EXPERT = 3584
A_IN_W = CONV_CH + DN_V_W + 2 * DN_HEADS + X_W
A_MIX_W = DN_V_W + X_W
B_IN_W = POOL_W + X_W
B_MIX_W = POOL_W + X_W
EPS = 1e-6

kernel_name = "hybrid_deltanet_pool_memxattn_decode_step"

def rmsnorm(x, w):
    xf = x.astype(jnp.float32)
    y = xf * lax.rsqrt(jnp.mean(xf * xf, axis=-1, keepdims=True) + EPS)
    return (y * w.astype(jnp.float32)).astype(x.dtype)

def l2norm(x):
    return x * lax.rsqrt(jnp.sum(x * x, axis=-1, keepdims=True) + EPS)

def swiglu(x, wi, wo):
    a, b = jnp.split(x @ wi, 2, axis=-1)
    return (jax.nn.silu(a) * b) @ wo

def causal_short_conv(xs_new, buf, w):
    t = xs_new.shape[1]
    xc = jnp.concatenate([buf.astype(xs_new.dtype), xs_new], axis=1)
    y = xc[:, 0:t] * w[0]
    for j in range(1, CONV_WIDTH):
        y = y + xc[:, j:j + t] * w[j]
    return jax.nn.silu(y), xc[:, -(CONV_WIDTH - 1):]

def gated_delta_chunked(q, k, v, g, beta, s0):
    b, t, h, _ = q.shape
    dv = v.shape[-1]
    n = t // CHUNK

    def chunks(a):
        a = a.reshape(b, n, CHUNK, h, *a.shape[3:])
        return jnp.moveaxis(a, (1, 3), (0, 2))

    qc, kc, vc, gc, bc = (chunks(a) for a in (q, k, v, g, beta))
    G = jnp.cumsum(gc, axis=-1)
    idx = jnp.arange(CHUNK)
    incl = idx[:, None] >= idx[None, :]
    strict = idx[:, None] > idx[None, :]
    decay = jnp.exp(jnp.where(incl, G[..., :, None] - G[..., None, :], -jnp.inf))
    kk = jnp.einsum('nbhid,nbhjd->nbhij', kc, kc)
    m = jnp.where(strict, bc[..., :, None] * kk * decay, 0.0)
    a_mat = m + jnp.eye(CHUNK, dtype=m.dtype)
    rhs = jnp.concatenate([vc * bc[..., None], kc * (bc * jnp.exp(G))[..., None]], axis=-1)
    sol = lax.linalg.triangular_solve(a_mat, rhs, left_side=True, lower=True, unit_diagonal=True)
    w_val, k_cd = sol[..., :dv], sol[..., dv:]
    qk = jnp.einsum('nbhid,nbhjd->nbhij', qc, kc) * decay
    q_dec = qc * jnp.exp(G)[..., None]
    g_last = G[..., -1:]
    k_tail = kc * jnp.exp(g_last - G)[..., None]
    c_decay = jnp.exp(g_last[..., 0])

    def step(s, xs):
        w_n, kcd_n, qk_n, qd_n, kt_n, cd_n = xs
        u = w_n - jnp.einsum('bhck,bhkv->bhcv', kcd_n, s)
        o = jnp.einsum('bhck,bhkv->bhcv', qd_n, s) + jnp.einsum('bhij,bhjv->bhiv', qk_n, u)
        s = s * cd_n[..., None, None] + jnp.einsum('bhck,bhcv->bhkv', kt_n, u)
        return s, o

    s_fin, o = lax.scan(step, s0, (w_val, k_cd, qk, q_dec, k_tail, c_decay))
    o = jnp.moveaxis(o, (0, 2), (1, 3)).reshape(b, t, h, dv)
    return o, s_fin

def gated_delta_recurrent(q, k, v, g, beta, s0):
    def step(s, xs):
        q_t, k_t, v_t, g_t, b_t = xs
        s = s * jnp.exp(g_t)[..., None, None]
        u = b_t[..., None] * (v_t - jnp.einsum('bhk,bhkv->bhv', k_t, s))
        s = s + jnp.einsum('bhk,bhv->bhkv', k_t, u)
        return s, jnp.einsum('bhk,bhkv->bhv', q_t, s)

    xs = tuple(jnp.moveaxis(a, 1, 0) for a in (q, k, v, g, beta))
    s_fin, o = lax.scan(step, s0, xs)
    return jnp.moveaxis(o, 0, 1), s_fin

def gated_deltanet(qkv, z, b_logit, a_logit, conv_buf, s0, conv_w, a_log, dt_bias, o_norm, chunked):
    bsz, t, _ = qkv.shape
    act, conv_new = causal_short_conv(qkv, conv_buf, conv_w)
    act = act.astype(jnp.float32)
    q, k, v = jnp.split(act, [DN_QK_W, 2 * DN_QK_W], axis=-1)
    q = l2norm(q.reshape(bsz, t, DN_HEADS, DN_DK)) * (DN_DK ** -0.5)
    k = l2norm(k.reshape(bsz, t, DN_HEADS, DN_DK))
    v = v.reshape(bsz, t, DN_HEADS, DN_DV)
    beta = jax.nn.sigmoid(b_logit.astype(jnp.float32))
    g = -jnp.exp(a_log.astype(jnp.float32)) * jax.nn.softplus(
        a_logit.astype(jnp.float32) + dt_bias.astype(jnp.float32))
    s0 = s0.astype(jnp.float32)
    if chunked:
        o, s_fin = gated_delta_chunked(q, k, v, g, beta, s0)
    else:
        o, s_fin = gated_delta_recurrent(q, k, v, g, beta, s0)
    o = o * lax.rsqrt(jnp.mean(o * o, axis=-1, keepdims=True) + EPS) * o_norm.astype(jnp.float32)
    o = o * jax.nn.silu(z.reshape(bsz, t, DN_HEADS, DN_DV).astype(jnp.float32))
    return o.reshape(bsz, t, DN_V_W).astype(qkv.dtype), s_fin, conv_new

def multiscale_pool(u_new, u_prev, start_pos, pool_w, pool_scale):
    bsz, t, c = u_new.shape
    p = u_prev.shape[1]
    u = jnp.concatenate([u_prev.astype(u_new.dtype), u_new], axis=1)
    cs = jnp.concatenate([jnp.zeros((bsz, 1, c), jnp.float32),
                          jnp.cumsum(u.astype(jnp.float32), axis=1)], axis=1)
    hi = p + 1 + jnp.arange(t)
    pos = start_pos + jnp.arange(t)
    outs = []
    for gi, w in enumerate(POOL_WINDOWS):
        sl = slice(gi * POOL_GW, (gi + 1) * POOL_GW)
        lo = jnp.maximum(hi - w, 0)
        cnt = jnp.minimum(pos + 1, w).astype(jnp.float32)
        mean = (cs[:, hi, sl] - cs[:, lo, sl]) / cnt[None, :, None]
        outs.append(mean - u_new[..., sl].astype(jnp.float32))
    d = jnp.stack(outs, axis=2)
    mixed = jnp.einsum('btgc,gcd->btgd', d, pool_w.astype(jnp.float32)).reshape(bsz, t, c)
    return (mixed * pool_scale.astype(jnp.float32)).astype(u_new.dtype), u[:, -POOL_BUF:]

def mem_kv(mem, norm_w, w_k, w_v):
    bsz, n, _ = mem.shape
    m = rmsnorm(mem, norm_w)
    return (m @ w_k).reshape(bsz, n, X_HEADS, X_DH), (m @ w_v).reshape(bsz, n, X_HEADS, X_DH)

def memory_attention(cq, mk, mv):
    bsz, t, _ = cq.shape
    q = cq.reshape(bsz, t, X_HEADS, X_DH)
    s = jnp.einsum('bthd,bmhd->bhtm', q, mk.astype(q.dtype)).astype(jnp.float32) * (X_DH ** -0.5)
    p = jax.nn.softmax(s, axis=-1).astype(q.dtype)
    o = jnp.einsum('bhtm,bmhd->bthd', p, mv.astype(q.dtype))
    return o.reshape(bsz, t, X_W)

def moe_swiglu(x, router_w, wi, wo):
    logits = (x @ router_w).astype(jnp.float32)
    top_v, top_i = lax.top_k(logits, TOP_K)
    gates = jax.nn.softmax(top_v, axis=-1)
    dispatch = jnp.sum(jax.nn.one_hot(top_i, N_EXPERTS, dtype=jnp.float32) * gates[..., None], axis=-2)
    y = jnp.zeros_like(x)
    for e in range(N_EXPERTS):
        y = y + dispatch[..., e:e + 1].astype(x.dtype) * swiglu(x, wi[e], wo[e])
    return y

def layer_a(x, mk, mv, s0, conv_buf, norm1, w_in, conv_w, a_log, dt_bias, o_norm, w_out,
            norm2, ffn_wi, ffn_wo, chunked):
    u = rmsnorm(x, norm1)
    proj = u @ w_in
    o1 = CONV_CH
    o2 = o1 + DN_V_W
    o3 = o2 + DN_HEADS
    o4 = o3 + DN_HEADS
    qkv, z, b_logit, a_logit, cq = jnp.split(proj, [o1, o2, o3, o4], axis=-1)
    dn, s_fin, conv_new = gated_deltanet(qkv, z, b_logit, a_logit, conv_buf, s0, conv_w,
                                         a_log, dt_bias, o_norm, chunked)
    xa = memory_attention(cq, mk, mv)
    h = x + jnp.concatenate([dn, xa], axis=-1) @ w_out
    h = h + swiglu(rmsnorm(h, norm2), ffn_wi, ffn_wo)
    return h, s_fin, conv_new

def layer_b(x, mk, mv, pool_prev, start_pos, norm1, w_in, pool_w, pool_scale, w_out,
            norm2, router_w, moe_wi, moe_wo):
    u = rmsnorm(x, norm1)
    proj = u @ w_in
    up, cq = jnp.split(proj, [POOL_W], axis=-1)
    pm, buf = multiscale_pool(up, pool_prev, start_pos, pool_w, pool_scale)
    xa = memory_attention(cq, mk, mv)
    h = x + jnp.concatenate([pm, xa], axis=-1) @ w_out
    h = h + moe_swiglu(rmsnorm(h, norm2), router_w, moe_wi, moe_wo)
    return h, buf

def setup_inputs(seed: int = 0) -> dict:
    key = jax.random.key(seed)
    ks = iter(jax.random.split(key, 40))

    def nrm(shape, scale):
        return jax.random.normal(next(ks), shape, jnp.float32) * scale

    def gain(shape):
        return 1.0 + nrm(shape, 0.1)

    na, nb = N_LAYERS_A, N_LAYERS_B
    return {
        'x_prompt': nrm((BATCH, SEQ, D_MODEL), 1.0),
        'x_sample': nrm((DEC_BATCH, DEC_SEQ, D_MODEL), 1.0),
        'state_dn': nrm((na, DEC_BATCH, DN_HEADS, DN_DK, DN_DV), 0.1),
        'state_dn_conv': nrm((na, DEC_BATCH, CONV_WIDTH - 1, CONV_CH), 1.0),
        'state_pool': nrm((nb, DEC_BATCH, POOL_BUF, POOL_W), 1.0),
        'cache_mem_k': nrm((DEPTH, DEC_BATCH, N_MEM, X_HEADS, X_DH), 1.0),
        'cache_mem_v': nrm((DEPTH, DEC_BATCH, N_MEM, X_HEADS, X_DH), 1.0),
        'mem_prompt': nrm((BATCH, N_MEM, D_MODEL), 1.0),
        'a_norm1': gain((na, D_MODEL)),
        'a_w_in': nrm((na, D_MODEL, A_IN_W), D_MODEL ** -0.5),
        'a_conv_w': nrm((na, CONV_WIDTH, CONV_CH), CONV_WIDTH ** -0.5),
        'a_a_log': jnp.log(jax.random.uniform(next(ks), (na, DN_HEADS), jnp.float32, 1.0, 16.0)),
        'a_dt_bias': -4.0 + nrm((na, DN_HEADS), 0.5),
        'a_o_norm': gain((na, DN_DV)),
        'a_w_out': nrm((na, A_MIX_W, D_MODEL), A_MIX_W ** -0.5),
        'a_norm2': gain((na, D_MODEL)),
        'a_ffn_wi': nrm((na, D_MODEL, 2 * D_FF), D_MODEL ** -0.5),
        'a_ffn_wo': nrm((na, D_FF, D_MODEL), D_FF ** -0.5),
        'b_norm1': gain((nb, D_MODEL)),
        'b_w_in': nrm((nb, D_MODEL, B_IN_W), D_MODEL ** -0.5),
        'b_pool_w': nrm((nb, POOL_GROUPS, POOL_GW, POOL_GW), POOL_GW ** -0.5),
        'b_pool_scale': gain((nb, POOL_W)),
        'b_w_out': nrm((nb, B_MIX_W, D_MODEL), B_MIX_W ** -0.5),
        'b_norm2': gain((nb, D_MODEL)),
        'b_router': nrm((nb, D_MODEL, N_EXPERTS), D_MODEL ** -0.5),
        'b_moe_wi': nrm((nb, N_EXPERTS, D_MODEL, 2 * D_FF_EXPERT), D_MODEL ** -0.5),
        'b_moe_wo': nrm((nb, N_EXPERTS, D_FF_EXPERT, D_MODEL), D_FF_EXPERT ** -0.5),
        'm_norm': gain((DEPTH, D_MODEL)),
        'm_w_k': nrm((DEPTH, D_MODEL, X_W), D_MODEL ** -0.5),
        'm_w_v': nrm((DEPTH, D_MODEL, X_W), D_MODEL ** -0.5),
        'final_norm': gain((D_MODEL,)),
    }

def reference(x_prompt, x_sample, state_dn, state_dn_conv, state_pool, cache_mem_k, cache_mem_v,
              mem_prompt, a_norm1, a_w_in, a_conv_w, a_a_log, a_dt_bias, a_o_norm, a_w_out,
              a_norm2, a_ffn_wi, a_ffn_wo, b_norm1, b_w_in, b_pool_w, b_pool_scale, b_w_out,
              b_norm2, b_router, b_moe_wi, b_moe_wo, m_norm, m_w_k, m_w_v, final_norm):
    bp = x_prompt.shape[0]
    hp, hs = x_prompt, x_sample
    dn_p, conv_p, pool_p, mk_p_all, mv_p_all = [], [], [], [], []
    dn_s, conv_s, pool_s = [], [], []
    for i in range(DEPTH):
        j = i // 2
        mk_p, mv_p = mem_kv(mem_prompt, m_norm[i], m_w_k[i], m_w_v[i])
        mk_p_all.append(mk_p)
        mv_p_all.append(mv_p)
        mk_s, mv_s = cache_mem_k[i], cache_mem_v[i]
        if i % 2 == 0:
            wa = (a_norm1[j], a_w_in[j], a_conv_w[j], a_a_log[j], a_dt_bias[j], a_o_norm[j],
                  a_w_out[j], a_norm2[j], a_ffn_wi[j], a_ffn_wo[j])
            s0_p = jnp.zeros((bp, DN_HEADS, DN_DK, DN_DV), jnp.float32)
            c0_p = jnp.zeros((bp, CONV_WIDTH - 1, CONV_CH), hp.dtype)
            hp, s_p, c_p = layer_a(hp, mk_p, mv_p, s0_p, c0_p, *wa, chunked=True)
            hs, s_s, c_s = layer_a(hs, mk_s, mv_s, state_dn[j], state_dn_conv[j], *wa, chunked=False)
            dn_p.append(s_p.astype(hp.dtype))
            conv_p.append(c_p)
            dn_s.append(s_s.astype(hs.dtype))
            conv_s.append(c_s)
        else:
            wb = (b_norm1[j], b_w_in[j], b_pool_w[j], b_pool_scale[j], b_w_out[j], b_norm2[j],
                  b_router[j], b_moe_wi[j], b_moe_wo[j])
            p0_p = jnp.zeros((bp, 0, POOL_W), hp.dtype)
            hp, buf_p = layer_b(hp, mk_p, mv_p, p0_p, 0, *wb)
            hs, buf_s = layer_b(hs, mk_s, mv_s, state_pool[j], PAST_LEN, *wb)
            pool_p.append(buf_p)
            pool_s.append(buf_s)
    y_prompt = rmsnorm(hp, final_norm)
    y_sample = rmsnorm(hs, final_norm)
    new_state_dn_prompt = jnp.stack(dn_p)
    new_state_dn_conv_prompt = jnp.stack(conv_p)
    new_state_pool_prompt = jnp.stack(pool_p)
    new_cache_mem_k_prompt = jnp.stack(mk_p_all)
    new_cache_mem_v_prompt = jnp.stack(mv_p_all)
    new_state_dn_sample = jnp.stack(dn_s)
    new_state_dn_conv_sample = jnp.stack(conv_s)
    new_state_pool_sample = jnp.stack(pool_s)
    return (y_prompt, y_sample, new_state_dn_prompt, new_state_dn_conv_prompt, new_state_pool_prompt,
            new_cache_mem_k_prompt, new_cache_mem_v_prompt, new_state_dn_sample,
            new_state_dn_conv_sample, new_state_pool_sample)


_drawn_inputs = setup_inputs


def setup_inputs(seed=0):
    import zlib

    import numpy as np

    out = dict(_drawn_inputs(seed))
    spreads = {}
    factors = {}
    for name, (base, spread) in spreads.items():
        noise = np.random.default_rng([zlib.crc32(name.encode()), seed]).standard_normal(out[name].shape)
        drawn = base * np.exp(spread * noise) if base else spread * noise
        out[name] = __import__('jax').numpy.asarray(drawn.astype(out[name].dtype))
    for name, factor in factors.items():
        out[name] = (out[name] * factor).astype(out[name].dtype)
    return out
```

```python
from contextlib import ExitStack

import numpy as np
import concourse.bass as bass
from concourse import mybir

F32 = mybir.dt.float32
F32R = mybir.dt.float32r
I32 = mybir.dt.int32
ALU = mybir.AluOpType
ACT = mybir.ActivationFunctionType
AX = mybir.AxisListType.X

P = 128
D = 1024
KD = D // P
SEQ, NS = 256, 8
T = SEQ + NS
H = 8
NCH = SEQ // P
CW = 4
CT = 24
PRE = CW - 1 + SEQ + CW * NS
ACTW = PRE - (CW - 1)
S0 = SEQ + CW - 1
XH = 4
NM = 256
MT = NM // P
BH = NS * XH
DBH = NS * H
FF = 2816
FT = FF // P
E = 8
FE = 3584
FCN = FE // 512
KE = FE // P
C = P
ROUNDS = -(-T // C)
PW = 15
PCOL = PW + SEQ + (PW + 1) * NS
EPS = 1e-6
SLOT = 4096
RING = 7
RING_A = 3
PERX = 42
NUP, NDOWN = 28, 14
XCH = 2048
XRAW = 7
XSET = 3
assert PERX % XRAW == 0 and PERX % XSET == 0
TURNED = {4 * f + 10: f for f in range(FE // 512 - 1)} | {32: FE // 512 - 1}
NLVL = 7

DENSE = ([("a_in", i) for i in range(9)] + [("mkv", i) for i in range(4)]
         + [("kc0", i) for i in range(2)] + [("vc0", i) for i in range(2)]
         + [("state", i) for i in range(2)]
         + [("a_out", i) for i in range(4)] + [("wi", i) for i in range(11)]
         + [("wo", i) for i in range(8)] + [("b_in", i) for i in range(3)] + [("pool", 0)]
         + [("kc1", i) for i in range(2)] + [("vc1", i) for i in range(2)]
         + [("b_out", i) for i in range(4)])
ND = len(DENSE)
AT = {c: n for n, c in enumerate(DENSE)}
WIDTH = {"a_in": 4096, "mkv": 4096, "kc0": 4096, "vc0": 4096, "state": 4096, "a_out": 3072,
         "wi": 4096, "wo": FT * P, "b_in": 4096, "pool": 2048, "kc1": 4096, "vc1": 4096,
         "b_out": 3072}
assert ND % RING_A == 0

CIDENT, CTRI, CSTRI, CNEG, CLVL = 0, P, 2 * P, 3 * P, 4 * P
CIOTA = CLVL + NLVL * P
CTIE = CIOTA + P
CINV = CTIE + E * E
CN = CINV + 4 * 16
GA1, GA2, GB1, GB2, GFIN, GM0, GM1, GPS = (8 * i for i in range(8))
GON = 64
GTAP = 65
GALOG = GTAP + CT * CW
GDT = GALOG + H
GN = GDT + H


def build(nc, ins, outs):
    ctx = ExitStack()
    with ctx:
        def sb(name, n, dt=F32):
            return ctx.enter_context(nc.sbuf_tensor(name, [P, n], dt))

        def sem(name):
            return ctx.enter_context(nc.semaphore(name))

        consts = sb("consts", CN)
        gains = sb("gains", GN)
        wba = sb("wba", KD * 16)
        router = sb("router", KD * E)
        ones = sb("ones", P)
        epsc = sb("epsc", 1)
        small = sb("small", 840)
        nsteps_i = sb("nsteps_i", 1, I32)
        hbuf = sb("hbuf", KD * T)
        ubuf = sb("ubuf", KD * T)
        base = (nc.sbuf_base + 63) // 64 * 64
        sb("weights", RING * SLOT + 32)

        def at(name, off, n, dt):
            return nc.alloc_sbuf_tensor_at(name, [P, n], dt, offset=base + 4 * off)

        ring = at("ring", 0, RING * SLOT, F32)
        whi = [at(f"whi{i}", 2 * i * XCH, XCH, F32R) for i in range(XSET)]
        wlo = [at(f"wlo{i}", (2 * i + 1) * XCH, XCH, F32R) for i in range(XSET)]
        assert 2 * XSET * XCH <= RING_A * SLOT
        raw = at("raw", 2 * XSET * XCH, XRAW * XCH, F32)
        tail = (2 * XSET + XRAW) * XCH
        GEN = 1056 + 3168 + 4 * 1024 + 648 + 8100
        gbase = (nc.sbuf_base + 63) // 64 * 64
        sb("activations", GEN + 32)

        def gat_(name, off, n, dt=F32):
            return nc.alloc_sbuf_tensor_at(name, [P, n], dt, offset=gbase + 4 * off)

        gen = gat_("gen", 0, GEN)
        PP = [ctx.enter_context(nc.psum_tensor(f"PP{i}", [P, 1024], F32)) for i in range(4)]

        def bank(b):
            return PP[b // 2][:, (b % 2) * 512:(b % 2) * 512 + 512]

        ident = consts[:, CIDENT:CIDENT + P]
        tri = consts[:, CTRI:CTRI + P]
        stri = consts[:, CSTRI:CSTRI + P]
        neg = consts[:, CNEG:CNEG + P]
        iota = consts[:, CIOTA:CIOTA + P]
        h = hbuf[:, :].rearrange("p (k t) -> p k t", k=KD)
        u = ubuf[:, :].rearrange("p (k t) -> p k t", k=KD)

        def cut(buf, at, n):
            return buf[:, at:at + n]

        arena = RING_A * SLOT
        pre = cut(ring, arena, CT * PRE).rearrange("p (m c) -> p m c", m=CT)
        act = cut(ring, arena + CT * PRE, CT * ACTW).rearrange("p (m c) -> p m c", m=CT)
        z = cut(ring, arena + CT * (PRE + ACTW), H * T).rearrange("p (m c) -> p m c", m=H)
        assert CT * (PRE + ACTW) + H * T <= (RING - RING_A) * SLOT
        hid = cut(ring, arena, FT * T).rearrange("p (m c) -> p m c", m=FT)
        DTb, MTb, MLb, Xb, PTb, Sb = (cut(ring, arena + 1024 * i, 1024) for i in range(6))
        cq = cut(gen, 0, XH * T).rearrange("p (m c) -> p m c", m=XH)
        cat = cut(gen, 1056, 12 * T).rearrange("p (m c) -> p m c", m=12)
        mk = [cut(gen, 4224 + 2048 * i, 1024) for i in range(2)]
        mv = [cut(gen, 5248 + 2048 * i, 1024) for i in range(2)]
        convio = cut(gen, 8320, 648)
        SC = 8968
        SCN = GEN - SC
        memT = cut(gen, 1056, KD * NM).rearrange("p (k t) -> p k t", k=KD)
        sq = cut(gen, SC, KD * T)
        rt = cut(gen, SC + 2112, 264)
        rs = cut(gen, SC + 2376, 264)
        memn = [cut(gen, SC + 2640 + 2048 * i, 2048).rearrange("p (k t) -> p k t", k=KD) for i in range(2)]
        assert 2640 + 4096 <= SCN
        sqq = cut(gen, SC, 4 * ACTW)
        rsq = cut(gen, SC + 4 * ACTW, 4 * ACTW)
        Pr = cut(gen, SC, 2048)
        PrT = cut(gen, SC + 2048, 2048)
        STs = cut(gen, SC, 64)
        P32 = cut(gen, SC + 64, 256)
        PT32 = cut(gen, SC + 320, 64)
        Tb, Ub, vtok, ktail = (cut(gen, SC + 1024 * i, 1024) for i in range(4))
        DS = SC + 4096
        kq = cut(gen, DS, 128).rearrange("p (n c) -> p n c", c=2)
        v64 = cut(gen, DS + 128, 64)
        kqd = cut(gen, DS + 192, 64)
        t64 = cut(gen, DS + 256, 64)
        u64 = cut(gen, DS + 320, 64)
        qku = cut(gen, DS + 384, 64)
        krow = cut(gen, DS + 448, 128)
        urow = cut(gen, DS + 576, 128)
        ublk = [cut(gen, DS + 704 + 512 * i, 512) for i in range(2)]
        sil = [cut(gen, SC + 2640 + 264 * i, 264) for i in range(2)]
        pin = cut(gen, SC, KD * PCOL).rearrange("p (m c) -> p m c", m=KD)
        psm = cut(gen, SC + KD * PCOL, KD * PCOL).rearrange("p (m c) -> p m c", m=KD)
        poolbuf = cut(gen, SC + KD * PCOL, KD * NS * PW)
        assert 2 * KD * PCOL <= SCN
        pst = cut(gen, 4224, 8 * 135)
        pd = cut(gen, 1056, KD * T).rearrange("p (m c) -> p m c", m=KD)
        pfix = cut(small, 512, 128)

        xtok = cut(gen, 0, 3 * D).rearrange("p (t c) -> p t c", t=3)
        hTh = gat_("hTh", 3072, KE * C, F32R)
        hTl = gat_("hTl", 3072 + KE * C, KE * C, F32R)
        xsh = gat_("xsh", 10240, KD * C, F32R)
        xsl = gat_("xsl", 11264, KD * C, F32R)
        yslot = cut(gen, 12288, D)
        disp = cut(gen, 13312, 384).rearrange("p (t c) -> p t c", t=3)
        dispg = cut(gen, 13696, 384).rearrange("p (t c) -> p t c", t=3)
        comb = cut(gen, 14080, T)
        esil = [cut(ubuf, 512 * i, 512) for i in range(2)]
        hslot = [cut(ubuf, 1024 + 512 * i, 512) for i in range(2)]
        rout = cut(ring, tail, 3 * E)
        rtmp = cut(ring, tail + 32, 3 * E * E)
        rtm2 = cut(ring, tail + 224, 3 * E * E)
        rr = [cut(ring, tail + 416 + 24 * i, 24) for i in range(8)]
        NSTX = (ROUNDS + 1) * E
        posx = cut(ring, tail + 608, NSTX * 3).rearrange("p (s t) -> p s t", t=3)
        gatex = cut(ring, tail + 608 + NSTX * 3, NSTX * 3).rearrange("p (s t) -> p s t", t=3)
        cnt8 = cut(ring, tail + 608 + 6 * NSTX, 16)
        fsq = cut(gen, 14400, KD * T)
        frt = cut(gen, 16512, 264)
        frs = cut(gen, 16776, 264)

        gba = cut(small, 0, 48).rearrange("p (t c) -> p t c", t=3)
        gx, gax, ge, gl, gg, gb = (cut(small, 48 + 24 * i, 24).rearrange("p (t c) -> p t c", t=3)
                                   for i in range(6))
        gea = cut(small, 192, 8)
        gd = cut(small, 200, 128)
        cG, cnG, cdl, ceG, ctail, ceGl, cbeG = (cut(small, 328 + 16 * i, 16) for i in range(7))
        sgb = cut(small, 440, 128)
        amx = cut(small, 568, 8)
        anm = cut(small, 576, 8)
        asum = cut(small, 584, 8)
        ars = cut(small, 592, 8)
        sgt = cut(small, 600, 128)
        cgt = cut(small, 728, 32)

        raw_loaded = [sem(f"raw_loaded{i}") for i in range(XRAW)]
        slot_loaded = [sem(f"slot_loaded{i}") for i in range(RING_A)]
        names = {}

        def s(name):
            if name not in names:
                names[name] = sem(name)
            return names[name]

        block = ctx.enter_context(nc.Block())

        def read_by(n):
            kind, i = DENSE[n]
            return {"a_in": ("ain_mm", 4 * (i + 1)), "mkv": ("mkv_mm", 6 * (i // 2) + (4, 6)[i % 2]),
                    "kc0": ("cache_mm", i + 1), "vc0": ("cache_mm", i + 3), "state": ("state_mm", i + 1),
                    "a_out": ("aout_mm", 2 * (i + 1)), "wi": ("wi_mm", 2 * (i + 1)), "wo": ("wo_mm", i + 1),
                    "b_in": ("bin_mm", 4 * (i + 1)), "pool": ("pm_mm", 8),
                    "kc1": ("cache_mm", i + 5), "vc1": ("cache_mm", i + 7), "b_out": ("bout_mm", 2 * (i + 1))}[kind]

        def arrived(eng, n):
            eng.wait_ge(slot_loaded[n % RING_A], 16 * (n // RING_A + 1))
            return ring[:, (n % RING_A) * SLOT:(n % RING_A) * SLOT + WIDTH[DENSE[n][0]]]

        wi_e = ins["wi_e"].rearrange("e (k p) n -> e p k n", p=P)
        wo_e = ins["wo_e"].rearrange("e (k p) n -> e p k n", p=P)

        def expert_source(e, c):
            if c < NUP:
                col = (c // 2 % 2) * FE + (c // 4) * 512
                k = 4 * (c % 2)
                return wi_e[bass.ds(e, 1), :, k:k + 4, col:col + 512].rearrange("e p k n -> p (e k) n")
            k = 2 * (c - NUP)
            return wo_e[bass.ds(e, 1), :, k:k + 2, :].rearrange("e p k n -> p (e k) n")

        def as_chunk(buf, c):
            return buf.rearrange("p (k n) -> p k n", n=512 if c < NUP else D)

        def raw_of(c):
            return cut(raw, (c % XRAW) * XCH, XCH)

        def new_state(v, g):
            i, n = g // 8, AT["state", g // 8]
            at = (n % RING_A) * SLOT + (g % 8) * 512
            v.wait_ge(s("sd_outer"), g + 1)
            for x in range(4):
                sl = ring[:, at + x * P:at + (x + 1) * P]
                ins_ = v.scalar_tensor_tensor(out=sl, in0=sl, scalar=sgb[:, 4 * g + x:4 * g + x + 1],
                                              in1=bank(2 + g % 2)[:, x * P:(x + 1) * P], op0=ALU.mult, op1=ALU.add)
            ins_.then_inc(s("state_new"), 1)

        @block.sync
        def _(sp):
            sp.dma_start(hbuf[:, :], ins["x"]).then_inc(s("x_loaded"), 16)
            sp.dma_start(gains[:, :], ins["gains"]).then_inc(s("x_loaded"), 16)
            sp.dma_start(consts[:, :], ins["consts"]).then_inc(s("consts_loaded"), 16)
            sp.dma_start(router[:, :], ins["router"]).then_inc(s("consts_loaded"), 16)
            sp.dma_start(wba[:, :], ins["wba"]).then_inc(s("consts_loaded"), 16)
            for n, (kind, i) in enumerate(DENSE):
                if n == 3:
                    sp.dma_start(memT, ins["mem"].rearrange("p (k t) -> p k t", k=KD)).then_inc(s("mem_loaded"), 16)
                    sp.dma_start(convio[:, 0:576], ins["convbuf"]).then_inc(s("convbuf_loaded"), 16)
                if n >= RING_A:
                    name, count = read_by(n - RING_A)
                    sp.wait_ge(s(name), count)
                    if DENSE[n - RING_A][0] == "state":
                        sp.wait_ge(s(f"state_stored{DENSE[n - RING_A][1]}"), 16)
                at = (n % RING_A) * SLOT
                sp.dma_start(ring[:, at:at + WIDTH[kind]], ins[kind][i]).then_inc(slot_loaded[n % RING_A], 16)
            def load(e, c, before):
                before()
                sp.dma_start(as_chunk(raw_of(c), c), expert_source(e, c)).then_inc(raw_loaded[c % XRAW], 16)

            def step(e, after, st):
                for c in range(XSET, PERX):
                    load(e, c, lambda: sp.wait_ge(s("w_lo"), st * PERX + (c - XRAW + 1)))
                for c in range(XSET):
                    load(after, c, lambda: sp.wait_ge(s("w_lo"), st * PERX + (PERX + c - XRAW + 1)))

            sp.wait_ge(s("wo_mm"), KD)
            for c in range(PERX + XSET):
                load(c // PERX, c % PERX, lambda: sp.wait_ge(s("w_lo"), c - XRAW + 1) if c >= XRAW else None)
            with sp.Fori(1, E - 1) as e:
                step(e, e + 1, e)
            step(E - 1, 0, E - 1)
            sp.wait_ge(s("steps_known"), 1)
            n_rounds = sp.value_load(nsteps_i[0:1, 0:1], min_val=1, max_val=ROUNDS)
            with sp.If(n_rounds > 1):
                with sp.Fori(1, n_rounds) as r:
                    with sp.Fori(0, E - 1) as e:
                        step(e, e + 1, r * E + e)
                    step(E - 1, 0, r * E + (E - 1))
            sp.wait_ge(s("kv_stored"), 64)
            sp.wait_ge(s("S_stored"), 16)
            sp.wait_ge(s("state_stored0"), 16)
            sp.wait_ge(s("state_stored1"), 16)
            sp.wait_ge(s("outputs_stored"), 48)

        @block.gpsimd
        def _(pool):
            pool.memset(ones[:, :], 1.0).then_inc(s("ones_set"), 1)
            pool.memset(epsc[:, :], EPS).then_inc(s("ones_set"), 1)

            def store(dst, src):
                pool.dma_start(dst, src).then_inc(s("outputs_stored"), 16)

            pool.wait_ge(s("mem_kv"), 16)
            for l in range(2):
                pool.dma_start(outs["mk"][l], mk[l]).then_inc(s("kv_stored"), 16)
                pool.dma_start(outs["mv"][l], mv[l]).then_inc(s("kv_stored"), 16)
            pool.wait_ge(s("conv_state"), 2)
            store(outs["conv"], convio)
            pool.wait_ge(s("S_done"), 2)
            pool.dma_start(outs["S"], Sb).then_inc(s("S_stored"), 16)
            for i in range(2):
                pool.wait_ge(s("state_new"), 8 * (i + 1))
                at = (AT["state", i] % RING_A) * SLOT
                pool.dma_start(outs["state"][i], ring[:, at:at + SLOT]).then_inc(s(f"state_stored{i}"), 16)
            pool.wait_ge(s("norm_u"), 32)
            pool.dma_start(poolbuf, ins["poolbuf"]).then_inc(s("poolbuf_loaded"), 16)
            pool.wait_ge(s("pool_state"), 2)
            store(outs["pool"], pst)
            pool.wait_ge(s("norm_u"), 56)
            store(outs["y"], ubuf[:, :])

        @block.scalar
        def _(a):
            own = [0]

            def link(ins_):
                own[0] += 1
                ins_.then_inc(s("act_own"), 1)
                a.wait_ge(s("act_own"), own[0])

            def norm(i, src, n, ready, scale, eps_in=epsc, sqb=None, rtb=None):
                sqb = sq if sqb is None else sqb
                rtb = rt if rtb is None else rtb
                for k in range(KD):
                    ready(k)
                    a.activation(sqb[:, k * n:(k + 1) * n], src[:, k, :], ACT.Square).then_inc(s("norm_sq"), 1)
                a.wait_ge(s("norm_ss"), i + 1)
                a.activation(rtb[:, 0:n], bank(0)[:, 0:n], ACT.Sqrt, bias=epsc[:, 0:1], scale=scale)\
                    .then_inc(s("norm_rt"), 1)

            a.wait_ge(s("ones_set"), 2)
            a.wait_ge(s("x_loaded"), 32)
            norm(0, h, T, lambda k: a.wait_ge(s("x_loaded"), 32), 1.0 / D)
            a.wait_ge(s("norm_ss"), 1)
            a.wait_ge(s("norm_rs"), 1)
            norm(1, memT, NM, lambda k: a.wait_ge(s("mem_loaded"), 16), 1.0 / D)

            a.wait_ge(s("ba_mm"), 1)
            a.wait_ge(s("gba_zero"), 1)
            a.activation(gba[:, 0:2, :], bank(1)[:, 0:32].rearrange("p (t c) -> p t c", t=2), ACT.Copy).then_inc(s("gba_out"), 1)
            a.activation(gba[0:NS, 2, :], bank(1)[0:NS, 32:48], ACT.Copy).then_inc(s("gba_out"), 1)
            a.wait_ge(s("gba_out"), 2)
            a.activation(gb, gba[:, :, 0:8], ACT.Exp, scale=-1.0).then_inc(s("gate_exp"), 1)
            a.activation(gea, gains[:, GALOG:GALOG + H], ACT.Exp).then_inc(s("gate_exp"), 1)
            a.wait_ge(s("gate_ax"), 1)
            link(a.activation(ge, gax, ACT.Exp, scale=-1.0))
            a.activation(gl, ge, ACT.Ln, bias=ones[:, 0:1]).then_inc(s("gate_exp"), 1)

            a.wait_ge(s("convbuf_loaded"), 16)
            smp = pre[:, :, CW - 1 + SEQ:PRE].rearrange("p m (b j) -> p m b j", j=CW)
            for b in range(NS):
                cb = convio[:, 0:576].rearrange("p (m b j) -> p m b j", m=CT, b=NS)
                a.activation(smp[:, :, b, 0:CW - 1], cb[:, :, b, :], ACT.Copy).then_inc(s("conv_rows"), 1)

            def silu_of(m):
                a.wait_ge(s("conv_done"), m + 1)
                a.activation(act[:, m, :], act[:, m, :], ACT.Silu).then_inc(s("conv_silu"), 1)

            for t in range(36):
                a.wait_ge(s("ain_mm"), t + 1)
                src = bank(t % 8)
                if t < CT:
                    a.activation(pre[:, t, CW - 1:CW - 1 + SEQ], src[:, 0:SEQ], ACT.Copy)
                    a.activation(smp[:, t, :, CW - 1], src[:, SEQ:T], ACT.Copy).then_inc(s("ain_out"), 1)
                elif t < 32:
                    a.activation(z[:, t - CT, :], src[:, 0:T], ACT.Silu).then_inc(s("ain_out"), 1)
                else:
                    a.activation(cq[:, t - 32, :], src[:, 0:T], ACT.Copy).then_inc(s("ain_out"), 1)
                if 8 <= t < 32:
                    silu_of(t - 8)

            for l in range(2):
                for x in range(4):
                    a.wait_ge(s("mkv_mm"), 6 * l + x + 1)
                    a.activation(mk[l][:, x * NM:(x + 1) * NM], bank(x)[:, 0:NM], ACT.Copy).then_inc(s("mem_kv"), 1)
                for x in range(2):
                    a.wait_ge(s("mkv_mm"), 6 * l + 4 + x + 1)
                    a.activation(mv[l][:, x * 512:x * 512 + 256], bank(4 + x)[:, 0:256], ACT.Copy).then_inc(s("mem_kv"), 1)
                    a.activation(mv[l][:, x * 512 + 256:x * 512 + 512], bank(4 + x)[:, 256:512], ACT.Copy).then_inc(s("mem_kv"), 1)

            a.wait_ge(s("conv_silu"), 16)
            for g in range(4):
                if g >= 1:
                    a.wait_ge(s("l2_mm"), g)
                a.activation(sqq, act[:, 4 * g:4 * g + 4, :].rearrange("p m c -> p (m c)"), ACT.Square).then_inc(s("l2_sq"), 1)
                a.wait_ge(s("l2_mm"), g + 1)
                if g >= 1:
                    a.wait_ge(s("l2_done"), g)
                for x in range(2):
                    a.activation(rsq[:, 2 * x * ACTW:2 * (x + 1) * ACTW].rearrange("p (m c) -> p m c", m=2),
                                 PP[x][:, :].rearrange("p (m c) -> p m c", m=2)[:, :, 0:ACTW],
                                 ACT.Sqrt, bias=epsc[:, 0:1]).then_inc(s("l2_rt"), 1)

            a.wait_ge(s("coef_dif"), 1)
            for dst, src in ((ceG, cG), (ctail, cdl), (ceGl, cgt[:, 0:16]), (sgb[:, 0:64], sgt[:, 0:64])):
                a.activation(dst, src, ACT.Exp).then_inc(s("coef_exp"), 1)

            def attention(l):
                for t in range(2):
                    a.wait_ge(s("att_max"), 3 * l + t + 1)
                    for x in range(XH):
                        a.activation(Pr[:, t * 1024 + x * NM:t * 1024 + (x + 1) * NM], PP[t][:, x * NM:(x + 1) * NM], ACT.Exp,
                                     bias=anm[:, t * 4 + x:t * 4 + x + 1], scale=P ** -0.5,
                                     accum_out=asum[:, t * 4 + x:t * 4 + x + 1]).then_inc(s("att_exp"), 1)
                v = PrT.rearrange("p (n t c) -> p n t c", t=2, c=P)
                for t in range(2):
                    a.wait_ge(s("att_tr"), 3 * l + t + 1)
                    a.activation(v[:, :, t, :], PP[2 + t][:, :].rearrange("p (n c) -> p n c", c=P), ACT.Copy).then_inc(s("att_pt"), 1)
                a.wait_ge(s("att_o"), 1 * l + 1)
                a.activation(cat[:, H:H + XH, 0:SEQ], PP[0][:, :].rearrange("p (m c) -> p m c", m=XH), ACT.Copy).then_inc(s("att_cat"), 1)
                a.wait_ge(s("cache_mm"), 4 * l + 2)
                a.activation(STs, bank(0)[:, 0:64], ACT.Copy).then_inc(s("sat_st"), 1)
                a.wait_ge(s("att_max"), 3 * l + 3)
                a.activation(P32[0:BH, :], bank(1)[0:BH, 0:NM], ACT.Exp, bias=anm[0:BH, 0:1], scale=P ** -0.5,
                             accum_out=asum[0:BH, 0:1]).then_inc(s("att_exp"), 1)
                a.wait_ge(s("att_tr"), 3 * l + 3)
                a.activation(PT32, bank(2)[:, 0:64], ACT.Copy).then_inc(s("sat_pt"), 1)
                a.wait_ge(s("cache_mm"), 4 * l + 4)
                a.activation(cat[:, H:H + XH, SEQ:T].rearrange("p x b -> p b x"),
                             bank(3)[:, 0:BH].rearrange("p (b x) -> p b x", x=XH), ACT.Copy).then_inc(s("att_cat"), 1)

            attention(0)

            for c in range(NCH):
                a.wait_ge(s("dl_neg"), c + 1)
                for x in range(H):
                    a.activation(DTb[:, x * P:(x + 1) * P], MLb[:, x * P:(x + 1) * P], ACT.Exp,
                                 bias=cnG[:, c * H + x:c * H + x + 1]).then_inc(s("dl_dt"), 1)
                a.activation(Xb, PP[0][:, :], ACT.Exp).then_inc(s("dl_eg"), 1)
                for lv in range(1, NLVL + 1):
                    if lv < NLVL:
                        for g in range(2):
                            a.wait_ge(s("dl_tt"), (c * (NLVL - 1) + lv - 1) * 2 + g + 1)
                            a.activation(Tb[:, g * 512:(g + 1) * 512], bank(g), ACT.Copy).then_inc(s("dl_t"), 1)
                        for g in range(2):
                            a.wait_ge(s("dl_xx"), (c * (NLVL - 1) + lv - 1) * 2 + g + 1)
                            a.activation(Xb[:, g * 512:(g + 1) * 512], bank(2 + g), ACT.Copy).then_inc(s("dl_x"), 1)
                a.wait_ge(s("dl_uu"), c + 1)
                a.activation(Tb, PP[1][:, :], ACT.Copy).then_inc(s("dl_u"), 1)
                a.wait_ge(s("dl_o"), c + 1)
                a.activation(cat[:, 0:H, c * P:(c + 1) * P], PP[2][:, :].rearrange("p (m c) -> p m c", m=H), ACT.Copy)\
                    .then_inc(s("dl_cat"), 1)

            a.wait_ge(s("sd_rows"), 1)
            a.activation(krow[0:DBH, :], bank(4)[0:DBH, 0:P], ACT.Copy).then_inc(s("sd_row"), 1)
            a.wait_ge(s("sd_rows"), 2)
            a.activation(urow[0:DBH, :], bank(5)[0:DBH, 0:P], ACT.Copy).then_inc(s("sd_row"), 1)

            a.wait_ge(s("dl_cat"), NCH)
            a.wait_ge(s("sd_cat"), 1)
            for x in range(H):
                a.activation(sq[:, x * T:(x + 1) * T], cat[:, x, :], ACT.Square).then_inc(s("on_sq"), 1)
            for x in range(H):
                a.wait_ge(s("on_mm"), x + 1)
                a.activation(sq[:, x * T:(x + 1) * T], bank(x)[:, 0:T], ACT.Sqrt, bias=epsc[:, 0:1], scale=1.0 / P)\
                    .then_inc(s("on_rt"), 1)

            norm(2, h, T, lambda k: a.wait_ge(s("aout_h"), k + 1), 1.0 / D)
            for f in range(FT):
                a.wait_ge(s("wi_mm"), f + 1)
                if f >= 2:
                    a.wait_ge(s("wi_hid"), f - 1)
                a.activation(sil[f % 2], bank(2 * (f % 4))[:, 0:T], ACT.Silu).then_inc(s("wi_sil"), 1)
            norm(3, h, T, lambda k: a.wait_ge(s("wo_h"), k + 1), 1.0 / D)

            psm_in = pin[:, :, PW + SEQ:PCOL].rearrange("p m (b j) -> p m b j", j=PW + 1)
            a.wait_ge(s("norm_u"), 40)
            a.wait_ge(s("pin_zero"), 1)
            a.wait_ge(s("poolbuf_loaded"), 16)
            a.wait_ge(s("pin_zero"), 2)
            for t in range(12):
                a.wait_ge(s("bin_mm"), t + 1)
                if t < 8:
                    a.activation(pin[:, t, PW:PW + SEQ], bank(t % 8)[:, 0:SEQ], ACT.Copy)
                    a.activation(psm_in[:, t, :, PW], bank(t % 8)[:, SEQ:T], ACT.Copy).then_inc(s("bin_out"), 1)
                else:
                    a.activation(cq[:, t - 8, :], bank(t % 8)[:, 0:T], ACT.Copy).then_inc(s("bin_out"), 1)
            for t in range(8):
                a.wait_ge(s("pm_mm"), t + 1)
                if t == 0:
                    a.wait_ge(s("pm_mm"), 8)
                a.activation(cat[:, t, :], bank(t)[:, 0:T], ACT.Copy, scale=gains[:, GPS + t:GPS + t + 1])\
                    .then_inc(s("pm_cat"), 1)
            attention(1)
            norm(4, h, T, lambda k: a.wait_ge(s("bout_h"), k + 1), 1.0 / D, sqb=fsq, rtb=frt)

            a.wait_ge(s("outputs_stored"), 32)
            for t in range(3):
                n = P if t < 2 else NS
                a.wait_ge(s("xt_mm"), t + 1)
                a.activation(xtok[0:n, t, :], PP[1 + t][0:n, :], ACT.Copy).then_inc(s("xt_out"), 1)
            a.wait_ge(s("rt_mm"), 1)
            a.wait_ge(s("rout_zero"), 1)
            a.activation(rout[:, 0:16], bank(0)[:, 0:16], ACT.Copy).then_inc(s("rt_out"), 1)
            a.activation(rout[0:NS, 16:24], bank(0)[0:NS, 16:24], ACT.Copy).then_inc(s("rt_out"), 1)
            a.wait_ge(s("rt_sub"), 1)
            a.activation(rr[1], rr[1], ACT.Exp).then_inc(s("rt_exp"), 1)
            def halve(c, st, again=0):
                a.wait_ge(raw_loaded[c % XRAW], st * (16 * PERX // XRAW) + (16 * (PERX // XRAW * again + c // XRAW + 1)))
                q = c + PERX * again - XSET
                if q >= 0:
                    name, n = ("up_mm", NUP) if q < NUP else ("down_mm", NDOWN)
                    a.wait_ge(s(name), st * n + ((q if q < NUP else q - NUP) + 1))
                a.activation(whi[c % XSET][:, :], raw_of(c), ACT.Copy).then_inc(s("w_hi"), 1)

            def slots():
                a.activation(xsh[:, :], PP[1][:, :], ACT.Copy).then_inc(s("xs_hi"), 1)

            a.wait_ge(s("gat_mm"), 1)
            slots()
            a.wait_ge(s("bout_mm"), KD)
            for c in range(XSET):
                halve(c, 0)

            a.wait_ge(s("steps_known"), 1)
            n_rounds = a.value_load(nsteps_i[0:1, 0:1], min_val=1, max_val=ROUNDS)
            with a.Fori(0, n_rounds * E) as st:
                for c in range(XSET, PERX):
                    halve(c, st)
                    if c % 4 == 0 and c // 4 - 1 < FCN:
                        f = c // 4 - 1
                        a.wait_ge(s("up_mm"), st * NUP + (4 * f + 2))
                        if f >= 2:
                            a.wait_ge(s("up_h"), st * FCN + (f - 1))
                        a.activation(esil[f % 2], bank(2 * (f % 2))[:, :], ACT.Silu).then_inc(s("up_sil"), 1)
                    if c in TURNED:
                        f = TURNED[c]
                        a.wait_ge(s("ht_mm"), st * FCN + (f + 1))
                        a.activation(hTh[:, 4 * f * C:4 * (f + 1) * C], bank(4 + f % 2), ACT.Copy).then_inc(s("ht_hi"), 1)
                    if c == NUP + 3:
                        a.wait_ge(s("gat_mm"), st + 2)
                        slots()
                halve(0, st, 1)
                halve(1, st, 1)
                a.wait_ge(s("down_mm"), st * NDOWN + NDOWN)
                a.activation(yslot, PP[3][:, :], ACT.Copy).then_inc(s("y_out"), 1)
                halve(2, st, 1)

            a.wait_ge(s("comb_h"), n_rounds * E * KD + KD)
            norm(5, h, T, lambda k: None, 1.0 / D, sqb=fsq, rtb=frt)

        @block.vector
        def _(v):
            own = [0]

            def link(ins_):
                own[0] += 1
                ins_.then_inc(s("dve_own"), 1)
                v.wait_ge(s("dve_own"), own[0])

            def norm(i, src, n, dsts, rtb=None, rsb=None):
                rtb = rt if rtb is None else rtb
                rsb = rs if rsb is None else rsb
                v.wait_ge(s("norm_rt"), i + 1)
                v.reciprocal(rsb[:, 0:n], rtb[:, 0:n]).then_inc(s("norm_rs"), 1)
                v.wait_ge(s("norm_rs"), i + 1)
                for dst, g in dsts:
                    for k in range(KD):
                        v.scalar_tensor_tensor(out=dst[:, k, :], in0=src[:, k, :], scalar=gains[:, g + k:g + k + 1],
                                               in1=rsb[:, 0:n], op0=ALU.mult, op1=ALU.mult).then_inc(s("norm_u"), 1)

            v.memset(gba, 0.0).then_inc(s("gba_zero"), 1)
            v.wait_ge(s("x_loaded"), 32)
            v.wait_ge(s("consts_loaded"), 48)
            v.memset(pre[:, :, 0:CW - 1], 0.0).then_inc(s("pre_zero"), 1)
            norm(0, h, T, [(u, GA1)])
            norm(1, memT, NM, [(memn[0], GM0), (memn[1], GM1)])

            v.wait_ge(s("gba_out"), 2)
            dt_b = gains[:, GDT:GDT + H].unsqueeze(1).to_broadcast([P, 3, H])
            link(v.tensor_tensor(gx, gba[:, :, 8:16], dt_b, ALU.add))
            v.scalar_tensor_tensor(out=gax, in0=gx, scalar=-1.0, in1=gx, op0=ALU.mult, op1=ALU.max).then_inc(s("gate_ax"), 1)
            v.wait_ge(s("gate_exp"), 1)
            link(v.tensor_scalar(gb, gb, 1.0, None, ALU.add))
            link(v.reciprocal(gb, gb))
            v.wait_ge(s("gate_exp"), 3)
            link(v.scalar_tensor_tensor(out=gl, in0=gx, scalar=0.0, in1=gl, op0=ALU.max, op1=ALU.add))
            v.wait_ge(s("gate_exp"), 2)
            link(v.scalar_tensor_tensor(out=gg, in0=gl, scalar=-1.0, in1=gea.unsqueeze(1).to_broadcast([P, 3, H]),
                                        op0=ALU.mult, op1=ALU.mult))
            dg8 = ident[0:NS, 0:NS].unsqueeze(2).to_broadcast([NS, NS, H])
            for i, val in enumerate((gg, gb)):
                v.tensor_tensor(gd[0:NS, 64 * i:64 * i + 64].rearrange("p (b x) -> p b x", x=H),
                                val[0:NS, 2, :].unsqueeze(1).to_broadcast([NS, NS, H]), dg8, ALU.mult)\
                    .then_inc(s("gate_done"), 1)

            v.wait_ge(s("conv_rows"), NS)
            v.wait_ge(s("pre_zero"), 1)
            for g in range(CT // 4):
                v.wait_ge(s("ain_out"), 4 * g + 4)
                for j in range(CW):
                    for m in range(4 * g, 4 * g + 4):
                        tap = gains[:, GTAP + m * CW + j:GTAP + m * CW + j + 1]
                        if j:
                            v.wait_ge(s("conv_tap"), 12 * g + 4 * (j - 1) + m - 4 * g + 1)
                        ins_ = v.tensor_scalar(act[:, m, :], pre[:, m, 0:ACTW], tap, None, ALU.mult) if j == 0 else \
                            v.scalar_tensor_tensor(out=act[:, m, :], in0=pre[:, m, j:j + ACTW], scalar=tap,
                                                   in1=act[:, m, :], op0=ALU.mult, op1=ALU.add)
                        ins_.then_inc(s("conv_tap") if j < CW - 1 else s("conv_done"), 1)
            cio = convio.rearrange("p (m c) -> p m c", m=CT)
            smp = pre[:, :, CW - 1 + SEQ:PRE].rearrange("p m (b j) -> p m b j", j=CW)
            v.tensor_copy(cio[:, :, 0:3], pre[:, :, SEQ:SEQ + 3]).then_inc(s("conv_state"), 1)
            for b in range(NS):
                ins_ = v.tensor_copy(cio[:, :, 3 + 3 * b:6 + 3 * b], smp[:, :, b, 1:CW])
            ins_.then_inc(s("conv_state"), 1)

            for g in range(4):
                v.wait_ge(s("l2_rt"), 2 * g + 2)
                link(v.reciprocal(rsq, rsq))
                sl = act[:, 4 * g:4 * g + 4, :].rearrange("p m c -> p (m c)")
                v.scalar_tensor_tensor(out=sl, in0=sl, scalar=P ** -0.5 if g < 2 else 1.0, in1=rsq,
                                       op0=ALU.mult, op1=ALU.mult).then_inc(s("l2_done"), 1)

            v.wait_ge(s("coef_mm"), 1)
            link(v.tensor_copy(cG, bank(0)[:, 0:16]))
            v.tensor_copy(cgt[:, 0:16], bank(0)[:, 16:32])
            link(v.tensor_copy(sgt, bank(0)[:, 32:160]))
            v.tensor_scalar(cnG, cG, -1.0, None, ALU.mult)
            v.tensor_copy(sgb[:, 64:128], sgt[:, 64:128])
            link(v.tensor_tensor(cdl, cgt[:, 0:16], cG, ALU.subtract))
            v.tensor_copy(cgt[:, 16:32], cG).then_inc(s("coef_dif"), 1)
            v.wait_ge(s("coef_exp"), 4)
            gbp = gb[:, 0:2, :].rearrange("p t c -> p (t c)")
            v.tensor_tensor(cbeG, ceG, gbp, ALU.mult).then_inc(s("coef_beg"), 1)

            def attention(l):
                for t in range(2):
                    v.wait_ge(s("att_mm"), 2 * l + t + 1)
                    link(v.reduce_max(amx[:, 4 * t:4 * t + 4], PP[t][:, :].rearrange("p (m c) -> p m c", m=XH), AX))
                    v.tensor_scalar(anm[:, 4 * t:4 * t + 4], amx[:, 4 * t:4 * t + 4], -(P ** -0.5), None, ALU.mult)\
                        .then_inc(s("att_max"), 1)
                for t in range(2):
                    v.wait_ge(s("att_exp"), 9 * l + 4 * t + 4)
                    link(v.reciprocal(ars[:, 4 * t:4 * t + 4], asum[:, 4 * t:4 * t + 4]))
                    pt = Pr[:, 1024 * t:1024 * (t + 1)].rearrange("p (m c) -> p m c", m=XH)
                    v.tensor_tensor(pt, pt, ars[:, 4 * t:4 * t + 4].unsqueeze(2).to_broadcast([P, XH, NM]), ALU.mult)\
                        .then_inc(s("att_p"), 1)
                v.wait_ge(s("sat_s"), 1 * l + 1)
                link(v.reduce_max(amx[0:BH, 0:1], bank(1)[0:BH, 0:NM], AX))
                v.tensor_scalar(anm[0:BH, 0:1], amx[0:BH, 0:1], -(P ** -0.5), None, ALU.mult).then_inc(s("att_max"), 1)
                v.wait_ge(s("att_exp"), 9 * l + 9)
                link(v.reciprocal(ars[0:BH, 0:1], asum[0:BH, 0:1]))
                v.tensor_scalar(P32[0:BH, :], P32[0:BH, :], ars[0:BH, 0:1], None, ALU.mult).then_inc(s("att_p"), 1)

            attention(0)

            def per_head(c, coef):
                return coef[:, c * H:(c + 1) * H].unsqueeze(2).to_broadcast([P, H, P])

            def heads(b):
                return b.rearrange("p (m c) -> p m c", m=H)

            for c in range(NCH):
                cols = slice(c * P, (c + 1) * P)
                v.wait_ge(s("conv_state"), 2)
                v.wait_ge(s("dl_grow"), c + 1)
                v.tensor_tensor(heads(MLb), heads(PP[0][:, :]), neg.unsqueeze(1).to_broadcast([P, H, P]), ALU.add)\
                    .then_inc(s("dl_neg"), 1)
                v.wait_ge(s("dl_dt"), H * (c + 1))
                v.wait_ge(s("dl_kk"), 2 * c + 1)
                v.tensor_tensor(PTb, PP[1][:, :], DTb, ALU.mult).then_inc(s("dl_pt"), 1)
                v.wait_ge(s("dl_kk"), 2 * c + 2)
                link(v.tensor_tensor(MTb, PP[2][:, :], DTb, ALU.mult))
                v.wait_ge(s("dl_brow"), c + 1)
                link(v.tensor_tensor(MTb, MTb, PP[3][:, :], ALU.mult))
                v.wait_ge(s("dl_eg"), c + 1)
                v.tensor_tensor(act[:, 0:H, cols], act[:, 0:H, cols], heads(Xb), ALU.mult).then_inc(s("dl_qd"), 1)
                v.wait_ge(s("dl_tok"), 2 * c + 1)
                v.tensor_tensor(heads(vtok), heads(PP[1][:, :]), per_head(c, gbp), ALU.mult).then_inc(s("dl_v"), 1)
                v.wait_ge(s("dl_tok"), 2 * c + 2)
                v.tensor_tensor(heads(ktail), heads(PP[2][:, :]), per_head(c, ctail), ALU.mult).then_inc(s("dl_kt"), 1)

                for lv in range(NLVL):
                    mask = consts[:, CLVL + lv * P:CLVL + (lv + 1) * P].unsqueeze(1).to_broadcast([P, H, P])
                    if lv >= 2:
                        v.wait_ge(s("dl_xx"), (c * (NLVL - 1) + lv - 1) * 2)
                    if lv:
                        v.wait_ge(s("dl_um"), 2 * (c * NLVL + lv))
                    v.tensor_tensor(heads(MLb), heads(MTb), mask, ALU.mult).then_inc(s("dl_ml"), 1)
                    if lv == 0:
                        v.wait_ge(s("dl_ml"), c * NLVL + 1)
                        for g in range(2):
                            v.tensor_tensor(heads(Ub)[:, 4 * g:4 * g + 4, :], ident.unsqueeze(1).to_broadcast([P, 4, P]),
                                            heads(MLb)[:, 4 * g:4 * g + 4, :], ALU.subtract).then_inc(s("dl_um"), 1)
                        continue
                    for g in range(2):
                        v.wait_ge(s("dl_du"), (c * (NLVL - 1) + lv - 1) * 2 + g + 1)
                        v.tensor_tensor(Ub[:, g * 512:(g + 1) * 512], Ub[:, g * 512:(g + 1) * 512], bank(4 + g), ALU.subtract)\
                            .then_inc(s("dl_um"), 1)
                if c:
                    v.wait_ge(s("dl_ks"), 1)
                    link(v.tensor_tensor(heads(Xb), heads(PP[0][:, :]), per_head(c, cbeG), ALU.mult))
                    v.tensor_tensor(Xb, vtok, Xb, ALU.subtract).then_inc(s("dl_r"), 1)
                v.wait_ge(s("dl_ds"), c + 1)
                if c == 0:
                    v.tensor_copy(Sb, PP[3][:, :]).then_inc(s("S_done"), 1)
                else:
                    v.wait_ge(s("S_done"), 1)
                    v.wait_ge(s("dl_o"), c + 1)
                    link(v.tensor_tensor(heads(Sb), heads(Sb), per_head(c, ceGl), ALU.mult))
                    v.tensor_tensor(Sb, Sb, PP[3][:, :], ALU.add).then_inc(s("S_done"), 1)

            def cols64(m0):
                return act[:, m0:m0 + H, S0:S0 + CW * (NS - 1) + 1:CW].rearrange("p x b -> p b x")

            def as_bx(b):
                return b.rearrange("p (b x) -> p b x", x=H)

            v.wait_ge(s("dl_ds"), NCH)
            v.tensor_copy(kq[:, :, 0].rearrange("p (b x) -> p b x", x=H), cols64(8))
            v.tensor_copy(kq[:, :, 1].rearrange("p (b x) -> p b x", x=H), cols64(0))
            link(v.tensor_copy(as_bx(v64), cols64(16)))
            link(v.tensor_copy(t64, kq[:, :, 0]))
            v.tensor_tensor(kqd, t64, kq[:, :, 1], ALU.mult).then_inc(s("sd_cols"), 1)
            v.wait_ge(s("sd_mm"), 1)
            rk = bank(0)[:, 0:128].rearrange("p (n c) -> p n c", c=2)
            egs, bs = sgb[:, 0:64], sgb[:, 64:128]
            v.wait_ge(s("sd_rows"), 1)
            link(v.tensor_tensor(t64, rk[:, :, 0], egs, ALU.mult))
            link(v.tensor_tensor(u64, v64, t64, ALU.subtract))
            link(v.tensor_tensor(u64, u64, bs, ALU.mult))
            v.tensor_tensor(qku, rk[:, :, 1], egs, ALU.mult).then_inc(s("sd_u"), 1)
            v.wait_ge(s("sd_u"), 1)
            link(v.tensor_tensor(t64, bank(1)[:, 0:64], u64, ALU.mult))
            v.tensor_tensor(cat[:, 0:H, SEQ:T].rearrange("p x b -> p b x"), as_bx(t64), as_bx(qku), ALU.add)\
                .then_inc(s("sd_cat"), 1)
            v.wait_ge(s("sd_row"), 2)
            for g in range(16):
                if g >= 2:
                    v.wait_ge(s("sd_outer"), g - 1)
                v.tensor_tensor(ublk[g % 2][0:DBH, :].rearrange("p (n c) -> p n c", c=P),
                                urow[0:DBH, :].unsqueeze(1).to_broadcast([DBH, 4, P]),
                                ident[0:DBH, 4 * g:4 * g + 4].unsqueeze(2).to_broadcast([DBH, 4, P]), ALU.mult)\
                    .then_inc(s("sd_blk"), 1)
                if g >= 1:
                    new_state(v, g - 1)
            new_state(v, 15)

            for x in range(H):
                v.wait_ge(s("on_rt"), x + 1)
                sl = sq[:, x * T:(x + 1) * T]
                link(v.reciprocal(sl, sl))
                link(v.scalar_tensor_tensor(out=sl, in0=sl, scalar=gains[:, GON:GON + 1], in1=z[:, x, :],
                                            op0=ALU.mult, op1=ALU.mult))
                v.tensor_tensor(cat[:, x, :], cat[:, x, :], sl, ALU.mult).then_inc(s("on_done"), 1)

            def residual(name, b):
                for t in range(KD):
                    v.wait_ge(s(f"{name}_mm"), t + 1)
                    v.tensor_tensor(h[:, t, :], h[:, t, :], bank(t)[:, 0:T], ALU.add).then_inc(s(f"{name}_h"), 1)

            residual("aout", 0)
            norm(2, h, T, [(u, GA2)])
            v.wait_ge(s("S_stored"), 16)
            for f in range(FT):
                v.wait_ge(s("wi_sil"), f + 1)
                v.tensor_tensor(hid[:, f, :], sil[f % 2], bank(2 * (f % 4) + 1)[:, 0:T], ALU.mult).then_inc(s("wi_hid"), 1)
            residual("wo", 0)
            norm(3, h, T, [(u, GB1)])

            v.wait_ge(s("norm_u"), 40)
            v.memset(pin[:, :, 0:PW], 0.0).then_inc(s("pin_zero"), 1)
            v.wait_ge(s("poolbuf_loaded"), 16)
            psv = pin[:, :, PW + SEQ:PCOL].rearrange("p m (b j) -> p m b j", j=PW + 1)
            pbv = poolbuf.rearrange("p (m b j) -> p m b j", m=KD, b=NS)
            for b in range(NS):
                ins_ = v.tensor_copy(psv[:, :, b, 0:PW], pbv[:, :, b, :])
            ins_.then_inc(s("pin_zero"), 1)
            v.wait_ge(s("bin_out"), 8)
            v.wait_ge(s("pin_zero"), 2)
            v.wait_ge(s("bin_mm"), 12)
            v.wait_ge(s("kv_stored"), 64)
            pstv = pst.rearrange("p (m c) -> p m c", m=KD)
            v.tensor_copy(pstv[:, :, 0:PW], pin[:, :, SEQ:SEQ + PW]).then_inc(s("pool_state"), 1)
            for b in range(NS):
                ins_ = v.tensor_copy(pstv[:, :, PW + PW * b:PW + PW * (b + 1)], psv[:, :, b, 1:PW + 1])
            ins_.then_inc(s("pool_state"), 1)
            src = pin
            for g in range(4):
                w = 2 << g
                m0 = 2 * g
                sh = w // 2
                if g % 2 == 0:
                    dst, frm = psm, pin
                else:
                    dst, frm = pin, psm
                if g == 0:
                    link(v.tensor_copy(u[:, :, 0:SEQ], pin[:, :, PW:PW + SEQ]))
                    link(v.tensor_copy(u[:, :, SEQ:T], psv[:, :, :, PW]))
                lo = 2 * sh - 1
                link(v.tensor_tensor(dst[:, m0:, lo:], frm[:, m0:, lo:], frm[:, m0:, lo - sh:PCOL - sh], ALU.add))
                v.scalar_tensor_tensor(out=pd[:, m0:m0 + 2, 0:SEQ], in0=dst[:, m0:m0 + 2, PW:PW + SEQ], scalar=1.0 / w,
                                       in1=u[:, m0:m0 + 2, 0:SEQ], op0=ALU.mult, op1=ALU.subtract)
                dsv = dst[:, :, PW + SEQ:PCOL].rearrange("p m (b j) -> p m b j", j=PW + 1)
                link(v.scalar_tensor_tensor(out=pd[:, m0:m0 + 2, SEQ:T], in0=dsv[:, m0:m0 + 2, :, PW], scalar=1.0 / w,
                                            in1=u[:, m0:m0 + 2, SEQ:T], op0=ALU.mult, op1=ALU.subtract))
                inv = consts[:, CINV + 16 * g:CINV + 16 * g + 16].unsqueeze(1).to_broadcast([P, 2, 16])
                fx = pfix[:, 0:32].rearrange("p (m c) -> p m c", m=2)
                link(v.tensor_tensor(fx, dst[:, m0:m0 + 2, PW:PW + 16], inv, ALU.mult))
                ins_ = v.tensor_tensor(pd[:, m0:m0 + 2, 0:16], fx, u[:, m0:m0 + 2, 0:16], ALU.subtract)
                link(ins_) if g < 3 else ins_.then_inc(s("pool_d"), 1)

            attention(1)
            residual("bout", 0)
            norm(4, h, T, [(u, GB2)], rtb=frt, rsb=frs)

            v.memset(rout, 0.0).then_inc(s("rout_zero"), 1)
            v.wait_ge(s("rt_out"), 2)
            lg = rout.rearrange("p (t e) -> p t e", t=3)
            rank, sel, gat, mx, pos = rr[0], rr[2], rr[3], rr[4], rr[5]
            for t in range(3):
                mine = lg[:, t, :].unsqueeze(2).to_broadcast([P, E, E])
                other = lg[:, t, :].unsqueeze(1).to_broadcast([P, E, E])
                o1 = rtmp[:, 64 * t:64 * t + 64].rearrange("p (a b) -> p a b", a=E)
                o2 = rtm2[:, 64 * t:64 * t + 64].rearrange("p (a b) -> p a b", a=E)
                tie = consts[:, CTIE:CTIE + 64].rearrange("p (a b) -> p a b", a=E)
                v.tensor_tensor(o1, other, mine, ALU.is_gt)
                link(v.tensor_tensor(o2, other, mine, ALU.is_equal))
                link(v.tensor_tensor(o2, o2, tie, ALU.mult))
                link(v.tensor_tensor(o1, o1, o2, ALU.add))
                v.reduce_sum(rank[:, 8 * t:8 * t + 8], o1, AX)
                link(v.reduce_max(mx[:, t:t + 1], lg[:, t, :], AX))
                v.tensor_scalar(rr[1][:, 8 * t:8 * t + 8], lg[:, t, :], mx[:, t:t + 1], None, ALU.subtract)\
                    .then_inc(s("rt_d"), 1)
            v.wait_ge(s("rt_d"), 3)
            v.tensor_scalar(sel, rank, 1.5, None, ALU.is_lt).then_inc(s("rt_sub"), 1)
            v.wait_ge(s("rt_exp"), 1)
            link(v.tensor_tensor(gat, rr[1], sel, ALU.mult))
            link(v.reduce_sum(mx[:, 0:3], gat.rearrange("p (t e) -> p t e", t=3), AX))
            link(v.reciprocal(mx[:, 0:3], mx[:, 0:3]))
            link(v.tensor_tensor(gat.rearrange("p (t e) -> p t e", t=3), gat.rearrange("p (t e) -> p t e", t=3),
                                 mx[:, 0:3].unsqueeze(2).to_broadcast([P, 3, E]), ALU.mult))
            v.wait_ge(s("pos_mm"), 1)
            link(v.tensor_copy(pos, bank(0)[:, 0:24]))
            link(v.tensor_copy(cnt8[:, 0:8], bank(0)[:, 24:32]))
            link(v.tensor_scalar(rr[6], sel, 1e4, -1e4, ALU.mult, ALU.add))
            link(v.tensor_tensor(pos, pos, rr[6], ALU.add))
            for r in range(ROUNDS + 1):
                v.tensor_scalar(posx[:, r * E:(r + 1) * E, :].rearrange("p e t -> p t e"),
                                pos.rearrange("p (t e) -> p t e", t=3), -float(r * C), None, ALU.add)
                link(v.tensor_copy(gatex[:, r * E:(r + 1) * E, :].rearrange("p e t -> p t e"),
                                   gat.rearrange("p (t e) -> p t e", t=3)))
            link(v.reduce_max(cnt8[:, 8:9], cnt8[:, 0:8], AX))
            link(v.memset(cnt8[:, 9:10], 1.0))
            for r in range(1, ROUNDS):
                link(v.scalar_tensor_tensor(out=cnt8[:, 9:10], in0=cnt8[:, 8:9], scalar=float(r * C), in1=cnt8[:, 9:10],
                                            op0=ALU.is_gt, op1=ALU.add))
            v.tensor_copy(nsteps_i[:, :], cnt8[:, 9:10]).then_inc(s("steps_known"), 1)

            def dispatch(dst, at):
                for t in range(3):
                    n = P if t < 2 else NS
                    v.tensor_scalar(dst[0:n, t, :], iota[0:n, :], posx[0:n, at, t:t + 1] if isinstance(at, int) else
                                    posx[0:n, bass.ds(at, 1), t:t + 1].rearrange("p a b -> p (a b)"), None, ALU.is_equal)\
                        .then_inc(s("disp"), 1)

            def halve(c, want):
                v.wait_ge(s("w_hi"), want)
                v.tensor_tensor(wlo[c % XSET][:, :], raw_of(c), whi[c % XSET][:, :].bitcast(F32), ALU.subtract)\
                    .then_inc(s("w_lo"), 1)

            def slots(want):
                v.wait_ge(s("xs_hi"), want)
                v.tensor_tensor(xsl[:, :], PP[1][:, :], xsh[:, :].bitcast(F32), ALU.subtract).then_inc(s("xs_lo"), 1)

            v.wait_ge(s("steps_known"), 1)
            dispatch(disp, 0)
            v.memset(comb, 0.0).then_inc(s("comb_out"), 1)
            v.memset(yslot, 0.0).then_inc(s("y_out"), 1)
            slots(1)
            for c in range(XSET):
                halve(c, c + 1)
            n_rounds = v.value_load(nsteps_i[0:1, 0:1], min_val=1, max_val=ROUNDS)

            def add_back(before):
                for t in range(KD):
                    v.wait_ge(s("cmb_mm"), before + (t + 1))
                    v.tensor_tensor(h[:, t, :], h[:, t, :], bank(2 + t % 4)[:, 0:T], ALU.add).then_inc(s("comb_h"), 1)

            with v.Fori(0, n_rounds * E) as st:
                v.wait_ge(s("disp"), st * 3 + 3)
                for t in range(3):
                    n = P if t < 2 else NS
                    v.tensor_scalar(dispg[0:n, t, :], disp[0:n, t, :],
                                    gatex[0:n, bass.ds(st, 1), t:t + 1].rearrange("p a b -> p (a b)"), None, ALU.mult)\
                        .then_inc(s("dispg"), 1)
                v.wait_ge(s("gat_mm"), st + 1)
                v.wait_ge(s("dispg"), st * 3 + 3)
                dispatch(disp, st + 1)
                for c in range(XSET, PERX):
                    halve(c, st * PERX + (c + 1))
                    if c == XSET:
                        add_back(st * KD)
                    if c % 4 == 2 and 0 <= c // 4 - 1 < FCN:
                        f = c // 4 - 1
                        v.wait_ge(s("up_sil"), st * FCN + (f + 1))
                        v.wait_ge(s("up_mm"), st * NUP + (4 * f + 4))
                        if f >= 2:
                            v.wait_ge(s("ht_mm"), st * FCN + (f - 1))
                        v.tensor_tensor(hslot[f % 2], esil[f % 2], bank(2 * (f % 2) + 1)[:, :], ALU.mult)\
                            .then_inc(s("up_h"), 1)
                    if c in TURNED:
                        f = TURNED[c]
                        v.wait_ge(s("ht_hi"), st * FCN + (f + 1))
                        sl = slice(4 * f * C, 4 * (f + 1) * C)
                        v.tensor_tensor(hTl[:, sl], bank(4 + f % 2), hTh[:, sl].bitcast(F32), ALU.subtract)\
                            .then_inc(s("ht_lo"), 1)
                    if c == NUP + 3:
                        slots(st + 2)
                    if c == NUP + 7:
                        v.wait_ge(s("cmb_tr"), st + 1)
                        v.tensor_copy(comb, bank(5)[:, 0:T]).then_inc(s("comb_out"), 1)
                for c in range(XSET):
                    halve(c, st * PERX + (PERX + c + 1))
            add_back(n_rounds * E * KD)
            norm(5, h, T, [(u, GFIN)], rtb=frt, rsb=frs)

        @block.tensor
        def _(t_):
            pe = t_

            def norm(i, n, sqb=None):
                sqb = sq if sqb is None else sqb
                pe.wait_ge(s("ones_set"), 1)
                for k in range(KD):
                    pe.wait_ge(s("norm_sq"), KD * i + k + 1)
                    mm = pe.matmul(bank(0)[:, 0:n], ones[:, :], sqb[:, k * n:(k + 1) * n], start=(k == 0), stop=(k == KD - 1))
                mm.then_inc(s("norm_ss"), 1)

            norm(0, T)
            pe.wait_ge(s("consts_loaded"), 48)
            pe.wait_ge(s("norm_u"), 8)
            wb = wba[:, :].rearrange("p (k c) -> p k c", k=KD)
            for t in range(3):
                n = P if t < 2 else NS
                for k in range(KD):
                    mm = pe.matmul(bank(1)[0:n, 16 * t:16 * t + 16], u[:, k, t * P:t * P + n], wb[:, k, :],
                                   start=(k == 0), stop=(k == KD - 1))
            mm.then_inc(s("ba_mm"), 1)
            norm(1, NM)
            pe.wait_ge(s("norm_rt"), 2)
            pe.wait_ge(s("gba_out"), 2)
            for t in range(36):
                w = arrived(pe, AT["a_in", t // 4]).rearrange("p (k c) -> p k c", k=KD)
                if t >= 8:
                    pe.wait_ge(s("ain_out"), t - 7)
                for k in range(KD):
                    mm = pe.matmul(bank(t % 8)[:, 0:T], w[:, k, (t % 4) * P:(t % 4 + 1) * P], u[:, k, :],
                                   start=(k == 0), stop=(k == KD - 1))
                mm.then_inc(s("ain_mm"), 1)
            pe.wait_ge(s("ain_out"), 36)
            pe.wait_ge(s("norm_u"), 24)
            for l in range(2):
                w = arrived(pe, AT["mkv", 2 * l]).rearrange("p (k c) -> p k c", k=KD)
                if l:
                    pe.wait_ge(s("mem_kv"), 8)
                for x in range(4):
                    for k in range(KD):
                        mm = pe.matmul(bank(x)[:, 0:NM], w[:, k, x * P:(x + 1) * P], memn[l][:, k, :],
                                       start=(k == 0), stop=(k == KD - 1))
                    mm.then_inc(s("mkv_mm"), 1)
                w = arrived(pe, AT["mkv", 2 * l + 1]).rearrange("p (k c) -> p k c", k=KD)
                for x in range(2):
                    for k in range(KD):
                        mm = pe.matmul(bank(4 + x), memn[l][:, k, x * P:(x + 1) * P], w[:, k, :],
                                       start=(k == 0), stop=(k == KD - 1))
                    mm.then_inc(s("mkv_mm"), 1)
            pe.wait_ge(s("mem_kv"), 16)
            for g in range(4):
                pe.wait_ge(s("l2_sq"), g + 1)
                if g:
                    pe.wait_ge(s("l2_rt"), 2 * g)
                for x in range(4):
                    mm = pe.matmul(bank(x)[:, 0:ACTW], ones[:, :], sqq[:, x * ACTW:(x + 1) * ACTW], start=True, stop=True)
                mm.then_inc(s("l2_mm"), 1)
            pe.wait_ge(s("l2_rt"), 8)
            pe.wait_ge(s("consts_loaded"), 48)
            pe.wait_ge(s("gate_done"), 2)
            gp = gg[:, 0:2, :].rearrange("p t c -> p (t c)")
            pe.matmul(bank(0)[:, 0:16], tri, gp, start=True, stop=True)
            pe.matmul(bank(0)[:, 16:32], ones[:, :], gp, start=True, stop=True)
            pe.matmul(bank(0)[:, 32:160], ones[0:NS, :], gd[0:NS, :], start=True, stop=True).then_inc(s("coef_mm"), 1)

            def attention(l, first, last):
                for t in range(2):
                    for x in range(XH):
                        mm = pe.matmul(PP[t][:, x * NM:(x + 1) * NM], cq[:, x, t * P:(t + 1) * P],
                                       mk[l][:, x * NM:(x + 1) * NM], start=True, stop=True)
                    mm.then_inc(s("att_mm"), 1)
                for t in range(2):
                    pe.wait_ge(s("att_p"), 3 * l + t + 1)
                    for n in range(XH * MT):
                        mm = pe.transpose(PP[2 + t][:, n * P:(n + 1) * P], Pr[:, t * 1024 + n * P:t * 1024 + (n + 1) * P], ident)
                    mm.then_inc(s("att_tr"), 1)
                pe.wait_ge(s("att_pt"), 2 * l + 2)
                for x in range(XH):
                    for m in range(MT):
                        mm = pe.matmul(PP[0][:, x * SEQ:(x + 1) * SEQ], mv[l][:, m * 512 + x * P:m * 512 + (x + 1) * P],
                                       PrT[:, (x * MT + m) * SEQ:(x * MT + m + 1) * SEQ], start=(m == 0), stop=(m == MT - 1))
                mm.then_inc(s("att_o"), 1)
                pe.wait_ge(s("att_cat"), 2 * l + 1)
                kd, vd = f"kc{l}", f"vc{l}"
                for n in range(BH):
                    b, x = n // XH, n % XH
                    w = arrived(pe, AT[kd, n // 16]) if n % 16 == 0 else w
                    for m in range(MT):
                        mm = pe.matmul(bank(0)[:, m * BH + n:m * BH + n + 1],
                                       w[:, (n % 16) * NM + m * P:(n % 16) * NM + (m + 1) * P],
                                       cq[:, x, SEQ + b:SEQ + b + 1], start=True, stop=True)
                    if n % 16 == 15:
                        mm.then_inc(s("cache_mm"), 1)
                pe.wait_ge(s("sat_st"), 1 * l + 1)
                for m in range(MT):
                    mm = pe.transpose(bank(1)[0:BH, m * P:(m + 1) * P], STs[:, m * BH:(m + 1) * BH], ident)
                mm.then_inc(s("sat_s"), 1)
                pe.wait_ge(s("att_p"), 3 * l + 3)
                for m in range(MT):
                    mm = pe.transpose(bank(2)[:, m * BH:(m + 1) * BH], P32[0:BH, m * P:(m + 1) * P], ident[0:BH, 0:BH])
                mm.then_inc(s("att_tr"), 1)
                pe.wait_ge(s("sat_pt"), 1 * l + 1)
                for n in range(BH):
                    b, x = n // XH, n % XH
                    w = arrived(pe, AT[vd, b // 4]) if n % 16 == 0 else w
                    for m in range(MT):
                        at = ((b % 4) * MT + m) * 512 + x * P
                        mm = pe.matmul(bank(3)[:, n:n + 1], w[:, at:at + P], PT32[:, m * BH + n:m * BH + n + 1],
                                       start=(m == 0), stop=(m == MT - 1))
                    if n % 16 == 15:
                        mm.then_inc(s("cache_mm"), 1)

            pe.wait_ge(s("coef_dif"), 1)
            pe.wait_ge(s("l2_done"), 4)
            attention(0, None, None)

            for c in range(NCH):
                cols = slice(c * P, (c + 1) * P)
                pe.wait_ge(s("att_cat"), 2)
                if c:
                    pe.wait_ge(s("dl_cat"), c)
                    pe.wait_ge(s("S_done"), c)
                for x in range(H):
                    gcol = gg[:, c, x:x + 1].to_broadcast([P, P])
                    mm = pe.matmul(PP[0][:, x * P:(x + 1) * P], gcol, tri, start=True, stop=True)
                mm.then_inc(s("dl_grow"), 1)
                for w_, (m0, m1) in enumerate(((8, 0), (8, 8))):
                    for x in range(H):
                        mm = pe.matmul(PP[1 + w_][:, x * P:(x + 1) * P], act[:, m0 + x, cols], act[:, m1 + x, cols],
                                       start=True, stop=True)
                    mm.then_inc(s("dl_kk"), 1)
                for x in range(H):
                    mm = pe.matmul(PP[3][:, x * P:(x + 1) * P], gb[:, c, x:x + 1].to_broadcast([P, P]), ident,
                                   start=True, stop=True)
                mm.then_inc(s("dl_brow"), 1)
                if c == 0:
                    pe.wait_ge(s("conv_silu"), 24)
                pe.wait_ge(s("dl_pt"), c + 1)
                for x in range(H):
                    mm = pe.transpose(PP[1][:, x * P:(x + 1) * P], act[:, 16 + x, cols], ident)
                mm.then_inc(s("dl_tok"), 1)
                pe.wait_ge(s("dl_qd"), c + 1)
                for x in range(H):
                    mm = pe.transpose(PP[2][:, x * P:(x + 1) * P], act[:, 8 + x, cols], ident)
                mm.then_inc(s("dl_tok"), 1)
                pe.wait_ge(s("dl_kt"), c + 1)
                for lv in range(1, NLVL):
                    n0 = (c * (NLVL - 1) + lv - 1) * 2
                    u0 = (c * NLVL + lv) * 2
                    for g in range(2):
                        pe.wait_ge(s("dl_um"), u0 - 2 + g + 1)
                        if n0 + g >= 2:
                            pe.wait_ge(s("dl_t"), n0 + g - 1)
                        for x in range(4 * g, 4 * g + 4):
                            mm = pe.transpose(PP[0][:, x * P:(x + 1) * P], Ub[:, x * P:(x + 1) * P], ident)
                        mm.then_inc(s("dl_tt"), 1)
                    pe.wait_ge(s("dl_ml"), c * NLVL + lv + 1)
                    for g in range(2):
                        pe.wait_ge(s("dl_t"), n0 + g + 1)
                        if n0 + g >= 2:
                            pe.wait_ge(s("dl_x"), n0 + g - 1)
                        for x in range(4 * g, 4 * g + 4):
                            mm = pe.matmul(PP[1][:, x * P:(x + 1) * P], MLb[:, x * P:(x + 1) * P], Tb[:, x * P:(x + 1) * P],
                                           start=True, stop=True)
                        mm.then_inc(s("dl_xx"), 1)
                    for g in range(2):
                        pe.wait_ge(s("dl_x"), n0 + g + 1)
                        for x in range(4 * g, 4 * g + 4):
                            mm = pe.matmul(PP[2][:, x * P:(x + 1) * P], Xb[:, x * P:(x + 1) * P], Ub[:, x * P:(x + 1) * P],
                                           start=True, stop=True)
                        mm.then_inc(s("dl_du"), 1)
                pe.wait_ge(s("dl_um"), (c + 1) * NLVL * 2)
                R = vtok
                if c:
                    for x in range(H):
                        mm = pe.matmul(PP[0][:, x * P:(x + 1) * P], act[:, 8 + x, cols], Sb[:, x * P:(x + 1) * P],
                                       start=True, stop=True)
                    mm.then_inc(s("dl_ks"), 1)
                    pe.wait_ge(s("dl_r"), 1)
                    R = Xb
                for x in range(H):
                    mm = pe.matmul(PP[1][:, x * P:(x + 1) * P], Ub[:, x * P:(x + 1) * P], R[:, x * P:(x + 1) * P],
                                   start=True, stop=True)
                mm.then_inc(s("dl_uu"), 1)
                pe.wait_ge(s("dl_u"), c + 1)
                uu = Tb
                for x in range(H):
                    if c:
                        pe.matmul(PP[2][:, x * P:(x + 1) * P], Sb[:, x * P:(x + 1) * P], act[:, x, cols], start=True, stop=False)
                    mm = pe.matmul(PP[2][:, x * P:(x + 1) * P], uu[:, x * P:(x + 1) * P], PTb[:, x * P:(x + 1) * P],
                                   start=(c == 0), stop=True)
                mm.then_inc(s("dl_o"), 1)
                for x in range(H):
                    mm = pe.matmul(PP[3][:, x * P:(x + 1) * P], ktail[:, x * P:(x + 1) * P], uu[:, x * P:(x + 1) * P],
                                   start=True, stop=True)
                mm.then_inc(s("dl_ds"), 1)

            pe.wait_ge(s("dl_cat"), NCH)
            pe.wait_ge(s("S_done"), NCH)
            pe.wait_ge(s("sd_cols"), 1)
            for i in range(2):
                w = arrived(pe, AT["state", i])
                for n in range(32 * i, 32 * i + 32):
                    mm = pe.matmul(bank(0)[:, 2 * n:2 * n + 2], w[:, (n % 32) * P:(n % 32 + 1) * P], kq[:, n, :],
                                   start=True, stop=True)
                mm.then_inc(s("state_mm"), 1)
            pe.matmul(bank(1)[:, 0:64], ones[:, :], kqd, start=True, stop=True).then_inc(s("sd_mm"), 1)
            pe.transpose(bank(4)[0:DBH, 0:P], t64, ident).then_inc(s("sd_rows"), 1)
            pe.wait_ge(s("sd_u"), 1)
            pe.transpose(bank(5)[0:DBH, 0:P], u64, ident).then_inc(s("sd_rows"), 1)
            pe.wait_ge(s("sd_row"), 2)
            for g in range(16):
                pe.wait_ge(s("sd_blk"), g + 1)
                if g >= 2:
                    pe.wait_ge(s("state_new"), g - 1)
                pe.matmul(bank(2 + g % 2), krow[0:DBH, :], ublk[g % 2][0:DBH, :], start=True, stop=True)\
                    .then_inc(s("sd_outer"), 1)
            pe.wait_ge(s("state_new"), 16)
            pe.wait_ge(s("sd_cat"), 1)
            for x in range(H):
                pe.wait_ge(s("on_sq"), x + 1)
                pe.matmul(bank(x)[:, 0:T], ones[:, :], sq[:, x * T:(x + 1) * T], start=True, stop=True).then_inc(s("on_mm"), 1)

            def project(kind, name, nk, per, src, free):
                for t in range(KD):
                    w = arrived(pe, AT[kind, t // per]).rearrange("p (k c) -> p k c", k=nk)
                    free(t)
                    for k in range(nk):
                        mm = pe.matmul(bank(t)[:, 0:T], w[:, k, (t % per) * P:(t % per + 1) * P], src[:, k, :],
                                       start=(k == 0), stop=(k == nk - 1))
                    mm.then_inc(s(f"{name}_mm"), 1)

            pe.wait_ge(s("on_done"), H)
            project("a_out", "aout", 12, 2, cat, lambda t: None)
            pe.wait_ge(s("aout_h"), KD)
            norm(2, T)
            pe.wait_ge(s("norm_u"), 32)
            for f in range(FT):
                w = arrived(pe, AT["wi", f // 2]).rearrange("p (k g c) -> p k g c", k=KD, g=2)
                if f >= 4:
                    pe.wait_ge(s("wi_hid"), f - 3)
                for g in range(2):
                    for k in range(KD):
                        mm = pe.matmul(bank(2 * (f % 4) + g)[:, 0:T], w[:, k, g, (f % 2) * P:(f % 2 + 1) * P], u[:, k, :],
                                       start=(k == 0), stop=(k == KD - 1))
                mm.then_inc(s("wi_mm"), 1)
            pe.wait_ge(s("wi_hid"), FT)
            project("wo", "wo", FT, 1, hid, lambda t: None)
            pe.wait_ge(s("wo_h"), KD)
            norm(3, T)
            pe.wait_ge(s("norm_u"), 40)
            for t in range(12):
                w = arrived(pe, AT["b_in", t // 4]).rearrange("p (k c) -> p k c", k=KD)
                if t >= 8:
                    pe.wait_ge(s("bin_out"), t - 7)
                for k in range(KD):
                    mm = pe.matmul(bank(t % 8)[:, 0:T], w[:, k, (t % 4) * P:(t % 4 + 1) * P], u[:, k, :],
                                   start=(k == 0), stop=(k == KD - 1))
                mm.then_inc(s("bin_mm"), 1)
            pe.wait_ge(s("bin_out"), 12)
            pe.wait_ge(s("pool_d"), 1)
            w = arrived(pe, AT["pool", 0]).rearrange("p (g k c) -> p g k c", g=4, k=2)
            for t in range(8):
                for k in range(2):
                    mm = pe.matmul(bank(t)[:, 0:T], w[:, t // 2, k, (t % 2) * P:(t % 2 + 1) * P], pd[:, (t // 2) * 2 + k, :],
                                   start=(k == 0), stop=(k == 1))
                mm.then_inc(s("pm_mm"), 1)
            pe.wait_ge(s("pm_cat"), 8)
            attention(1, None, None)
            pe.wait_ge(s("att_cat"), 4)
            project("b_out", "bout", 12, 2, cat, lambda t: None)
            pe.wait_ge(s("bout_h"), KD)
            norm(4, T, sqb=fsq)
            pe.wait_ge(s("norm_u"), 48)
            pe.wait_ge(s("consts_loaded"), 48)
            rw = router[:, :].rearrange("p (k c) -> p k c", k=KD)
            for t in range(3):
                n = P if t < 2 else NS
                for k in range(KD):
                    mm = pe.matmul(bank(0)[0:n, E * t:E * t + E], u[:, k, t * P:t * P + n], rw[:, k, :],
                                   start=(k == 0), stop=(k == KD - 1))
            mm.then_inc(s("rt_mm"), 1)
            for t in range(3):
                n = P if t < 2 else NS
                for k in range(KD):
                    mm = pe.transpose(PP[1 + t][0:n, k * P:(k + 1) * P], u[:, k, t * P:t * P + n], ident)
                mm.then_inc(s("xt_mm"), 1)
            pe.wait_ge(s("rt_sub"), 1)
            sel = rr[2]
            pe.matmul(bank(0)[:, 0:8], stri, sel[:, 0:8], start=True, stop=True)
            pe.matmul(bank(0)[:, 8:16], stri, sel[:, 8:16], start=True, stop=False)
            pe.matmul(bank(0)[:, 8:16], ones[:, :], sel[:, 0:8], start=False, stop=True)
            pe.matmul(bank(0)[:, 16:24], stri, sel[:, 16:24], start=True, stop=False)
            pe.matmul(bank(0)[:, 16:24], ones[:, :], sel[:, 0:8], start=False, stop=False)
            pe.matmul(bank(0)[:, 16:24], ones[:, :], sel[:, 8:16], start=False, stop=True)
            pe.matmul(bank(0)[:, 24:32], ones[:, :], sel[:, 0:8], start=True, stop=False)
            pe.matmul(bank(0)[:, 24:32], ones[:, :], sel[:, 8:16], start=False, stop=False)
            pe.matmul(bank(0)[:, 24:32], ones[0:NS, :], sel[0:NS, 16:24], start=False, stop=True).then_inc(s("pos_mm"), 1)

            def gather():
                for k in range(KD):
                    for t in range(3):
                        n = P if t < 2 else NS
                        mm = pe.matmul(PP[1][:, k * C:(k + 1) * C], xtok[0:n, t, k * P:(k + 1) * P], disp[0:n, t, :],
                                       start=(t == 0), stop=(t == 2))
                mm.then_inc(s("gat_mm"), 1)

            pe.wait_ge(s("xt_out"), 3)
            pe.wait_ge(s("disp"), 3)
            gather()
            pe.wait_ge(s("steps_known"), 1)
            n_rounds = pe.value_load(nsteps_i[0:1, 0:1], min_val=1, max_val=ROUNDS)

            def split_product(out, lhs, rhs, first, last):
                for i, (l, r) in enumerate(((0, 0), (0, 1), (1, 0))):
                    mm = pe.matmul(out, lhs[l], rhs[r], start=first and i == 0, stop=last and i == 2)
                return mm

            def combine(before):
                for t in range(KD):
                    if t >= 4:
                        pe.wait_ge(s("comb_h"), before + (t - 3))
                    pe.matmul(bank(2 + t % 4)[:, 0:T], yslot[:, t * P:(t + 1) * P], comb, start=True, stop=True)\
                        .then_inc(s("cmb_mm"), 1)

            with pe.Fori(0, n_rounds * E) as st:
                def up(c):
                    f, g = c // 4, c // 2 % 2
                    pe.wait_ge(s("w_lo"), st * PERX + (c + 1))
                    w = [as_chunk(x[c % XSET][:, :], c) for x in (whi, wlo)]
                    for k in range(4):
                        kk = (c % 2) * 4 + k
                        mm = split_product(bank(2 * (f % 2) + g), [x[:, kk * C:(kk + 1) * C] for x in (xsh, xsl)],
                                           [x[:, k, :] for x in w], kk == 0, kk == KD - 1)
                    mm.then_inc(s("up_mm"), 1)

                def turn(f):
                    pe.wait_ge(s("up_h"), st * FCN + (f + 1))
                    if f >= 2:
                        pe.wait_ge(s("ht_lo"), st * FCN + (f - 1))
                    for x in range(4):
                        mm = pe.transpose(bank(4 + f % 2)[:, x * C:(x + 1) * C], hslot[f % 2][:, x * P:(x + 1) * P], ident)
                    mm.then_inc(s("ht_mm"), 1)

                pe.wait_ge(s("xs_lo"), st + 1)
                for c in range(NUP):
                    if c % 4 == 0 and c >= 8:
                        pe.wait_ge(s("up_h"), st * FCN + (c // 4 - 1))
                    if c == 4:
                        pe.wait_ge(s("comb_h"), st * KD + KD)
                    up(c)
                    if c == 1:
                        pe.wait_ge(s("y_out"), st + 1)
                        pe.wait_ge(s("comb_out"), st + 1)
                        combine(st * KD)
                    if c % 4 == 3 and c > 3:
                        turn(c // 4 - 1)
                pe.wait_ge(s("disp"), st * 3 + 6)
                pe.wait_ge(s("up_h"), st * FCN + (FCN - 1))
                gather()
                turn(FCN - 1)
                for j in range(NDOWN):
                    c = NUP + j
                    pe.wait_ge(s("w_lo"), st * PERX + (c + 1))
                    pe.wait_ge(s("ht_lo"), st * FCN + (j // 2 + 1))
                    w = [as_chunk(x[c % XSET][:, :], c) for x in (whi, wlo)]
                    for k in range(2):
                        kk = 2 * j + k
                        for g in range(2):
                            mm = split_product(bank(6 + g), [x[:, kk * C:(kk + 1) * C] for x in (hTh, hTl)],
                                               [x[:, k, g * 512:(g + 1) * 512] for x in w], kk == 0, kk == KE - 1)
                    mm.then_inc(s("down_mm"), 1)
                    if j == 4:
                        pe.wait_ge(s("dispg"), st * 3 + 3)
                        pe.wait_ge(s("up_h"), st * FCN + FCN)
                        pe.wait_ge(s("ht_lo"), st * FCN + (FCN - 1))
                        for t in range(3):
                            n = P if t < 2 else NS
                            mm = pe.transpose(bank(5)[:, t * P:t * P + n], dispg[0:n, t, :], ident[0:n, 0:n])
                        mm.then_inc(s("cmb_tr"), 1)
            pe.wait_ge(s("y_out"), n_rounds * E + 1)
            pe.wait_ge(s("comb_out"), n_rounds * E + 1)
            pe.wait_ge(s("xs_lo"), n_rounds * E + 1)
            combine(n_rounds * E * KD)
            pe.wait_ge(s("comb_h"), n_rounds * E * KD + KD)
            norm(5, T, sqb=fsq)


def kernel(**inputs):
    import concourse.bacc as bacc
    from concourse.bass_utils import run_bass_kernel_spmd

    f = {k: np.asarray(v) for k, v in inputs.items()}

    def fm(x):
        t, d = x.shape
        return x.T.reshape(d // P, P, t).transpose(1, 0, 2).reshape(P, -1)

    def tiles(w, per):
        k, n = w.shape
        return w.reshape(k // P, P, n // per, per).transpose(2, 1, 0, 3).reshape(n // per, P, -1)

    def col(g):
        return g.reshape(-1, P).T

    def rows(g):
        return np.broadcast_to(g.reshape(1, -1), (P, g.size))

    w_in = f["a_w_in"][0]
    split = CT * P + H * P
    ff = f["a_ffn_wi"][0]
    ffa = ff.reshape(KD, P, 2, FT // 2, 256).transpose(3, 1, 0, 2, 4).reshape(FT // 2, P, -1)
    kc = f["cache_mem_k"]
    vc = f["cache_mem_v"]
    i = np.arange(P)
    J, I = i[:, None], i[None, :]
    lvl = [((I >> (l + 1)) == (J >> (l + 1))) & (((I >> l) & 1) == 1) & (((J >> l) & 1) == 0) for l in range(NLVL)]
    tie = (np.arange(E)[None, :] < np.arange(E)[:, None]).reshape(1, -1)
    cinv = np.stack([1.0 / np.minimum(np.arange(16) + 1, 2 << g) for g in range(4)]).reshape(1, -1)
    consts = np.concatenate([J == I, J <= I, J < I, np.where(J <= I, 0.0, -1e30)] + lvl
                            + [np.broadcast_to(I, (P, P)), np.broadcast_to(tie, (P, E * E)),
                               np.broadcast_to(cinv, (P, 64))], axis=1).astype(np.float32)
    gains = np.concatenate([col(f["a_norm1"]), col(f["a_norm2"]), col(f["b_norm1"]), col(f["b_norm2"]),
                            col(f["final_norm"]), col(f["m_norm"][0]), col(f["m_norm"][1]), col(f["b_pool_scale"]),
                            col(f["a_o_norm"]),
                            f["a_conv_w"][0].reshape(CW, CT, P).transpose(2, 1, 0).reshape(P, -1),
                            rows(f["a_a_log"]), rows(f["a_dt_bias"])], axis=1)
    arrays = {
        "x": fm(np.concatenate([f["x_prompt"][0], f["x_sample"][:, 0]], axis=0)),
        "mem": fm(f["mem_prompt"][0]),
        "gains": gains,
        "consts": consts,
        "wba": w_in[:, split:split + 16].reshape(KD, P, 16).transpose(1, 0, 2).reshape(P, -1),
        "router": f["b_router"][0].reshape(KD, P, E).transpose(1, 0, 2).reshape(P, -1),
        "convbuf": f["state_dn_conv"][0].reshape(NS, CW - 1, CT, P).transpose(3, 2, 0, 1).reshape(P, -1),
        "poolbuf": f["state_pool"][0].reshape(NS, PW, KD, P).transpose(3, 2, 0, 1).reshape(P, -1),
        "a_in": tiles(np.concatenate([w_in[:, :split], w_in[:, split + 16:]], axis=1), 512),
        "mkv": np.concatenate([tiles(f[n][l], 512) for l in range(2) for n in ("m_w_k", "m_w_v")]),
        "state": f["state_dn"][0].reshape(2, 32, P, P).transpose(0, 2, 1, 3).reshape(2, P, -1),
        "a_out": tiles(f["a_w_out"][0], 256),
        "wi": ffa,
        "wo": tiles(f["a_ffn_wo"][0], P),
        "b_in": tiles(f["b_w_in"][0], 512),
        "pool": f["b_pool_w"].reshape(1, 4, 2, P, 256).transpose(0, 3, 1, 2, 4).reshape(1, P, -1),
        "b_out": tiles(f["b_w_out"][0], 256),
        "wi_e": f["b_moe_wi"][0],
        "wo_e": f["b_moe_wo"][0],
    }
    for l in range(2):
        arrays[f"kc{l}"] = kc[l].reshape(2, 4, NM, XH, P).transpose(0, 4, 1, 3, 2).reshape(2, P, -1)
        arrays[f"vc{l}"] = vc[l].reshape(2, 4, MT, P, XH * P).transpose(0, 3, 1, 2, 4).reshape(2, P, -1)
    shapes = {"y": (P, KD * T), "S": (P, 1024), "conv": (P, 648), "pool": (P, 8 * 135), "mk": (2, P, 1024),
              "mv": (2, P, 1024), "state": (2, P, SLOT)}
    nc = bacc.Bacc("TRN2", target_bir_lowering=False, num_devices=1)
    ins = {}
    sent = {}
    for name, a in arrays.items():
        a = np.ascontiguousarray(a)
        sent[f"in_{name}"] = a
        ins[name] = nc.dram_tensor(f"in_{name}", a.shape, F32, kind="ExternalInput").ap()
    outs = {n: nc.dram_tensor(f"out_{n}", sh, F32, kind="ExternalOutput").ap() for n, sh in shapes.items()}
    build(nc, ins, outs)
    r = run_bass_kernel_spmd(nc, [sent], core_ids=[0])
    o = {n: r.results[0][f"out_{n}"] for n in shapes}

    y = o["y"].reshape(P, KD, T).transpose(2, 1, 0).reshape(T, D)
    S = o["S"].reshape(P, H, P).transpose(1, 0, 2)[None, None]
    cv = o["conv"].reshape(P, CT, 27).transpose(2, 1, 0).reshape(27, CT * P)
    pl = o["pool"].reshape(P, KD, 135).transpose(2, 1, 0).reshape(135, D)
    mk = o["mk"].reshape(2, P, XH, NM).transpose(0, 3, 2, 1)[:, None]
    mv = o["mv"].reshape(2, P, MT, XH, P).transpose(0, 2, 1, 3, 4).reshape(2, 1, NM, XH, P)
    st = o["state"].reshape(2, P, 32, P).transpose(0, 2, 1, 3).reshape(1, NS, H, P, P)
    c = np.ascontiguousarray
    return (c(y[None, :SEQ]), c(y[SEQ:, None]), c(S), c(cv[None, None, :3]), c(pl[None, None, :PW]), c(mk), c(mv), c(st),
            c(cv[3:].reshape(1, NS, CW - 1, CT * P)), c(pl[PW:].reshape(1, NS, PW, D)))
```

```python
from contextlib import ExitStack

import numpy as np
import concourse.bass as bass
from concourse import mybir

F32 = mybir.dt.float32
F32R = mybir.dt.float32r
I32 = mybir.dt.int32
ALU = mybir.AluOpType
ACT = mybir.ActivationFunctionType
AX = mybir.AxisListType.X

P = 128
D = 1024
KD = D // P
SEQ, NS = 256, 8
T = SEQ + NS
H = 8
NCH = SEQ // P
CW = 4
CT = 24
PRE = CW - 1 + SEQ + CW * NS
ACTW = PRE - (CW - 1)
S0 = SEQ + CW - 1
XH = 4
NM = 256
MT = NM // P
BH = NS * XH
DBH = NS * H
FF = 2816
FT = FF // P
E = 8
FE = 3584
FCN = FE // 512
KE = FE // P
C = P
ROUNDS = -(-T // C)
PW = 15
PCOL = PW + SEQ + (PW + 1) * NS
EPS = 1e-6
DCH = 2048
DRAW = 2
DSET = 2
ARENA = DRAW * DCH + DSET * 2 * DCH
WREG = 28672
PERX = 42
NUP, NDOWN = 28, 14
XCH = 2048
XRAW = 7
XSET = 3
assert PERX % XRAW == 0 and PERX % XSET == 0
TURNED = {4 * f + 10: f for f in range(FE // 512 - 1)} | {32: FE // 512 - 1}
NLVL = 7

KINDS = [("mkv", 8, 2048, True), ("a_in", 18, 2048, True), ("kc0", 4, 2048, False), ("vc0", 4, 2048, False),
         ("a_out", 8, 12 * P, True), ("wi", 22, 2048, True),
         ("wo", 16, FT // 2 * P, True), ("b_in", 6, 2048, True), ("pool", 1, 2048, False),
         ("kc1", 4, 2048, False), ("vc1", 4, 2048, False), ("b_out", 8, 12 * P, True)]
DENSE = [(kind, i) for kind, n, _, _ in KINDS for i in range(n)]
ND = len(DENSE)
AT = {c: n for n, c in enumerate(DENSE)}
WIDTH = {kind: w for kind, _, w, _ in KINDS}
SPLIT = {kind: x for kind, _, _, x in KINDS}
HALVED = [n for n, (kind, _) in enumerate(DENSE) if SPLIT[kind]]
TURN = {n: q for q, n in enumerate(HALVED)}
RUN = {n: ("mkv", "a_in").count(k) or 2 * ("a_out", "wi", "wo", "b_in").count(k) or 3 for n, (k, _) in enumerate(DENSE)}
CHUNKS = {"aout": "a_out", "wo": "wo", "bout": "b_out"}

CIDENT, CTRI, CSTRI, CNEG, CLVL = 0, P, 2 * P, 3 * P, 4 * P
CIOTA = CLVL + NLVL * P
CTIE = CIOTA + P
CINV = CTIE + E * E
CN = CINV + 4 * 16
GA1, GA2, GB1, GB2, GFIN, GM0, GM1, GPS = (8 * i for i in range(8))
GON = 64
GTAP = 65
GALOG = GTAP + CT * CW
GDT = GALOG + H
GN = GDT + H


def build(nc, ins, outs):
    ctx = ExitStack()
    with ctx:
        def sb(name, n, dt=F32):
            return ctx.enter_context(nc.sbuf_tensor(name, [P, n], dt))

        def sem(name):
            return ctx.enter_context(nc.semaphore(name))

        consts = sb("consts", CN)
        gains = sb("gains", GN)
        wba = sb("wba", KD * 16)
        router = sb("router", KD * E)
        ones = sb("ones", P)
        epsc = sb("epsc", 1)
        small = sb("small", 840)
        nsteps_i = sb("nsteps_i", 1, I32)
        hbuf = sb("hbuf", KD * T)
        ubuf = sb("ubuf", KD * T)
        base = (nc.sbuf_base + 63) // 64 * 64
        sb("weights", WREG + 32)

        def at(name, off, n, dt):
            return nc.alloc_sbuf_tensor_at(name, [P, n], dt, offset=base + 4 * off)

        ring = at("ring", 0, WREG, F32)
        whi = [at(f"whi{i}", 2 * i * XCH, XCH, F32R) for i in range(XSET)]
        wlo = [at(f"wlo{i}", (2 * i + 1) * XCH, XCH, F32R) for i in range(XSET)]
        assert 2 * XSET * XCH <= ARENA
        draw = [ring[:, i * DCH:(i + 1) * DCH] for i in range(DRAW)]
        dhi = [at(f"dhi{i}", DRAW * DCH + 2 * i * DCH, DCH, F32R) for i in range(DSET)]
        dlo = [at(f"dlo{i}", DRAW * DCH + (2 * i + 1) * DCH, DCH, F32R) for i in range(DSET)]
        raw = at("raw", 2 * XSET * XCH, XRAW * XCH, F32)
        tail = (2 * XSET + XRAW) * XCH
        PP = [ctx.enter_context(nc.psum_tensor(f"PP{i}", [P, 1024], F32)) for i in range(4)]

        def bank(b):
            return PP[b // 2][:, (b % 2) * 512:(b % 2) * 512 + 512]

        ident = consts[:, CIDENT:CIDENT + P]
        tri = consts[:, CTRI:CTRI + P]
        stri = consts[:, CSTRI:CSTRI + P]
        neg = consts[:, CNEG:CNEG + P]
        iota = consts[:, CIOTA:CIOTA + P]
        h = hbuf[:, :].rearrange("p (k t) -> p k t", k=KD)
        u = ubuf[:, :].rearrange("p (k t) -> p k t", k=KD)

        def cut(buf, at, n):
            return buf[:, at:at + n]

        arena = ARENA
        pre = cut(ring, arena, CT * PRE).rearrange("p (m c) -> p m c", m=CT)
        act = cut(ring, arena + CT * PRE, CT * ACTW).rearrange("p (m c) -> p m c", m=CT)
        z = cut(ring, arena + CT * (PRE + ACTW), H * T).rearrange("p (m c) -> p m c", m=H)
        assert CT * (PRE + ACTW) + H * T <= WREG - ARENA
        state = ring[:, DRAW * DCH:DRAW * DCH + DBH * P]
        assert DBH * P == DSET * 2 * DCH
        memh = [at(f"memh{i}", arena + 4096 * i, 2048, F32R) for i in range(2)]
        meml = [at(f"meml{i}", arena + 4096 * i + 2048, 2048, F32R) for i in range(2)]
        cath = [at("cath0", arena, 12 * T, F32R)]
        catl = [at("catl0", arena + 12 * T, 12 * T, F32R)]
        hidh = at("hidh", arena, FT * T, F32R)
        hidl = at("hidl", arena + FT * T, FT * T, F32R)
        uh = [None, at("uh1", arena + 2 * FT * T, KD * T, F32R)]
        ul = [None, at("ul1", arena + 2 * FT * T + KD * T, KD * T, F32R)]
        assert 2 * FT * T + 2 * KD * T <= WREG - ARENA
        DTb, MTb, MLb, Xb, PTb, Sb = (cut(ring, arena + 1024 * i, 1024) for i in range(6))
        GEN = 1056 + 3168 + 4 * 1024 + 648 + 8100
        gbase = (nc.sbuf_base + 63) // 64 * 64
        sb("activations", GEN + 32)

        def gat_(name, off, n, dt=F32):
            return nc.alloc_sbuf_tensor_at(name, [P, n], dt, offset=gbase + 4 * off)

        gen = gat_("gen", 0, GEN)
        uh[0], ul[0] = gat_("uh0", 1056, KD * T, F32R), gat_("ul0", 8968 + 4688, KD * T, F32R)
        uh.append(gat_("uh2", 1056, KD * T, F32R))
        ul.append(gat_("ul2", 1056 + KD * T, KD * T, F32R))
        cath.append(gat_("cath1", 4224, 12 * T, F32R))
        catl.append(gat_("catl1", 8968, 12 * T, F32R))
        cq = cut(gen, 0, XH * T).rearrange("p (m c) -> p m c", m=XH)
        cat = cut(gen, 1056, 12 * T).rearrange("p (m c) -> p m c", m=12)
        mk = [cut(gen, 4224 + 2048 * i, 1024) for i in range(2)]
        mv = [cut(gen, 5248 + 2048 * i, 1024) for i in range(2)]
        convio = cut(gen, 8320, 648)
        SC = 8968
        SCN = GEN - SC
        memT = cut(gen, 1056, KD * NM).rearrange("p (k t) -> p k t", k=KD)
        sq = cut(gen, SC, KD * T)
        rt = cut(gen, SC + 2112, 264)
        rs = cut(gen, SC + 2376, 264)
        memn = [cut(gen, SC + 2640 + 2048 * i, 2048).rearrange("p (k t) -> p k t", k=KD) for i in range(2)]
        assert 2640 + 4096 <= SCN
        sqq = cut(gen, SC, 4 * ACTW)
        rsq = cut(gen, SC + 4 * ACTW, 4 * ACTW)
        Pr = cut(gen, SC, 2048)
        PrT = cut(gen, SC + 2048, 2048)
        STs = cut(gen, SC, 64)
        P32 = cut(gen, SC + 64, 256)
        PT32 = cut(gen, SC + 320, 64)
        Tb, Ub, vtok, ktail = (cut(gen, SC + 1024 * i, 1024) for i in range(4))
        DS = SC + 4096
        kq = cut(gen, DS, 128).rearrange("p (n c) -> p n c", c=2)
        v64 = cut(gen, DS + 128, 64)
        kqd = cut(gen, DS + 192, 64)
        t64 = cut(gen, DS + 256, 64)
        u64 = cut(gen, DS + 320, 64)
        qku = cut(gen, DS + 384, 64)
        krow = cut(gen, DS + 448, 128)
        urow = cut(gen, DS + 576, 128)
        ublk = [cut(gen, DS + 704 + 512 * i, 512) for i in range(2)]
        sil = [cut(gen, SC + 2640 + 264 * i, 264) for i in range(2)]
        hidf = [cut(gen, SC + 264 * i, 264) for i in range(2)]
        pin = cut(gen, SC, KD * PCOL).rearrange("p (m c) -> p m c", m=KD)
        psm = cut(gen, SC + KD * PCOL, KD * PCOL).rearrange("p (m c) -> p m c", m=KD)
        poolbuf = cut(gen, SC + KD * PCOL, KD * NS * PW)
        assert 2 * KD * PCOL <= SCN
        pst = cut(gen, 4224, 8 * 135)
        pd = cut(gen, 1056, KD * T).rearrange("p (m c) -> p m c", m=KD)
        pfix = cut(small, 512, 128)

        xtok = cut(gen, 0, 3 * D).rearrange("p (t c) -> p t c", t=3)
        hTh = gat_("hTh", 3072, KE * C, F32R)
        hTl = gat_("hTl", 3072 + KE * C, KE * C, F32R)
        xsh = gat_("xsh", 10240, KD * C, F32R)
        xsl = gat_("xsl", 11264, KD * C, F32R)
        yslot = cut(gen, 12288, D)
        disp = cut(gen, 13312, 384).rearrange("p (t c) -> p t c", t=3)
        dispg = cut(gen, 13696, 384).rearrange("p (t c) -> p t c", t=3)
        comb = cut(gen, 14080, T)
        esil = [cut(ubuf, 512 * i, 512) for i in range(2)]
        hslot = [cut(ubuf, 1024 + 512 * i, 512) for i in range(2)]
        rout = cut(ring, tail, 3 * E)
        rtmp = cut(ring, tail + 32, 3 * E * E)
        rtm2 = cut(ring, tail + 224, 3 * E * E)
        rr = [cut(ring, tail + 416 + 24 * i, 24) for i in range(8)]
        NSTX = (ROUNDS + 1) * E
        posx = cut(ring, tail + 608, NSTX * 3).rearrange("p (s t) -> p s t", t=3)
        gatex = cut(ring, tail + 608 + NSTX * 3, NSTX * 3).rearrange("p (s t) -> p s t", t=3)
        cnt8 = cut(ring, tail + 608 + 6 * NSTX, 16)
        fsq = cut(gen, 14400, KD * T)
        frt = cut(gen, 16512, 264)
        frs = cut(gen, 16776, 264)

        gba = cut(small, 0, 48).rearrange("p (t c) -> p t c", t=3)
        gx, gax, ge, gl, gg, gb = (cut(small, 48 + 24 * i, 24).rearrange("p (t c) -> p t c", t=3)
                                   for i in range(6))
        gea = cut(small, 192, 8)
        gd = cut(small, 200, 128)
        cG, cnG, cdl, ceG, ctail, ceGl, cbeG = (cut(small, 328 + 16 * i, 16) for i in range(7))
        sgb = cut(small, 440, 128)
        amx = cut(small, 568, 8)
        anm = cut(small, 576, 8)
        asum = cut(small, 584, 8)
        ars = cut(small, 592, 8)
        sgt = cut(small, 600, 128)
        cgt = cut(small, 728, 32)

        raw_loaded = [sem(f"raw_loaded{i}") for i in range(XRAW)]
        slot_loaded = [sem(f"slot_loaded{i}") for i in range(DRAW)]
        names = {}

        def s(name):
            if name not in names:
                names[name] = sem(name)
            return names[name]

        block = ctx.enter_context(nc.Block())

        def read_by(n):
            kind, i = DENSE[n]
            return {"mkv": ("mkv_mm", 2 * (i + 1)), "a_in": ("ain_mm", 2 * (i + 1)),
                    "kc0": ("cache_mm", i + 1), "vc0": ("cache_mm", i + 5),
                    "a_out": ("aout_mm", i + 1), "wi": ("wi_mm", i + 1), "wo": ("wo_mm", i + 1),
                    "b_in": ("bin_mm", 2 * (i + 1)), "pool": ("pm_mm", 8),
                    "kc1": ("cache_mm", i + 9), "vc1": ("cache_mm", i + 13), "b_out": ("bout_mm", i + 1)}[kind]

        def arrived(eng, n):
            eng.wait_ge(slot_loaded[n % DRAW], 16 * (n // DRAW + 1))
            return draw[n % DRAW][:, 0:WIDTH[DENSE[n][0]]]

        def halves(n):
            q, w = TURN[n], WIDTH[DENSE[n][0]]
            return dhi[q % DSET][:, 0:w], dlo[q % DSET][:, 0:w]

        def dense_high(a, n):
            x, q = arrived(a, n), TURN[n]
            if q >= DSET:
                name, count = read_by(HALVED[q - DSET])
                a.wait_ge(s(name), count)
            a.activation(halves(n)[0], x, ACT.Copy).then_inc(s("d_hi"), 1)

        def dense_low(v, n):
            v.wait_ge(s("d_hi"), TURN[n] + 1)
            high, low = halves(n)
            v.tensor_tensor(low, draw[n % DRAW][:, 0:WIDTH[DENSE[n][0]]], high.bitcast(F32), ALU.subtract)\
                .then_inc(s("d_lo"), 1)

        wi_e = ins["wi_e"].rearrange("e (k p) n -> e p k n", p=P)
        wo_e = ins["wo_e"].rearrange("e (k p) n -> e p k n", p=P)

        def expert_source(e, c):
            if c < NUP:
                col = (c // 2 % 2) * FE + (c // 4) * 512
                k = 4 * (c % 2)
                return wi_e[bass.ds(e, 1), :, k:k + 4, col:col + 512].rearrange("e p k n -> p (e k) n")
            k = 2 * (c - NUP)
            return wo_e[bass.ds(e, 1), :, k:k + 2, :].rearrange("e p k n -> p (e k) n")

        def as_chunk(buf, c):
            return buf.rearrange("p (k n) -> p k n", n=512 if c < NUP else D)

        def raw_of(c):
            return cut(raw, (c % XRAW) * XCH, XCH)

        def new_state(v, g):
            v.wait_ge(s("sd_outer"), g + 1)
            for x in range(4):
                sl = state[:, (4 * g + x) * P:(4 * g + x + 1) * P]
                ins_ = v.scalar_tensor_tensor(out=sl, in0=sl, scalar=sgb[:, 4 * g + x:4 * g + x + 1],
                                              in1=bank(2 + g % 2)[:, x * P:(x + 1) * P], op0=ALU.mult, op1=ALU.add)
            ins_.then_inc(s("state_new"), 1)

        @block.sync
        def _(sp):
            sp.dma_start(hbuf[:, :], ins["x"]).then_inc(s("x_loaded"), 16)
            sp.dma_start(memT, ins["mem"].rearrange("p (k t) -> p k t", k=KD)).then_inc(s("mem_loaded"), 16)
            sp.dma_start(gains[:, :], ins["gains"]).then_inc(s("x_loaded"), 16)
            sp.dma_start(consts[:, :], ins["consts"]).then_inc(s("consts_loaded"), 16)
            sp.dma_start(router[:, :], ins["router"]).then_inc(s("consts_loaded"), 16)
            sp.dma_start(wba[:, :], ins["wba"]).then_inc(s("consts_loaded"), 16)
            for n, (kind, i) in enumerate(DENSE):
                if n == 2:
                    sp.dma_start(convio[:, 0:576], ins["convbuf"]).then_inc(s("convbuf_loaded"), 16)
                if (kind, i) == ("kc0", 0):
                    sp.wait_ge(s("ain_mm"), 36)
                    for x in range(4):
                        sl = slice(x * DCH, (x + 1) * DCH)
                        sp.dma_start(state[:, sl], ins["state"][x]).then_inc(s("state_loaded"), 16)
                if n >= DRAW:
                    old = n - DRAW
                    name, count = ("d_lo", TURN[old] + 1) if SPLIT[DENSE[old][0]] else read_by(old)
                    sp.wait_ge(s(name), count)
                sp.dma_start(draw[n % DRAW][:, 0:WIDTH[kind]], ins[kind][i]).then_inc(slot_loaded[n % DRAW], 16)
            def load(e, c, before):
                before()
                sp.dma_start(as_chunk(raw_of(c), c), expert_source(e, c)).then_inc(raw_loaded[c % XRAW], 16)

            def step(e, after, st):
                for c in range(XSET, PERX):
                    load(e, c, lambda: sp.wait_ge(s("w_lo"), st * PERX + (c - XRAW + 1)))
                for c in range(XSET):
                    load(after, c, lambda: sp.wait_ge(s("w_lo"), st * PERX + (PERX + c - XRAW + 1)))

            sp.wait_ge(s("wo_mm"), KD)
            for c in range(PERX + XSET):
                load(c // PERX, c % PERX, lambda: sp.wait_ge(s("w_lo"), c - XRAW + 1) if c >= XRAW else None)
            with sp.Fori(1, E - 1) as e:
                step(e, e + 1, e)
            step(E - 1, 0, E - 1)
            sp.wait_ge(s("steps_known"), 1)
            n_rounds = sp.value_load(nsteps_i[0:1, 0:1], min_val=1, max_val=ROUNDS)
            with sp.If(n_rounds > 1):
                with sp.Fori(1, n_rounds) as r:
                    with sp.Fori(0, E - 1) as e:
                        step(e, e + 1, r * E + e)
                    step(E - 1, 0, r * E + (E - 1))
            sp.wait_ge(s("kv_stored"), 64)
            sp.wait_ge(s("S_stored"), 16)
            sp.wait_ge(s("state_stored0"), 32)
            sp.wait_ge(s("state_stored1"), 32)
            sp.wait_ge(s("outputs_stored"), 48)

        @block.gpsimd
        def _(pool):
            pool.memset(ones[:, :], 1.0).then_inc(s("ones_set"), 1)
            pool.memset(epsc[:, :], EPS).then_inc(s("ones_set"), 1)

            def store(dst, src):
                pool.dma_start(dst, src).then_inc(s("outputs_stored"), 16)

            pool.wait_ge(s("mem_kv"), 16)
            for l in range(2):
                pool.dma_start(outs["mk"][l], mk[l]).then_inc(s("kv_stored"), 16)
                pool.dma_start(outs["mv"][l], mv[l]).then_inc(s("kv_stored"), 16)
            pool.wait_ge(s("conv_state"), 2)
            store(outs["conv"], convio)
            pool.wait_ge(s("S_done"), 2)
            pool.dma_start(outs["S"], Sb).then_inc(s("S_stored"), 16)
            for i in range(4):
                pool.wait_ge(s("state_new"), 4 * (i + 1))
                pool.dma_start(outs["state"][i], state[:, i * DCH:(i + 1) * DCH]).then_inc(s(f"state_stored{i // 2}"), 16)
            pool.wait_ge(s("norm_u"), 32)
            pool.dma_start(poolbuf, ins["poolbuf"]).then_inc(s("poolbuf_loaded"), 16)
            pool.wait_ge(s("pool_state"), 2)
            store(outs["pool"], pst)
            pool.wait_ge(s("norm_u"), 56)
            store(outs["y"], ubuf[:, :])

        @block.scalar
        def _(a):
            own = [0]

            def link(ins_):
                own[0] += 1
                ins_.then_inc(s("act_own"), 1)
                a.wait_ge(s("act_own"), own[0])

            def norm(i, src, n, ready, scale, eps_in=epsc, sqb=None, rtb=None):
                sqb = sq if sqb is None else sqb
                rtb = rt if rtb is None else rtb
                for k in range(KD):
                    ready(k)
                    a.activation(sqb[:, k * n:(k + 1) * n], src[:, k, :], ACT.Square).then_inc(s("norm_sq"), 1)
                a.wait_ge(s("norm_ss"), i + 1)
                a.activation(rtb[:, 0:n], bank(0)[:, 0:n], ACT.Sqrt, bias=epsc[:, 0:1], scale=scale)\
                    .then_inc(s("norm_rt"), 1)

            a.wait_ge(s("ones_set"), 2)
            a.wait_ge(s("x_loaded"), 32)
            def high(dst, src, n, tiles, ready):
                for k in tiles:
                    ready(k)
                    a.activation(dst[:, k * n:(k + 1) * n], src[:, k, :], ACT.Copy).then_inc(s("m_hi"), 1)

            def next_high(n):
                q = TURN[n] + DSET
                if q < len(HALVED) and RUN[HALVED[q]] == RUN[n]:
                    dense_high(a, HALVED[q])

            norm(0, memT, NM, lambda k: a.wait_ge(s("mem_loaded"), 16), 1.0 / D)
            dense_high(a, 0)
            dense_high(a, 1)
            a.wait_ge(s("norm_rs"), 1)
            norm(1, h, T, lambda k: a.wait_ge(s("x_loaded"), 32), 1.0 / D)
            for l in range(2):
                high(memh[l], memn[l], NM, range(KD), lambda k: a.wait_ge(s("norm_u"), KD * l + k + 1))

            for g in range(16):
                l, i = g // 8, g % 8
                a.wait_ge(s("mkv_mm"), g + 1)
                if i < 4:
                    a.activation(mk[l][:, i * NM:(i + 1) * NM], bank(i)[:, 0:NM], ACT.Copy).then_inc(s("mem_kv"), 1)
                else:
                    half, x = (i - 4) // 2, i % 2
                    a.activation(mv[l][:, x * 512 + half * 256:x * 512 + half * 256 + 256], bank(i)[:, 0:256], ACT.Copy)\
                        .then_inc(s("mem_kv"), 1)
                if g == 5:
                    high(uh[0], u, T, range(KD), lambda k: a.wait_ge(s("norm_u"), 2 * KD + k + 1))
                if i % 2:
                    next_high(g // 2)

            a.wait_ge(s("ba_mm"), 1)
            a.wait_ge(s("gba_zero"), 1)
            a.activation(gba[:, 0:2, :], bank(1)[:, 0:32].rearrange("p (t c) -> p t c", t=2), ACT.Copy).then_inc(s("gba_out"), 1)
            a.activation(gba[0:NS, 2, :], bank(1)[0:NS, 32:48], ACT.Copy).then_inc(s("gba_out"), 1)
            a.wait_ge(s("gba_out"), 2)
            a.activation(gb, gba[:, :, 0:8], ACT.Exp, scale=-1.0).then_inc(s("gate_exp"), 1)
            a.activation(gea, gains[:, GALOG:GALOG + H], ACT.Exp).then_inc(s("gate_exp"), 1)
            a.wait_ge(s("gate_ax"), 1)
            link(a.activation(ge, gax, ACT.Exp, scale=-1.0))
            a.activation(gl, ge, ACT.Ln, bias=ones[:, 0:1]).then_inc(s("gate_exp"), 1)

            a.wait_ge(s("convbuf_loaded"), 16)
            smp = pre[:, :, CW - 1 + SEQ:PRE].rearrange("p m (b j) -> p m b j", j=CW)
            for b in range(NS):
                cb = convio[:, 0:576].rearrange("p (m b j) -> p m b j", m=CT, b=NS)
                a.activation(smp[:, :, b, 0:CW - 1], cb[:, :, b, :], ACT.Copy).then_inc(s("conv_rows"), 1)

            def silu_of(m):
                a.wait_ge(s("conv_done"), m + 1)
                a.activation(act[:, m, :], act[:, m, :], ACT.Silu).then_inc(s("conv_silu"), 1)

            for t in range(36):
                a.wait_ge(s("ain_mm"), t + 1)
                if t % 2:
                    next_high(AT["a_in", t // 2])
                src = bank(t % 8)
                if t < CT:
                    a.activation(pre[:, t, CW - 1:CW - 1 + SEQ], src[:, 0:SEQ], ACT.Copy)
                    a.activation(smp[:, t, :, CW - 1], src[:, SEQ:T], ACT.Copy).then_inc(s("ain_out"), 1)
                elif t < 32:
                    a.activation(z[:, t - CT, :], src[:, 0:T], ACT.Silu).then_inc(s("ain_out"), 1)
                else:
                    a.activation(cq[:, t - 32, :], src[:, 0:T], ACT.Copy).then_inc(s("ain_out"), 1)
                if 8 <= t < 32:
                    silu_of(t - 8)

            a.wait_ge(s("conv_silu"), 16)
            for g in range(4):
                if g >= 1:
                    a.wait_ge(s("l2_mm"), g)
                a.activation(sqq, act[:, 4 * g:4 * g + 4, :].rearrange("p m c -> p (m c)"), ACT.Square).then_inc(s("l2_sq"), 1)
                a.wait_ge(s("l2_mm"), g + 1)
                if g >= 1:
                    a.wait_ge(s("l2_done"), g)
                for x in range(2):
                    a.activation(rsq[:, 2 * x * ACTW:2 * (x + 1) * ACTW].rearrange("p (m c) -> p m c", m=2),
                                 PP[x][:, :].rearrange("p (m c) -> p m c", m=2)[:, :, 0:ACTW],
                                 ACT.Sqrt, bias=epsc[:, 0:1]).then_inc(s("l2_rt"), 1)

            a.wait_ge(s("coef_dif"), 1)
            for dst, src in ((ceG, cG), (ctail, cdl), (ceGl, cgt[:, 0:16]), (sgb[:, 0:64], sgt[:, 0:64])):
                a.activation(dst, src, ACT.Exp).then_inc(s("coef_exp"), 1)

            def attention(l):
                for t in range(2):
                    a.wait_ge(s("att_max"), 3 * l + t + 1)
                    for x in range(XH):
                        a.activation(Pr[:, t * 1024 + x * NM:t * 1024 + (x + 1) * NM], PP[t][:, x * NM:(x + 1) * NM], ACT.Exp,
                                     bias=anm[:, t * 4 + x:t * 4 + x + 1], scale=P ** -0.5,
                                     accum_out=asum[:, t * 4 + x:t * 4 + x + 1]).then_inc(s("att_exp"), 1)
                v = PrT.rearrange("p (n t c) -> p n t c", t=2, c=P)
                for t in range(2):
                    a.wait_ge(s("att_tr"), 3 * l + t + 1)
                    a.activation(v[:, :, t, :], PP[2 + t][:, :].rearrange("p (n c) -> p n c", c=P), ACT.Copy).then_inc(s("att_pt"), 1)
                a.wait_ge(s("att_o"), 1 * l + 1)
                a.activation(cat[:, H:H + XH, 0:SEQ], PP[0][:, :].rearrange("p (m c) -> p m c", m=XH), ACT.Copy).then_inc(s("att_cat"), 1)
                a.wait_ge(s("cache_mm"), 8 * l + 4)
                a.activation(STs, bank(0)[:, 0:64], ACT.Copy).then_inc(s("sat_st"), 1)
                a.wait_ge(s("att_max"), 3 * l + 3)
                a.activation(P32[0:BH, :], bank(1)[0:BH, 0:NM], ACT.Exp, bias=anm[0:BH, 0:1], scale=P ** -0.5,
                             accum_out=asum[0:BH, 0:1]).then_inc(s("att_exp"), 1)
                a.wait_ge(s("att_tr"), 3 * l + 3)
                a.activation(PT32, bank(2)[:, 0:64], ACT.Copy).then_inc(s("sat_pt"), 1)
                a.wait_ge(s("cache_mm"), 8 * l + 8)
                a.activation(cat[:, H:H + XH, SEQ:T].rearrange("p x b -> p b x"),
                             bank(3)[:, 0:BH].rearrange("p (b x) -> p b x", x=XH), ACT.Copy).then_inc(s("att_cat"), 1)

            attention(0)

            for c in range(NCH):
                a.wait_ge(s("dl_neg"), c + 1)
                for x in range(H):
                    a.activation(DTb[:, x * P:(x + 1) * P], MLb[:, x * P:(x + 1) * P], ACT.Exp,
                                 bias=cnG[:, c * H + x:c * H + x + 1]).then_inc(s("dl_dt"), 1)
                a.activation(Xb, PP[0][:, :], ACT.Exp).then_inc(s("dl_eg"), 1)
                for lv in range(1, NLVL + 1):
                    if lv < NLVL:
                        for g in range(2):
                            a.wait_ge(s("dl_tt"), (c * (NLVL - 1) + lv - 1) * 2 + g + 1)
                            a.activation(Tb[:, g * 512:(g + 1) * 512], bank(g), ACT.Copy).then_inc(s("dl_t"), 1)
                        for g in range(2):
                            a.wait_ge(s("dl_xx"), (c * (NLVL - 1) + lv - 1) * 2 + g + 1)
                            a.activation(Xb[:, g * 512:(g + 1) * 512], bank(2 + g), ACT.Copy).then_inc(s("dl_x"), 1)
                a.wait_ge(s("dl_uu"), c + 1)
                a.activation(Tb, PP[1][:, :], ACT.Copy).then_inc(s("dl_u"), 1)
                a.wait_ge(s("dl_o"), c + 1)
                a.activation(cat[:, 0:H, c * P:(c + 1) * P], PP[2][:, :].rearrange("p (m c) -> p m c", m=H), ACT.Copy)\
                    .then_inc(s("dl_cat"), 1)

            a.wait_ge(s("sd_rows"), 1)
            a.activation(krow[0:DBH, :], bank(4)[0:DBH, 0:P], ACT.Copy).then_inc(s("sd_row"), 1)
            a.wait_ge(s("sd_rows"), 2)
            a.activation(urow[0:DBH, :], bank(5)[0:DBH, 0:P], ACT.Copy).then_inc(s("sd_row"), 1)

            a.wait_ge(s("dl_cat"), NCH)
            a.wait_ge(s("sd_cat"), 1)
            for x in range(H):
                a.activation(sq[:, x * T:(x + 1) * T], cat[:, x, :], ACT.Square).then_inc(s("on_sq"), 1)
            for x in range(H):
                a.wait_ge(s("on_mm"), x + 1)
                a.activation(sq[:, x * T:(x + 1) * T], bank(x)[:, 0:T], ACT.Sqrt, bias=epsc[:, 0:1], scale=1.0 / P)\
                    .then_inc(s("on_rt"), 1)
            a.wait_ge(s("att_cat"), 2)
            high(cath[0], cat, T, range(H, H + XH), lambda k: None)
            for i in range(DSET):
                a.wait_ge(s(f"state_stored{i}"), 32)
                dense_high(a, AT["a_out", i])
            high(cath[0], cat, T, range(H), lambda k: a.wait_ge(s("on_done"), k + 1))

            def residual_norm(i, name, last):
                for t in range(KD + 1):
                    if t < KD:
                        for n in last(t):
                            next_high(n)
                    if t:
                        a.wait_ge(s(f"{name}_h"), t)
                        a.activation(sq[:, (t - 1) * T:t * T], h[:, t - 1, :], ACT.Square).then_inc(s("norm_sq"), 1)
                a.wait_ge(s("norm_ss"), i + 1)
                a.activation(rt[:, 0:T], bank(0)[:, 0:T], ACT.Sqrt, bias=epsc[:, 0:1], scale=1.0 / D).then_inc(s("norm_rt"), 1)

            residual_norm(2, "aout", lambda t: [AT["a_out", t]])
            high(uh[1], u, T, range(KD), lambda k: a.wait_ge(s("norm_u"), 3 * KD + k + 1))
            for f in range(FT):
                a.wait_ge(s("wi_mm"), f + 1)
                if f >= 2:
                    a.wait_ge(s("wi_prod"), f - 1)
                a.activation(sil[f % 2], bank(2 * (f % 4))[:, 0:T], ACT.Silu).then_inc(s("wi_sil"), 1)
                next_high(AT["wi", f])
                a.wait_ge(s("wi_prod"), f + 1)
                a.activation(hidh[:, f * T:(f + 1) * T], hidf[f % 2], ACT.Copy).then_inc(s("hid_hi"), 1)
            residual_norm(3, "wo", lambda t: [AT["wo", 2 * t], AT["wo", 2 * t + 1]])
            high(uh[2], u, T, range(KD), lambda k: a.wait_ge(s("norm_u"), 4 * KD + k + 1))

            psm_in = pin[:, :, PW + SEQ:PCOL].rearrange("p m (b j) -> p m b j", j=PW + 1)
            a.wait_ge(s("norm_u"), 40)
            a.wait_ge(s("pin_zero"), 1)
            a.wait_ge(s("poolbuf_loaded"), 16)
            a.wait_ge(s("pin_zero"), 2)
            for t in range(12):
                a.wait_ge(s("bin_mm"), t + 1)
                if t % 2:
                    next_high(AT["b_in", t // 2])
                if t < 8:
                    a.activation(pin[:, t, PW:PW + SEQ], bank(t % 8)[:, 0:SEQ], ACT.Copy)
                    a.activation(psm_in[:, t, :, PW], bank(t % 8)[:, SEQ:T], ACT.Copy).then_inc(s("bin_out"), 1)
                else:
                    a.activation(cq[:, t - 8, :], bank(t % 8)[:, 0:T], ACT.Copy).then_inc(s("bin_out"), 1)
            for t in range(8):
                a.wait_ge(s("pm_mm"), t + 1)
                if t == 0:
                    a.wait_ge(s("pm_mm"), 8)
                a.activation(cat[:, t, :], bank(t)[:, 0:T], ACT.Copy, scale=gains[:, GPS + t:GPS + t + 1])\
                    .then_inc(s("pm_cat"), 1)
            attention(1)
            a.wait_ge(s("pm_cat"), 8)
            a.wait_ge(s("att_cat"), 4)
            a.wait_ge(s("outputs_stored"), 32)
            high(cath[1], cat, T, range(12), lambda k: None)
            for i in range(DSET):
                dense_high(a, AT["b_out", i])
            for t in range(KD - DSET):
                next_high(AT["b_out", t])
            norm(4, h, T, lambda k: a.wait_ge(s("bout_h"), k + 1), 1.0 / D, sqb=fsq, rtb=frt)

            a.wait_ge(s("outputs_stored"), 32)
            for t in range(3):
                n = P if t < 2 else NS
                a.wait_ge(s("xt_mm"), t + 1)
                a.activation(xtok[0:n, t, :], PP[1 + t][0:n, :], ACT.Copy).then_inc(s("xt_out"), 1)
            a.wait_ge(s("rt_mm"), 1)
            a.wait_ge(s("rout_zero"), 1)
            a.activation(rout[:, 0:16], bank(0)[:, 0:16], ACT.Copy).then_inc(s("rt_out"), 1)
            a.activation(rout[0:NS, 16:24], bank(0)[0:NS, 16:24], ACT.Copy).then_inc(s("rt_out"), 1)
            a.wait_ge(s("rt_sub"), 1)
            a.activation(rr[1], rr[1], ACT.Exp).then_inc(s("rt_exp"), 1)
            def halve(c, st, again=0):
                a.wait_ge(raw_loaded[c % XRAW], st * (16 * PERX // XRAW) + (16 * (PERX // XRAW * again + c // XRAW + 1)))
                q = c + PERX * again - XSET
                if q >= 0:
                    name, n = ("up_mm", NUP) if q < NUP else ("down_mm", NDOWN)
                    a.wait_ge(s(name), st * n + ((q if q < NUP else q - NUP) + 1))
                a.activation(whi[c % XSET][:, :], raw_of(c), ACT.Copy).then_inc(s("w_hi"), 1)

            def slots():
                a.activation(xsh[:, :], PP[1][:, :], ACT.Copy).then_inc(s("xs_hi"), 1)

            a.wait_ge(s("gat_mm"), 1)
            slots()
            a.wait_ge(s("bout_mm"), KD)
            for c in range(XSET):
                halve(c, 0)

            a.wait_ge(s("steps_known"), 1)
            n_rounds = a.value_load(nsteps_i[0:1, 0:1], min_val=1, max_val=ROUNDS)
            with a.Fori(0, n_rounds * E) as st:
                for c in range(XSET, PERX):
                    halve(c, st)
                    if c % 4 == 0 and c // 4 - 1 < FCN:
                        f = c // 4 - 1
                        a.wait_ge(s("up_mm"), st * NUP + (4 * f + 2))
                        if f >= 2:
                            a.wait_ge(s("up_h"), st * FCN + (f - 1))
                        a.activation(esil[f % 2], bank(2 * (f % 2))[:, :], ACT.Silu).then_inc(s("up_sil"), 1)
                    if c in TURNED:
                        f = TURNED[c]
                        a.wait_ge(s("ht_mm"), st * FCN + (f + 1))
                        a.activation(hTh[:, 4 * f * C:4 * (f + 1) * C], bank(4 + f % 2), ACT.Copy).then_inc(s("ht_hi"), 1)
                    if c == NUP + 3:
                        a.wait_ge(s("gat_mm"), st + 2)
                        slots()
                halve(0, st, 1)
                halve(1, st, 1)
                a.wait_ge(s("down_mm"), st * NDOWN + NDOWN)
                a.activation(yslot, PP[3][:, :], ACT.Copy).then_inc(s("y_out"), 1)
                halve(2, st, 1)

            a.wait_ge(s("comb_h"), n_rounds * E * KD + KD)
            norm(5, h, T, lambda k: None, 1.0 / D, sqb=fsq, rtb=frt)

        @block.vector
        def _(v):
            own = [0]

            def link(ins_):
                own[0] += 1
                ins_.then_inc(s("dve_own"), 1)
                v.wait_ge(s("dve_own"), own[0])

            m_lo = [0]

            def low(dst, high_, src, n, k):
                m_lo[0] += 1
                v.wait_ge(s("m_hi"), m_lo[0])
                v.tensor_tensor(dst[:, k * n:(k + 1) * n], src[:, k, :], high_[:, k * n:(k + 1) * n].bitcast(F32), ALU.subtract)\
                    .then_inc(s("m_lo"), 1)

            def next_low(n):
                q = TURN[n] + DSET
                if q < len(HALVED) and RUN[HALVED[q]] == RUN[n]:
                    dense_low(v, HALVED[q])

            def norm(i, src, n, dsts, rtb=None, rsb=None, halves_=None):
                rtb = rt if rtb is None else rtb
                rsb = rs if rsb is None else rsb
                v.wait_ge(s("norm_rt"), i + 1)
                if i:
                    v.wait_ge(s("norm_u"), (i + 1) * KD)
                v.reciprocal(rsb[:, 0:n], rtb[:, 0:n]).then_inc(s("norm_rs"), 1)
                v.wait_ge(s("norm_rs"), i + 1)
                for dst, g in dsts:
                    for k in range(KD + 2):
                        if k < KD:
                            v.scalar_tensor_tensor(out=dst[:, k, :], in0=src[:, k, :], scalar=gains[:, g + k:g + k + 1],
                                                   in1=rsb[:, 0:n], op0=ALU.mult, op1=ALU.mult).then_inc(s("norm_u"), 1)
                        if k >= 2 and halves_:
                            low(halves_[1], halves_[0], dst, n, k - 2)

            v.memset(gba, 0.0).then_inc(s("gba_zero"), 1)
            v.wait_ge(s("x_loaded"), 32)
            v.wait_ge(s("consts_loaded"), 48)
            norm(0, memT, NM, [(memn[0], GM0), (memn[1], GM1)])
            norm(1, h, T, [(u, GA1)])
            dense_low(v, 0)
            for k in range(KD):
                low(meml[0], memh[0], memn[0], NM, k)
            dense_low(v, 1)
            for k in range(KD):
                low(meml[1], memh[1], memn[1], NM, k)
            for i in range(8):
                if i == 3:
                    for k in range(KD):
                        low(ul[0], uh[0], u, T, k)
                next_low(i)

            v.wait_ge(s("gba_out"), 2)
            dt_b = gains[:, GDT:GDT + H].unsqueeze(1).to_broadcast([P, 3, H])
            link(v.tensor_tensor(gx, gba[:, :, 8:16], dt_b, ALU.add))
            v.scalar_tensor_tensor(out=gax, in0=gx, scalar=-1.0, in1=gx, op0=ALU.mult, op1=ALU.max).then_inc(s("gate_ax"), 1)
            v.wait_ge(s("gate_exp"), 1)
            link(v.tensor_scalar(gb, gb, 1.0, None, ALU.add))
            link(v.reciprocal(gb, gb))
            v.wait_ge(s("gate_exp"), 3)
            link(v.scalar_tensor_tensor(out=gl, in0=gx, scalar=0.0, in1=gl, op0=ALU.max, op1=ALU.add))
            v.wait_ge(s("gate_exp"), 2)
            link(v.scalar_tensor_tensor(out=gg, in0=gl, scalar=-1.0, in1=gea.unsqueeze(1).to_broadcast([P, 3, H]),
                                        op0=ALU.mult, op1=ALU.mult))
            dg8 = ident[0:NS, 0:NS].unsqueeze(2).to_broadcast([NS, NS, H])
            for i, val in enumerate((gg, gb)):
                v.tensor_tensor(gd[0:NS, 64 * i:64 * i + 64].rearrange("p (b x) -> p b x", x=H),
                                val[0:NS, 2, :].unsqueeze(1).to_broadcast([NS, NS, H]), dg8, ALU.mult)\
                    .then_inc(s("gate_done"), 1)

            v.wait_ge(s("mkv_mm"), 16)
            v.memset(pre[:, :, 0:CW - 1], 0.0).then_inc(s("pre_zero"), 1)
            v.wait_ge(s("conv_rows"), NS)
            v.wait_ge(s("pre_zero"), 1)
            for c in range(18):
                next_low(AT["a_in", c])
                g = c - 1
                if not 0 <= g < CT // 2:
                    continue
                v.wait_ge(s("ain_out"), 2 * g + 2)
                for j in range(CW):
                    for m in range(2 * g, 2 * g + 2):
                        tap = gains[:, GTAP + m * CW + j:GTAP + m * CW + j + 1]
                        if j:
                            v.wait_ge(s("conv_tap"), 6 * g + 2 * (j - 1) + m - 2 * g + 1)
                        ins_ = v.tensor_scalar(act[:, m, :], pre[:, m, 0:ACTW], tap, None, ALU.mult) if j == 0 else \
                            v.scalar_tensor_tensor(out=act[:, m, :], in0=pre[:, m, j:j + ACTW], scalar=tap,
                                                   in1=act[:, m, :], op0=ALU.mult, op1=ALU.add)
                        ins_.then_inc(s("conv_tap") if j < CW - 1 else s("conv_done"), 1)
            cio = convio.rearrange("p (m c) -> p m c", m=CT)
            smp = pre[:, :, CW - 1 + SEQ:PRE].rearrange("p m (b j) -> p m b j", j=CW)
            v.tensor_copy(cio[:, :, 0:3], pre[:, :, SEQ:SEQ + 3]).then_inc(s("conv_state"), 1)
            for b in range(NS):
                ins_ = v.tensor_copy(cio[:, :, 3 + 3 * b:6 + 3 * b], smp[:, :, b, 1:CW])
            ins_.then_inc(s("conv_state"), 1)

            for g in range(4):
                v.wait_ge(s("l2_rt"), 2 * g + 2)
                link(v.reciprocal(rsq, rsq))
                sl = act[:, 4 * g:4 * g + 4, :].rearrange("p m c -> p (m c)")
                v.scalar_tensor_tensor(out=sl, in0=sl, scalar=P ** -0.5 if g < 2 else 1.0, in1=rsq,
                                       op0=ALU.mult, op1=ALU.mult).then_inc(s("l2_done"), 1)

            v.wait_ge(s("coef_mm"), 1)
            link(v.tensor_copy(cG, bank(0)[:, 0:16]))
            v.tensor_copy(cgt[:, 0:16], bank(0)[:, 16:32])
            link(v.tensor_copy(sgt, bank(0)[:, 32:160]))
            v.tensor_scalar(cnG, cG, -1.0, None, ALU.mult)
            v.tensor_copy(sgb[:, 64:128], sgt[:, 64:128])
            link(v.tensor_tensor(cdl, cgt[:, 0:16], cG, ALU.subtract))
            v.tensor_copy(cgt[:, 16:32], cG).then_inc(s("coef_dif"), 1)
            v.wait_ge(s("coef_exp"), 4)
            gbp = gb[:, 0:2, :].rearrange("p t c -> p (t c)")
            v.tensor_tensor(cbeG, ceG, gbp, ALU.mult).then_inc(s("coef_beg"), 1)

            def attention(l):
                for t in range(2):
                    v.wait_ge(s("att_mm"), 2 * l + t + 1)
                    link(v.reduce_max(amx[:, 4 * t:4 * t + 4], PP[t][:, :].rearrange("p (m c) -> p m c", m=XH), AX))
                    v.tensor_scalar(anm[:, 4 * t:4 * t + 4], amx[:, 4 * t:4 * t + 4], -(P ** -0.5), None, ALU.mult)\
                        .then_inc(s("att_max"), 1)
                for t in range(2):
                    v.wait_ge(s("att_exp"), 9 * l + 4 * t + 4)
                    link(v.reciprocal(ars[:, 4 * t:4 * t + 4], asum[:, 4 * t:4 * t + 4]))
                    pt = Pr[:, 1024 * t:1024 * (t + 1)].rearrange("p (m c) -> p m c", m=XH)
                    v.tensor_tensor(pt, pt, ars[:, 4 * t:4 * t + 4].unsqueeze(2).to_broadcast([P, XH, NM]), ALU.mult)\
                        .then_inc(s("att_p"), 1)
                v.wait_ge(s("sat_s"), 1 * l + 1)
                link(v.reduce_max(amx[0:BH, 0:1], bank(1)[0:BH, 0:NM], AX))
                v.tensor_scalar(anm[0:BH, 0:1], amx[0:BH, 0:1], -(P ** -0.5), None, ALU.mult).then_inc(s("att_max"), 1)
                v.wait_ge(s("att_exp"), 9 * l + 9)
                link(v.reciprocal(ars[0:BH, 0:1], asum[0:BH, 0:1]))
                v.tensor_scalar(P32[0:BH, :], P32[0:BH, :], ars[0:BH, 0:1], None, ALU.mult).then_inc(s("att_p"), 1)

            attention(0)

            def per_head(c, coef):
                return coef[:, c * H:(c + 1) * H].unsqueeze(2).to_broadcast([P, H, P])

            def heads(b):
                return b.rearrange("p (m c) -> p m c", m=H)

            for c in range(NCH):
                cols = slice(c * P, (c + 1) * P)
                v.wait_ge(s("conv_state"), 2)
                v.wait_ge(s("dl_grow"), c + 1)
                v.tensor_tensor(heads(MLb), heads(PP[0][:, :]), neg.unsqueeze(1).to_broadcast([P, H, P]), ALU.add)\
                    .then_inc(s("dl_neg"), 1)
                v.wait_ge(s("dl_dt"), H * (c + 1))
                v.wait_ge(s("dl_kk"), 2 * c + 1)
                v.tensor_tensor(PTb, PP[1][:, :], DTb, ALU.mult).then_inc(s("dl_pt"), 1)
                v.wait_ge(s("dl_kk"), 2 * c + 2)
                link(v.tensor_tensor(MTb, PP[2][:, :], DTb, ALU.mult))
                v.wait_ge(s("dl_brow"), c + 1)
                link(v.tensor_tensor(MTb, MTb, PP[3][:, :], ALU.mult))
                v.wait_ge(s("dl_eg"), c + 1)
                v.tensor_tensor(act[:, 0:H, cols], act[:, 0:H, cols], heads(Xb), ALU.mult).then_inc(s("dl_qd"), 1)
                v.wait_ge(s("dl_tok"), 2 * c + 1)
                v.tensor_tensor(heads(vtok), heads(PP[1][:, :]), per_head(c, gbp), ALU.mult).then_inc(s("dl_v"), 1)
                v.wait_ge(s("dl_tok"), 2 * c + 2)
                v.tensor_tensor(heads(ktail), heads(PP[2][:, :]), per_head(c, ctail), ALU.mult).then_inc(s("dl_kt"), 1)

                for lv in range(NLVL):
                    mask = consts[:, CLVL + lv * P:CLVL + (lv + 1) * P].unsqueeze(1).to_broadcast([P, H, P])
                    if lv >= 2:
                        v.wait_ge(s("dl_xx"), (c * (NLVL - 1) + lv - 1) * 2)
                    if lv:
                        v.wait_ge(s("dl_um"), 2 * (c * NLVL + lv))
                    v.tensor_tensor(heads(MLb), heads(MTb), mask, ALU.mult).then_inc(s("dl_ml"), 1)
                    if lv == 0:
                        v.wait_ge(s("dl_ml"), c * NLVL + 1)
                        for g in range(2):
                            v.tensor_tensor(heads(Ub)[:, 4 * g:4 * g + 4, :], ident.unsqueeze(1).to_broadcast([P, 4, P]),
                                            heads(MLb)[:, 4 * g:4 * g + 4, :], ALU.subtract).then_inc(s("dl_um"), 1)
                        continue
                    for g in range(2):
                        v.wait_ge(s("dl_du"), (c * (NLVL - 1) + lv - 1) * 2 + g + 1)
                        v.tensor_tensor(Ub[:, g * 512:(g + 1) * 512], Ub[:, g * 512:(g + 1) * 512], bank(4 + g), ALU.subtract)\
                            .then_inc(s("dl_um"), 1)
                if c:
                    v.wait_ge(s("dl_ks"), 1)
                    link(v.tensor_tensor(heads(Xb), heads(PP[0][:, :]), per_head(c, cbeG), ALU.mult))
                    v.tensor_tensor(Xb, vtok, Xb, ALU.subtract).then_inc(s("dl_r"), 1)
                v.wait_ge(s("dl_ds"), c + 1)
                if c == 0:
                    v.tensor_copy(Sb, PP[3][:, :]).then_inc(s("S_done"), 1)
                else:
                    v.wait_ge(s("S_done"), 1)
                    v.wait_ge(s("dl_o"), c + 1)
                    link(v.tensor_tensor(heads(Sb), heads(Sb), per_head(c, ceGl), ALU.mult))
                    v.tensor_tensor(Sb, Sb, PP[3][:, :], ALU.add).then_inc(s("S_done"), 1)

            def cols64(m0):
                return act[:, m0:m0 + H, S0:S0 + CW * (NS - 1) + 1:CW].rearrange("p x b -> p b x")

            def as_bx(b):
                return b.rearrange("p (b x) -> p b x", x=H)

            v.wait_ge(s("dl_ds"), NCH)
            v.tensor_copy(kq[:, :, 0].rearrange("p (b x) -> p b x", x=H), cols64(8))
            v.tensor_copy(kq[:, :, 1].rearrange("p (b x) -> p b x", x=H), cols64(0))
            link(v.tensor_copy(as_bx(v64), cols64(16)))
            link(v.tensor_copy(t64, kq[:, :, 0]))
            v.tensor_tensor(kqd, t64, kq[:, :, 1], ALU.mult).then_inc(s("sd_cols"), 1)
            v.wait_ge(s("sd_mm"), 1)
            rk = bank(0)[:, 0:128].rearrange("p (n c) -> p n c", c=2)
            egs, bs = sgb[:, 0:64], sgb[:, 64:128]
            v.wait_ge(s("sd_rows"), 1)
            link(v.tensor_tensor(t64, rk[:, :, 0], egs, ALU.mult))
            link(v.tensor_tensor(u64, v64, t64, ALU.subtract))
            link(v.tensor_tensor(u64, u64, bs, ALU.mult))
            v.tensor_tensor(qku, rk[:, :, 1], egs, ALU.mult).then_inc(s("sd_u"), 1)
            v.wait_ge(s("sd_u"), 1)
            link(v.tensor_tensor(t64, bank(1)[:, 0:64], u64, ALU.mult))
            v.tensor_tensor(cat[:, 0:H, SEQ:T].rearrange("p x b -> p b x"), as_bx(t64), as_bx(qku), ALU.add)\
                .then_inc(s("sd_cat"), 1)
            v.wait_ge(s("sd_row"), 2)
            for g in range(16):
                if g >= 2:
                    v.wait_ge(s("sd_outer"), g - 1)
                v.tensor_tensor(ublk[g % 2][0:DBH, :].rearrange("p (n c) -> p n c", c=P),
                                urow[0:DBH, :].unsqueeze(1).to_broadcast([DBH, 4, P]),
                                ident[0:DBH, 4 * g:4 * g + 4].unsqueeze(2).to_broadcast([DBH, 4, P]), ALU.mult)\
                    .then_inc(s("sd_blk"), 1)
                if g >= 1:
                    new_state(v, g - 1)
            new_state(v, 15)

            for x in range(H):
                v.wait_ge(s("on_rt"), x + 1)
                sl = sq[:, x * T:(x + 1) * T]
                link(v.reciprocal(sl, sl))
                link(v.scalar_tensor_tensor(out=sl, in0=sl, scalar=gains[:, GON:GON + 1], in1=z[:, x, :],
                                            op0=ALU.mult, op1=ALU.mult))
                v.tensor_tensor(cat[:, x, :], cat[:, x, :], sl, ALU.mult).then_inc(s("on_done"), 1)
            v.wait_ge(s("S_stored"), 16)
            for k in range(H, H + XH):
                low(catl[0], cath[0], cat, T, k)
            for i in range(DSET):
                dense_low(v, AT["a_out", i])
            for k in range(H):
                low(catl[0], cath[0], cat, T, k)

            def residual(name, chunks):
                for t in range(KD):
                    v.wait_ge(s(f"{name}_mm"), chunks * (t + 1))
                    v.tensor_tensor(h[:, t, :], h[:, t, :], bank(t)[:, 0:T], ALU.add).then_inc(s(f"{name}_h"), 1)
                    for i in range(chunks):
                        next_low(AT[CHUNKS[name], chunks * t + i])

            residual("aout", 1)
            norm(2, h, T, [(u, GA2)], halves_=(uh[1], ul[1]))
            for f in range(FT):
                v.wait_ge(s("wi_sil"), f + 1)
                if f >= 2:
                    v.wait_ge(s("hid_hi"), f - 1)
                    v.wait_ge(s("hid_lo"), f - 1)
                v.tensor_tensor(hidf[f % 2], sil[f % 2], bank(2 * (f % 4) + 1)[:, 0:T], ALU.mult).then_inc(s("wi_prod"), 1)
                next_low(AT["wi", f])
                v.wait_ge(s("hid_hi"), f + 1)
                sl = slice(f * T, (f + 1) * T)
                v.tensor_tensor(hidl[:, sl], hidf[f % 2], hidh[:, sl].bitcast(F32), ALU.subtract).then_inc(s("hid_lo"), 1)
            residual("wo", 2)
            norm(3, h, T, [(u, GB1)], halves_=(uh[2], ul[2]))

            v.wait_ge(s("norm_u"), 40)
            v.memset(pin[:, :, 0:PW], 0.0).then_inc(s("pin_zero"), 1)
            v.wait_ge(s("poolbuf_loaded"), 16)
            psv = pin[:, :, PW + SEQ:PCOL].rearrange("p m (b j) -> p m b j", j=PW + 1)
            pbv = poolbuf.rearrange("p (m b j) -> p m b j", m=KD, b=NS)
            for b in range(NS):
                ins_ = v.tensor_copy(psv[:, :, b, 0:PW], pbv[:, :, b, :])
            ins_.then_inc(s("pin_zero"), 1)
            for i in range(6):
                next_low(AT["b_in", i])
            v.wait_ge(s("bin_out"), 8)
            v.wait_ge(s("pin_zero"), 2)
            v.wait_ge(s("bin_mm"), 12)
            v.wait_ge(s("kv_stored"), 64)
            pstv = pst.rearrange("p (m c) -> p m c", m=KD)
            v.tensor_copy(pstv[:, :, 0:PW], pin[:, :, SEQ:SEQ + PW]).then_inc(s("pool_state"), 1)
            for b in range(NS):
                ins_ = v.tensor_copy(pstv[:, :, PW + PW * b:PW + PW * (b + 1)], psv[:, :, b, 1:PW + 1])
            ins_.then_inc(s("pool_state"), 1)
            src = pin
            for g in range(4):
                w = 2 << g
                m0 = 2 * g
                sh = w // 2
                if g % 2 == 0:
                    dst, frm = psm, pin
                else:
                    dst, frm = pin, psm
                if g == 0:
                    link(v.tensor_copy(u[:, :, 0:SEQ], pin[:, :, PW:PW + SEQ]))
                    link(v.tensor_copy(u[:, :, SEQ:T], psv[:, :, :, PW]))
                lo = 2 * sh - 1
                link(v.tensor_tensor(dst[:, m0:, lo:], frm[:, m0:, lo:], frm[:, m0:, lo - sh:PCOL - sh], ALU.add))
                v.scalar_tensor_tensor(out=pd[:, m0:m0 + 2, 0:SEQ], in0=dst[:, m0:m0 + 2, PW:PW + SEQ], scalar=1.0 / w,
                                       in1=u[:, m0:m0 + 2, 0:SEQ], op0=ALU.mult, op1=ALU.subtract)
                dsv = dst[:, :, PW + SEQ:PCOL].rearrange("p m (b j) -> p m b j", j=PW + 1)
                link(v.scalar_tensor_tensor(out=pd[:, m0:m0 + 2, SEQ:T], in0=dsv[:, m0:m0 + 2, :, PW], scalar=1.0 / w,
                                            in1=u[:, m0:m0 + 2, SEQ:T], op0=ALU.mult, op1=ALU.subtract))
                inv = consts[:, CINV + 16 * g:CINV + 16 * g + 16].unsqueeze(1).to_broadcast([P, 2, 16])
                fx = pfix[:, 0:32].rearrange("p (m c) -> p m c", m=2)
                link(v.tensor_tensor(fx, dst[:, m0:m0 + 2, PW:PW + 16], inv, ALU.mult))
                ins_ = v.tensor_tensor(pd[:, m0:m0 + 2, 0:16], fx, u[:, m0:m0 + 2, 0:16], ALU.subtract)
                link(ins_) if g < 3 else ins_.then_inc(s("pool_d"), 1)

            attention(1)
            for k in range(12):
                low(catl[1], cath[1], cat, T, k)
            for i in range(DSET):
                dense_low(v, AT["b_out", i])
            residual("bout", 1)
            norm(4, h, T, [(u, GB2)], rtb=frt, rsb=frs)

            v.memset(rout, 0.0).then_inc(s("rout_zero"), 1)
            v.wait_ge(s("rt_out"), 2)
            lg = rout.rearrange("p (t e) -> p t e", t=3)
            rank, sel, gat, mx, pos = rr[0], rr[2], rr[3], rr[4], rr[5]
            for t in range(3):
                mine = lg[:, t, :].unsqueeze(2).to_broadcast([P, E, E])
                other = lg[:, t, :].unsqueeze(1).to_broadcast([P, E, E])
                o1 = rtmp[:, 64 * t:64 * t + 64].rearrange("p (a b) -> p a b", a=E)
                o2 = rtm2[:, 64 * t:64 * t + 64].rearrange("p (a b) -> p a b", a=E)
                tie = consts[:, CTIE:CTIE + 64].rearrange("p (a b) -> p a b", a=E)
                v.tensor_tensor(o1, other, mine, ALU.is_gt)
                link(v.tensor_tensor(o2, other, mine, ALU.is_equal))
                link(v.tensor_tensor(o2, o2, tie, ALU.mult))
                link(v.tensor_tensor(o1, o1, o2, ALU.add))
                v.reduce_sum(rank[:, 8 * t:8 * t + 8], o1, AX)
                link(v.reduce_max(mx[:, t:t + 1], lg[:, t, :], AX))
                v.tensor_scalar(rr[1][:, 8 * t:8 * t + 8], lg[:, t, :], mx[:, t:t + 1], None, ALU.subtract)\
                    .then_inc(s("rt_d"), 1)
            v.wait_ge(s("rt_d"), 3)
            v.tensor_scalar(sel, rank, 1.5, None, ALU.is_lt).then_inc(s("rt_sub"), 1)
            v.wait_ge(s("rt_exp"), 1)
            link(v.tensor_tensor(gat, rr[1], sel, ALU.mult))
            link(v.reduce_sum(mx[:, 0:3], gat.rearrange("p (t e) -> p t e", t=3), AX))
            link(v.reciprocal(mx[:, 0:3], mx[:, 0:3]))
            link(v.tensor_tensor(gat.rearrange("p (t e) -> p t e", t=3), gat.rearrange("p (t e) -> p t e", t=3),
                                 mx[:, 0:3].unsqueeze(2).to_broadcast([P, 3, E]), ALU.mult))
            v.wait_ge(s("pos_mm"), 1)
            link(v.tensor_copy(pos, bank(0)[:, 0:24]))
            link(v.tensor_copy(cnt8[:, 0:8], bank(0)[:, 24:32]))
            link(v.tensor_scalar(rr[6], sel, 1e4, -1e4, ALU.mult, ALU.add))
            link(v.tensor_tensor(pos, pos, rr[6], ALU.add))
            for r in range(ROUNDS + 1):
                v.tensor_scalar(posx[:, r * E:(r + 1) * E, :].rearrange("p e t -> p t e"),
                                pos.rearrange("p (t e) -> p t e", t=3), -float(r * C), None, ALU.add)
                link(v.tensor_copy(gatex[:, r * E:(r + 1) * E, :].rearrange("p e t -> p t e"),
                                   gat.rearrange("p (t e) -> p t e", t=3)))
            link(v.reduce_max(cnt8[:, 8:9], cnt8[:, 0:8], AX))
            link(v.memset(cnt8[:, 9:10], 1.0))
            for r in range(1, ROUNDS):
                link(v.scalar_tensor_tensor(out=cnt8[:, 9:10], in0=cnt8[:, 8:9], scalar=float(r * C), in1=cnt8[:, 9:10],
                                            op0=ALU.is_gt, op1=ALU.add))
            v.tensor_copy(nsteps_i[:, :], cnt8[:, 9:10]).then_inc(s("steps_known"), 1)

            def dispatch(dst, at):
                for t in range(3):
                    n = P if t < 2 else NS
                    v.tensor_scalar(dst[0:n, t, :], iota[0:n, :], posx[0:n, at, t:t + 1] if isinstance(at, int) else
                                    posx[0:n, bass.ds(at, 1), t:t + 1].rearrange("p a b -> p (a b)"), None, ALU.is_equal)\
                        .then_inc(s("disp"), 1)

            def halve(c, want):
                v.wait_ge(s("w_hi"), want)
                v.tensor_tensor(wlo[c % XSET][:, :], raw_of(c), whi[c % XSET][:, :].bitcast(F32), ALU.subtract)\
                    .then_inc(s("w_lo"), 1)

            def slots(want):
                v.wait_ge(s("xs_hi"), want)
                v.tensor_tensor(xsl[:, :], PP[1][:, :], xsh[:, :].bitcast(F32), ALU.subtract).then_inc(s("xs_lo"), 1)

            v.wait_ge(s("steps_known"), 1)
            dispatch(disp, 0)
            v.memset(comb, 0.0).then_inc(s("comb_out"), 1)
            v.memset(yslot, 0.0).then_inc(s("y_out"), 1)
            slots(1)
            for c in range(XSET):
                halve(c, c + 1)
            n_rounds = v.value_load(nsteps_i[0:1, 0:1], min_val=1, max_val=ROUNDS)

            def add_back(before):
                for t in range(KD):
                    v.wait_ge(s("cmb_mm"), before + (t + 1))
                    v.tensor_tensor(h[:, t, :], h[:, t, :], bank(2 + t % 4)[:, 0:T], ALU.add).then_inc(s("comb_h"), 1)

            with v.Fori(0, n_rounds * E) as st:
                v.wait_ge(s("disp"), st * 3 + 3)
                for t in range(3):
                    n = P if t < 2 else NS
                    v.tensor_scalar(dispg[0:n, t, :], disp[0:n, t, :],
                                    gatex[0:n, bass.ds(st, 1), t:t + 1].rearrange("p a b -> p (a b)"), None, ALU.mult)\
                        .then_inc(s("dispg"), 1)
                v.wait_ge(s("gat_mm"), st + 1)
                v.wait_ge(s("dispg"), st * 3 + 3)
                dispatch(disp, st + 1)
                for c in range(XSET, PERX):
                    halve(c, st * PERX + (c + 1))
                    if c == XSET:
                        add_back(st * KD)
                    if c % 4 == 2 and 0 <= c // 4 - 1 < FCN:
                        f = c // 4 - 1
                        v.wait_ge(s("up_sil"), st * FCN + (f + 1))
                        v.wait_ge(s("up_mm"), st * NUP + (4 * f + 4))
                        if f >= 2:
                            v.wait_ge(s("ht_mm"), st * FCN + (f - 1))
                        v.tensor_tensor(hslot[f % 2], esil[f % 2], bank(2 * (f % 2) + 1)[:, :], ALU.mult)\
                            .then_inc(s("up_h"), 1)
                    if c in TURNED:
                        f = TURNED[c]
                        v.wait_ge(s("ht_hi"), st * FCN + (f + 1))
                        sl = slice(4 * f * C, 4 * (f + 1) * C)
                        v.tensor_tensor(hTl[:, sl], bank(4 + f % 2), hTh[:, sl].bitcast(F32), ALU.subtract)\
                            .then_inc(s("ht_lo"), 1)
                    if c == NUP + 3:
                        slots(st + 2)
                    if c == NUP + 7:
                        v.wait_ge(s("cmb_tr"), st + 1)
                        v.tensor_copy(comb, bank(5)[:, 0:T]).then_inc(s("comb_out"), 1)
                for c in range(XSET):
                    halve(c, st * PERX + (PERX + c + 1))
            add_back(n_rounds * E * KD)
            norm(5, h, T, [(u, GFIN)], rtb=frt, rsb=frs)

        @block.tensor
        def _(t_):
            pe = t_

            def norm(i, n, sqb=None):
                sqb = sq if sqb is None else sqb
                pe.wait_ge(s("ones_set"), 1)
                for k in range(KD):
                    pe.wait_ge(s("norm_sq"), KD * i + k + 1)
                    mm = pe.matmul(bank(0)[:, 0:n], ones[:, :], sqb[:, k * n:(k + 1) * n], start=(k == 0), stop=(k == KD - 1))
                mm.then_inc(s("norm_ss"), 1)

            def split_product(out, lhs, rhs, first, last):
                for i, (l, r) in enumerate(((0, 0), (0, 1), (1, 0))):
                    mm = pe.matmul(out, lhs[l], rhs[r], start=first and i == 0, stop=last and i == 2)
                return mm

            def weights(n, nk):
                pe.wait_ge(s("d_lo"), TURN[n] + 1)
                return [x.rearrange("p (k c) -> p k c", k=nk) for x in halves(n)]

            def tile(out, w, col, moving, n, ks, first=True, last=True, ready=None):
                for i, (kw, km) in enumerate(ks):
                    if ready is not None:
                        pe.wait_ge(s("m_lo"), ready(i))
                    mm = split_product(out, [x[:, kw, col:col + P] for x in w],
                                       [x[:, km * n:(km + 1) * n] for x in moving],
                                       first and i == 0, last and i == len(ks) - 1)
                return mm

            norm(0, NM)
            norm(1, T)
            pe.wait_ge(s("norm_rt"), 2)
            square = [(k, k) for k in range(KD)]
            for g in range(16):
                l, i = g // 8, g % 8
                w = weights(g // 2, KD)
                if g >= 8:
                    pe.wait_ge(s("mem_kv"), g - 7)
                if i == 0:
                    pe.wait_ge(s("m_lo"), KD * (l + 1))
                if i < 4:
                    mm = tile(bank(i)[:, 0:NM], w, (i % 2) * P, (memh[l], meml[l]), NM, square)
                else:
                    x = i % 2
                    for k in range(KD):
                        mm = split_product(bank(i)[:, 0:256], [y[:, k * NM + x * P:k * NM + (x + 1) * P] for y in (memh[l], meml[l])],
                                           [y[:, k, :] for y in w], k == 0, k == KD - 1)
                mm.then_inc(s("mkv_mm"), 1)
            pe.wait_ge(s("mem_kv"), 16)
            pe.wait_ge(s("consts_loaded"), 48)
            pe.wait_ge(s("norm_u"), 3 * KD)
            wb = wba[:, :].rearrange("p (k c) -> p k c", k=KD)
            for t in range(3):
                n = P if t < 2 else NS
                for k in range(KD):
                    mm = pe.matmul(bank(1)[0:n, 16 * t:16 * t + 16], u[:, k, t * P:t * P + n], wb[:, k, :],
                                   start=(k == 0), stop=(k == KD - 1))
            mm.then_inc(s("ba_mm"), 1)
            pe.wait_ge(s("gba_out"), 2)
            pe.wait_ge(s("m_lo"), 3 * KD)
            for t in range(36):
                w = weights(AT["a_in", t // 2], KD)
                if t >= 8:
                    pe.wait_ge(s("ain_out"), t - 7)
                tile(bank(t % 8)[:, 0:T], w, (t % 2) * P, (uh[0], ul[0]), T, square).then_inc(s("ain_mm"), 1)
            pe.wait_ge(s("ain_out"), 36)
            for g in range(4):
                pe.wait_ge(s("l2_sq"), g + 1)
                if g:
                    pe.wait_ge(s("l2_rt"), 2 * g)
                for x in range(4):
                    mm = pe.matmul(bank(x)[:, 0:ACTW], ones[:, :], sqq[:, x * ACTW:(x + 1) * ACTW], start=True, stop=True)
                mm.then_inc(s("l2_mm"), 1)
            pe.wait_ge(s("l2_rt"), 8)
            pe.wait_ge(s("consts_loaded"), 48)
            pe.wait_ge(s("gate_done"), 2)
            gp = gg[:, 0:2, :].rearrange("p t c -> p (t c)")
            pe.matmul(bank(0)[:, 0:16], tri, gp, start=True, stop=True)
            pe.matmul(bank(0)[:, 16:32], ones[:, :], gp, start=True, stop=True)
            pe.matmul(bank(0)[:, 32:160], ones[0:NS, :], gd[0:NS, :], start=True, stop=True).then_inc(s("coef_mm"), 1)

            def attention(l, first, last):
                for t in range(2):
                    for x in range(XH):
                        mm = pe.matmul(PP[t][:, x * NM:(x + 1) * NM], cq[:, x, t * P:(t + 1) * P],
                                       mk[l][:, x * NM:(x + 1) * NM], start=True, stop=True)
                    mm.then_inc(s("att_mm"), 1)
                for t in range(2):
                    pe.wait_ge(s("att_p"), 3 * l + t + 1)
                    for n in range(XH * MT):
                        mm = pe.transpose(PP[2 + t][:, n * P:(n + 1) * P], Pr[:, t * 1024 + n * P:t * 1024 + (n + 1) * P], ident)
                    mm.then_inc(s("att_tr"), 1)
                pe.wait_ge(s("att_pt"), 2 * l + 2)
                for x in range(XH):
                    for m in range(MT):
                        mm = pe.matmul(PP[0][:, x * SEQ:(x + 1) * SEQ], mv[l][:, m * 512 + x * P:m * 512 + (x + 1) * P],
                                       PrT[:, (x * MT + m) * SEQ:(x * MT + m + 1) * SEQ], start=(m == 0), stop=(m == MT - 1))
                mm.then_inc(s("att_o"), 1)
                pe.wait_ge(s("att_cat"), 2 * l + 1)
                kd, vd = f"kc{l}", f"vc{l}"
                for n in range(BH):
                    b, x = n // XH, n % XH
                    w = arrived(pe, AT[kd, n // 8]) if n % 8 == 0 else w
                    for m in range(MT):
                        mm = pe.matmul(bank(0)[:, m * BH + n:m * BH + n + 1],
                                       w[:, (n % 8) * NM + m * P:(n % 8) * NM + (m + 1) * P],
                                       cq[:, x, SEQ + b:SEQ + b + 1], start=True, stop=True)
                    if n % 8 == 7:
                        mm.then_inc(s("cache_mm"), 1)
                pe.wait_ge(s("sat_st"), 1 * l + 1)
                for m in range(MT):
                    mm = pe.transpose(bank(1)[0:BH, m * P:(m + 1) * P], STs[:, m * BH:(m + 1) * BH], ident)
                mm.then_inc(s("sat_s"), 1)
                pe.wait_ge(s("att_p"), 3 * l + 3)
                for m in range(MT):
                    mm = pe.transpose(bank(2)[:, m * BH:(m + 1) * BH], P32[0:BH, m * P:(m + 1) * P], ident[0:BH, 0:BH])
                mm.then_inc(s("att_tr"), 1)
                pe.wait_ge(s("sat_pt"), 1 * l + 1)
                for n in range(BH):
                    b, x = n // XH, n % XH
                    w = arrived(pe, AT[vd, b // 2]) if n % 8 == 0 else w
                    for m in range(MT):
                        at = ((b % 2) * MT + m) * 512 + x * P
                        mm = pe.matmul(bank(3)[:, n:n + 1], w[:, at:at + P], PT32[:, m * BH + n:m * BH + n + 1],
                                       start=(m == 0), stop=(m == MT - 1))
                    if n % 8 == 7:
                        mm.then_inc(s("cache_mm"), 1)

            pe.wait_ge(s("coef_dif"), 1)
            pe.wait_ge(s("l2_done"), 4)
            attention(0, None, None)

            for c in range(NCH):
                cols = slice(c * P, (c + 1) * P)
                pe.wait_ge(s("att_cat"), 2)
                if c:
                    pe.wait_ge(s("dl_cat"), c)
                    pe.wait_ge(s("S_done"), c)
                for x in range(H):
                    gcol = gg[:, c, x:x + 1].to_broadcast([P, P])
                    mm = pe.matmul(PP[0][:, x * P:(x + 1) * P], gcol, tri, start=True, stop=True)
                mm.then_inc(s("dl_grow"), 1)
                for w_, (m0, m1) in enumerate(((8, 0), (8, 8))):
                    for x in range(H):
                        mm = pe.matmul(PP[1 + w_][:, x * P:(x + 1) * P], act[:, m0 + x, cols], act[:, m1 + x, cols],
                                       start=True, stop=True)
                    mm.then_inc(s("dl_kk"), 1)
                for x in range(H):
                    mm = pe.matmul(PP[3][:, x * P:(x + 1) * P], gb[:, c, x:x + 1].to_broadcast([P, P]), ident,
                                   start=True, stop=True)
                mm.then_inc(s("dl_brow"), 1)
                if c == 0:
                    pe.wait_ge(s("conv_silu"), 24)
                pe.wait_ge(s("dl_pt"), c + 1)
                for x in range(H):
                    mm = pe.transpose(PP[1][:, x * P:(x + 1) * P], act[:, 16 + x, cols], ident)
                mm.then_inc(s("dl_tok"), 1)
                pe.wait_ge(s("dl_qd"), c + 1)
                for x in range(H):
                    mm = pe.transpose(PP[2][:, x * P:(x + 1) * P], act[:, 8 + x, cols], ident)
                mm.then_inc(s("dl_tok"), 1)
                pe.wait_ge(s("dl_kt"), c + 1)
                for lv in range(1, NLVL):
                    n0 = (c * (NLVL - 1) + lv - 1) * 2
                    u0 = (c * NLVL + lv) * 2
                    for g in range(2):
                        pe.wait_ge(s("dl_um"), u0 - 2 + g + 1)
                        if n0 + g >= 2:
                            pe.wait_ge(s("dl_t"), n0 + g - 1)
                        for x in range(4 * g, 4 * g + 4):
                            mm = pe.transpose(PP[0][:, x * P:(x + 1) * P], Ub[:, x * P:(x + 1) * P], ident)
                        mm.then_inc(s("dl_tt"), 1)
                    pe.wait_ge(s("dl_ml"), c * NLVL + lv + 1)
                    for g in range(2):
                        pe.wait_ge(s("dl_t"), n0 + g + 1)
                        if n0 + g >= 2:
                            pe.wait_ge(s("dl_x"), n0 + g - 1)
                        for x in range(4 * g, 4 * g + 4):
                            mm = pe.matmul(PP[1][:, x * P:(x + 1) * P], MLb[:, x * P:(x + 1) * P], Tb[:, x * P:(x + 1) * P],
                                           start=True, stop=True)
                        mm.then_inc(s("dl_xx"), 1)
                    for g in range(2):
                        pe.wait_ge(s("dl_x"), n0 + g + 1)
                        for x in range(4 * g, 4 * g + 4):
                            mm = pe.matmul(PP[2][:, x * P:(x + 1) * P], Xb[:, x * P:(x + 1) * P], Ub[:, x * P:(x + 1) * P],
                                           start=True, stop=True)
                        mm.then_inc(s("dl_du"), 1)
                pe.wait_ge(s("dl_um"), (c + 1) * NLVL * 2)
                R = vtok
                if c:
                    for x in range(H):
                        mm = pe.matmul(PP[0][:, x * P:(x + 1) * P], act[:, 8 + x, cols], Sb[:, x * P:(x + 1) * P],
                                       start=True, stop=True)
                    mm.then_inc(s("dl_ks"), 1)
                    pe.wait_ge(s("dl_r"), 1)
                    R = Xb
                for x in range(H):
                    mm = pe.matmul(PP[1][:, x * P:(x + 1) * P], Ub[:, x * P:(x + 1) * P], R[:, x * P:(x + 1) * P],
                                   start=True, stop=True)
                mm.then_inc(s("dl_uu"), 1)
                pe.wait_ge(s("dl_u"), c + 1)
                uu = Tb
                for x in range(H):
                    if c:
                        pe.matmul(PP[2][:, x * P:(x + 1) * P], Sb[:, x * P:(x + 1) * P], act[:, x, cols], start=True, stop=False)
                    mm = pe.matmul(PP[2][:, x * P:(x + 1) * P], uu[:, x * P:(x + 1) * P], PTb[:, x * P:(x + 1) * P],
                                   start=(c == 0), stop=True)
                mm.then_inc(s("dl_o"), 1)
                for x in range(H):
                    mm = pe.matmul(PP[3][:, x * P:(x + 1) * P], ktail[:, x * P:(x + 1) * P], uu[:, x * P:(x + 1) * P],
                                   start=True, stop=True)
                mm.then_inc(s("dl_ds"), 1)

            pe.wait_ge(s("dl_cat"), NCH)
            pe.wait_ge(s("S_done"), NCH)
            pe.wait_ge(s("sd_cols"), 1)
            pe.wait_ge(s("state_loaded"), 64)
            for n in range(DBH):
                mm = pe.matmul(bank(0)[:, 2 * n:2 * n + 2], state[:, n * P:(n + 1) * P], kq[:, n, :], start=True, stop=True)
            pe.matmul(bank(1)[:, 0:64], ones[:, :], kqd, start=True, stop=True).then_inc(s("sd_mm"), 1)
            pe.transpose(bank(4)[0:DBH, 0:P], t64, ident).then_inc(s("sd_rows"), 1)
            pe.wait_ge(s("sd_u"), 1)
            pe.transpose(bank(5)[0:DBH, 0:P], u64, ident).then_inc(s("sd_rows"), 1)
            pe.wait_ge(s("sd_row"), 2)
            for g in range(16):
                pe.wait_ge(s("sd_blk"), g + 1)
                if g >= 2:
                    pe.wait_ge(s("state_new"), g - 1)
                pe.matmul(bank(2 + g % 2), krow[0:DBH, :], ublk[g % 2][0:DBH, :], start=True, stop=True)\
                    .then_inc(s("sd_outer"), 1)
            pe.wait_ge(s("state_new"), 16)
            pe.wait_ge(s("sd_cat"), 1)
            for x in range(H):
                pe.wait_ge(s("on_sq"), x + 1)
                pe.matmul(bank(x)[:, 0:T], ones[:, :], sq[:, x * T:(x + 1) * T], start=True, stop=True).then_inc(s("on_mm"), 1)

            order = [(k, k) for k in (*range(H, H + XH), *range(H))]
            base_a = 3 * KD
            for t in range(KD):
                w = weights(AT["a_out", t], 12)
                tile(bank(t)[:, 0:T], w, 0, (cath[0], catl[0]), T, order,
                     ready=(lambda i: base_a + i + 1) if t == 0 else None).then_inc(s("aout_mm"), 1)
            pe.wait_ge(s("aout_h"), KD)
            norm(2, T)
            base_f = base_a + 12
            for f in range(FT):
                w = [x.rearrange("p k (g c) -> p k g c", g=2) for x in weights(AT["wi", f], KD)]
                if f >= 4:
                    pe.wait_ge(s("wi_prod"), f - 3)
                if f == 0:
                    pe.wait_ge(s("norm_rt"), 3)
                for g in range(2):
                    mm = tile(bank(2 * (f % 4) + g)[:, 0:T], [x[:, :, g, :] for x in w], 0, (uh[1], ul[1]), T, square,
                              ready=(lambda i: base_f + i + 1) if f == 0 and g == 0 else None)
                mm.then_inc(s("wi_mm"), 1)
            pe.wait_ge(s("wi_prod"), FT)
            for t in range(KD):
                for half in range(2):
                    w = weights(AT["wo", 2 * t + half], FT // 2)
                    ks = [(k, half * (FT // 2) + k) for k in range(FT // 2)]
                    for i, (kw, km) in enumerate(ks):
                        if t == 0:
                            pe.wait_ge(s("hid_lo"), km + 1)
                        mm = split_product(bank(t)[:, 0:T], [x[:, kw, :] for x in w],
                                           [x[:, km * T:(km + 1) * T] for x in (hidh, hidl)], km == 0, km == FT - 1)
                    mm.then_inc(s("wo_mm"), 1)
            pe.wait_ge(s("wo_h"), KD)
            norm(3, T)
            base_b = base_f + KD
            for t in range(12):
                w = weights(AT["b_in", t // 2], KD)
                if t >= 8:
                    pe.wait_ge(s("bin_out"), t - 7)
                if t == 0:
                    pe.wait_ge(s("norm_rt"), 4)
                tile(bank(t % 8)[:, 0:T], w, (t % 2) * P, (uh[2], ul[2]), T, square,
                     ready=(lambda i: base_b + i + 1) if t == 0 else None).then_inc(s("bin_mm"), 1)
            pe.wait_ge(s("bin_out"), 12)
            pe.wait_ge(s("pool_d"), 1)
            w = arrived(pe, AT["pool", 0]).rearrange("p (g k c) -> p g k c", g=4, k=2)
            for t in range(8):
                for k in range(2):
                    mm = pe.matmul(bank(t)[:, 0:T], w[:, t // 2, k, (t % 2) * P:(t % 2 + 1) * P], pd[:, (t // 2) * 2 + k, :],
                                   start=(k == 0), stop=(k == 1))
                mm.then_inc(s("pm_mm"), 1)
            pe.wait_ge(s("pm_cat"), 8)
            attention(1, None, None)
            pe.wait_ge(s("att_cat"), 4)
            base_o = base_b + KD
            for t in range(KD):
                w = weights(AT["b_out", t], 12)
                tile(bank(t)[:, 0:T], w, 0, (cath[1], catl[1]), T, [(k, k) for k in range(12)],
                     ready=(lambda i: base_o + i + 1) if t == 0 else None).then_inc(s("bout_mm"), 1)
            pe.wait_ge(s("bout_h"), KD)
            norm(4, T, sqb=fsq)
            pe.wait_ge(s("norm_u"), 48)
            pe.wait_ge(s("consts_loaded"), 48)
            rw = router[:, :].rearrange("p (k c) -> p k c", k=KD)
            for t in range(3):
                n = P if t < 2 else NS
                for k in range(KD):
                    mm = pe.matmul(bank(0)[0:n, E * t:E * t + E], u[:, k, t * P:t * P + n], rw[:, k, :],
                                   start=(k == 0), stop=(k == KD - 1))
            mm.then_inc(s("rt_mm"), 1)
            for t in range(3):
                n = P if t < 2 else NS
                for k in range(KD):
                    mm = pe.transpose(PP[1 + t][0:n, k * P:(k + 1) * P], u[:, k, t * P:t * P + n], ident)
                mm.then_inc(s("xt_mm"), 1)
            pe.wait_ge(s("rt_sub"), 1)
            sel = rr[2]
            pe.matmul(bank(0)[:, 0:8], stri, sel[:, 0:8], start=True, stop=True)
            pe.matmul(bank(0)[:, 8:16], stri, sel[:, 8:16], start=True, stop=False)
            pe.matmul(bank(0)[:, 8:16], ones[:, :], sel[:, 0:8], start=False, stop=True)
            pe.matmul(bank(0)[:, 16:24], stri, sel[:, 16:24], start=True, stop=False)
            pe.matmul(bank(0)[:, 16:24], ones[:, :], sel[:, 0:8], start=False, stop=False)
            pe.matmul(bank(0)[:, 16:24], ones[:, :], sel[:, 8:16], start=False, stop=True)
            pe.matmul(bank(0)[:, 24:32], ones[:, :], sel[:, 0:8], start=True, stop=False)
            pe.matmul(bank(0)[:, 24:32], ones[:, :], sel[:, 8:16], start=False, stop=False)
            pe.matmul(bank(0)[:, 24:32], ones[0:NS, :], sel[0:NS, 16:24], start=False, stop=True).then_inc(s("pos_mm"), 1)

            def gather():
                for k in range(KD):
                    for t in range(3):
                        n = P if t < 2 else NS
                        mm = pe.matmul(PP[1][:, k * C:(k + 1) * C], xtok[0:n, t, k * P:(k + 1) * P], disp[0:n, t, :],
                                       start=(t == 0), stop=(t == 2))
                mm.then_inc(s("gat_mm"), 1)

            pe.wait_ge(s("xt_out"), 3)
            pe.wait_ge(s("disp"), 3)
            gather()
            pe.wait_ge(s("steps_known"), 1)
            n_rounds = pe.value_load(nsteps_i[0:1, 0:1], min_val=1, max_val=ROUNDS)

            def combine(before):
                for t in range(KD):
                    if t >= 4:
                        pe.wait_ge(s("comb_h"), before + (t - 3))
                    pe.matmul(bank(2 + t % 4)[:, 0:T], yslot[:, t * P:(t + 1) * P], comb, start=True, stop=True)\
                        .then_inc(s("cmb_mm"), 1)

            with pe.Fori(0, n_rounds * E) as st:
                def up(c):
                    f, g = c // 4, c // 2 % 2
                    pe.wait_ge(s("w_lo"), st * PERX + (c + 1))
                    w = [as_chunk(x[c % XSET][:, :], c) for x in (whi, wlo)]
                    for k in range(4):
                        kk = (c % 2) * 4 + k
                        mm = split_product(bank(2 * (f % 2) + g), [x[:, kk * C:(kk + 1) * C] for x in (xsh, xsl)],
                                           [x[:, k, :] for x in w], kk == 0, kk == KD - 1)
                    mm.then_inc(s("up_mm"), 1)

                def turn(f):
                    pe.wait_ge(s("up_h"), st * FCN + (f + 1))
                    if f >= 2:
                        pe.wait_ge(s("ht_lo"), st * FCN + (f - 1))
                    for x in range(4):
                        mm = pe.transpose(bank(4 + f % 2)[:, x * C:(x + 1) * C], hslot[f % 2][:, x * P:(x + 1) * P], ident)
                    mm.then_inc(s("ht_mm"), 1)

                pe.wait_ge(s("xs_lo"), st + 1)
                for c in range(NUP):
                    if c % 4 == 0 and c >= 8:
                        pe.wait_ge(s("up_h"), st * FCN + (c // 4 - 1))
                    if c == 4:
                        pe.wait_ge(s("comb_h"), st * KD + KD)
                    up(c)
                    if c == 1:
                        pe.wait_ge(s("y_out"), st + 1)
                        pe.wait_ge(s("comb_out"), st + 1)
                        combine(st * KD)
                    if c % 4 == 3 and c > 3:
                        turn(c // 4 - 1)
                pe.wait_ge(s("disp"), st * 3 + 6)
                pe.wait_ge(s("up_h"), st * FCN + (FCN - 1))
                gather()
                turn(FCN - 1)
                for j in range(NDOWN):
                    c = NUP + j
                    pe.wait_ge(s("w_lo"), st * PERX + (c + 1))
                    pe.wait_ge(s("ht_lo"), st * FCN + (j // 2 + 1))
                    w = [as_chunk(x[c % XSET][:, :], c) for x in (whi, wlo)]
                    for k in range(2):
                        kk = 2 * j + k
                        for g in range(2):
                            mm = split_product(bank(6 + g), [x[:, kk * C:(kk + 1) * C] for x in (hTh, hTl)],
                                               [x[:, k, g * 512:(g + 1) * 512] for x in w], kk == 0, kk == KE - 1)
                    mm.then_inc(s("down_mm"), 1)
                    if j == 4:
                        pe.wait_ge(s("dispg"), st * 3 + 3)
                        pe.wait_ge(s("up_h"), st * FCN + FCN)
                        pe.wait_ge(s("ht_lo"), st * FCN + (FCN - 1))
                        for t in range(3):
                            n = P if t < 2 else NS
                            mm = pe.transpose(bank(5)[:, t * P:t * P + n], dispg[0:n, t, :], ident[0:n, 0:n])
                        mm.then_inc(s("cmb_tr"), 1)
            pe.wait_ge(s("y_out"), n_rounds * E + 1)
            pe.wait_ge(s("comb_out"), n_rounds * E + 1)
            pe.wait_ge(s("xs_lo"), n_rounds * E + 1)
            combine(n_rounds * E * KD)
            pe.wait_ge(s("comb_h"), n_rounds * E * KD + KD)
            norm(5, T, sqb=fsq)


def kernel(**inputs):
    import concourse.bacc as bacc
    from concourse.bass_utils import run_bass_kernel_spmd

    f = {k: np.asarray(v) for k, v in inputs.items()}

    def fm(x):
        t, d = x.shape
        return x.T.reshape(d // P, P, t).transpose(1, 0, 2).reshape(P, -1)

    def tiles(w, per):
        k, n = w.shape
        return w.reshape(k // P, P, n // per, per).transpose(2, 1, 0, 3).reshape(n // per, P, -1)

    def col(g):
        return g.reshape(-1, P).T

    def rows(g):
        return np.broadcast_to(g.reshape(1, -1), (P, g.size))

    w_in = f["a_w_in"][0]
    split = CT * P + H * P
    ff = f["a_ffn_wi"][0]
    ffa = ff.reshape(KD, P, 2, FT, P).transpose(3, 1, 0, 2, 4).reshape(FT, P, -1)
    kc = f["cache_mem_k"]
    vc = f["cache_mem_v"]
    i = np.arange(P)
    J, I = i[:, None], i[None, :]
    lvl = [((I >> (l + 1)) == (J >> (l + 1))) & (((I >> l) & 1) == 1) & (((J >> l) & 1) == 0) for l in range(NLVL)]
    tie = (np.arange(E)[None, :] < np.arange(E)[:, None]).reshape(1, -1)
    cinv = np.stack([1.0 / np.minimum(np.arange(16) + 1, 2 << g) for g in range(4)]).reshape(1, -1)
    consts = np.concatenate([J == I, J <= I, J < I, np.where(J <= I, 0.0, -1e30)] + lvl
                            + [np.broadcast_to(I, (P, P)), np.broadcast_to(tie, (P, E * E)),
                               np.broadcast_to(cinv, (P, 64))], axis=1).astype(np.float32)
    gains = np.concatenate([col(f["a_norm1"]), col(f["a_norm2"]), col(f["b_norm1"]), col(f["b_norm2"]),
                            col(f["final_norm"]), col(f["m_norm"][0]), col(f["m_norm"][1]), col(f["b_pool_scale"]),
                            col(f["a_o_norm"]),
                            f["a_conv_w"][0].reshape(CW, CT, P).transpose(2, 1, 0).reshape(P, -1),
                            rows(f["a_a_log"]), rows(f["a_dt_bias"])], axis=1)
    arrays = {
        "x": fm(np.concatenate([f["x_prompt"][0], f["x_sample"][:, 0]], axis=0)),
        "mem": fm(f["mem_prompt"][0]),
        "gains": gains,
        "consts": consts,
        "wba": w_in[:, split:split + 16].reshape(KD, P, 16).transpose(1, 0, 2).reshape(P, -1),
        "router": f["b_router"][0].reshape(KD, P, E).transpose(1, 0, 2).reshape(P, -1),
        "convbuf": f["state_dn_conv"][0].reshape(NS, CW - 1, CT, P).transpose(3, 2, 0, 1).reshape(P, -1),
        "poolbuf": f["state_pool"][0].reshape(NS, PW, KD, P).transpose(3, 2, 0, 1).reshape(P, -1),
        "a_in": tiles(np.concatenate([w_in[:, :split], w_in[:, split + 16:]], axis=1), 256),
        "mkv": np.concatenate([tiles(f[n][l], 256) for l in range(2) for n in ("m_w_k", "m_w_v")]),
        "state": f["state_dn"][0].reshape(4, 16, P, P).transpose(0, 2, 1, 3).reshape(4, P, -1),
        "a_out": tiles(f["a_w_out"][0], P),
        "wi": ffa,
        "wo": f["a_ffn_wo"][0].reshape(2, FT // 2, P, KD, P).transpose(3, 0, 2, 1, 4).reshape(2 * KD, P, -1),
        "b_in": tiles(f["b_w_in"][0], 256),
        "pool": f["b_pool_w"].reshape(1, 4, 2, P, 256).transpose(0, 3, 1, 2, 4).reshape(1, P, -1),
        "b_out": tiles(f["b_w_out"][0], P),
        "wi_e": f["b_moe_wi"][0],
        "wo_e": f["b_moe_wo"][0],
    }
    for l in range(2):
        arrays[f"kc{l}"] = kc[l].reshape(4, 2, NM, XH, P).transpose(0, 4, 1, 3, 2).reshape(4, P, -1)
        arrays[f"vc{l}"] = vc[l].reshape(4, 2, MT, P, XH * P).transpose(0, 3, 1, 2, 4).reshape(4, P, -1)
    shapes = {"y": (P, KD * T), "S": (P, 1024), "conv": (P, 648), "pool": (P, 8 * 135), "mk": (2, P, 1024),
              "mv": (2, P, 1024), "state": (4, P, DCH)}
    nc = bacc.Bacc("TRN2", target_bir_lowering=False, num_devices=1)
    ins = {}
    sent = {}
    for name, a in arrays.items():
        a = np.ascontiguousarray(a)
        sent[f"in_{name}"] = a
        ins[name] = nc.dram_tensor(f"in_{name}", a.shape, F32, kind="ExternalInput").ap()
    outs = {n: nc.dram_tensor(f"out_{n}", sh, F32, kind="ExternalOutput").ap() for n, sh in shapes.items()}
    build(nc, ins, outs)
    r = run_bass_kernel_spmd(nc, [sent], core_ids=[0])
    o = {n: r.results[0][f"out_{n}"] for n in shapes}

    y = o["y"].reshape(P, KD, T).transpose(2, 1, 0).reshape(T, D)
    S = o["S"].reshape(P, H, P).transpose(1, 0, 2)[None, None]
    cv = o["conv"].reshape(P, CT, 27).transpose(2, 1, 0).reshape(27, CT * P)
    pl = o["pool"].reshape(P, KD, 135).transpose(2, 1, 0).reshape(135, D)
    mk = o["mk"].reshape(2, P, XH, NM).transpose(0, 3, 2, 1)[:, None]
    mv = o["mv"].reshape(2, P, MT, XH, P).transpose(0, 2, 1, 3, 4).reshape(2, 1, NM, XH, P)
    st = o["state"].reshape(4, P, 16, P).transpose(0, 2, 1, 3).reshape(1, NS, H, P, P)
    c = np.ascontiguousarray
    return (c(y[None, :SEQ]), c(y[SEQ:, None]), c(S), c(cv[None, None, :3]), c(pl[None, None, :PW]), c(mk), c(mv), c(st),
            c(cv[3:].reshape(1, NS, CW - 1, CT * P)), c(pl[PW:].reshape(1, NS, PW, D)))
```

```python
from contextlib import ExitStack

import numpy as np
import concourse.bass as bass
from concourse import mybir

F32 = mybir.dt.float32
F32R = mybir.dt.float32r
I32 = mybir.dt.int32
ALU = mybir.AluOpType
ACT = mybir.ActivationFunctionType
AX = mybir.AxisListType.X

P = 128
D = 1024
KD = D // P
SEQ, NS = 256, 8
T = SEQ + NS
H = 8
NCH = SEQ // P
CW = 4
CT = 24
PRE = CW - 1 + SEQ + CW * NS
ACTW = PRE - (CW - 1)
S0 = SEQ + CW - 1
XH = 4
NM = 256
MT = NM // P
BH = NS * XH
DBH = NS * H
FF = 2816
FT = FF // P
E = 8
FE = 3584
FCN = FE // 512
KE = FE // P
C = P
ROUNDS = -(-T // C)
PW = 15
PCOL = PW + SEQ + (PW + 1) * NS
EPS = 1e-6
DCH = 2048
DRAW = 2
DSET = 2
ARENA = DRAW * DCH + DSET * 2 * DCH
WREG = 28672
PERX = 42
NUP, NDOWN = 28, 14
XCH = 2048
XRAW = 7
XSET = 3
assert PERX % XRAW == 0 and PERX % XSET == 0
TURNED = {4 * f + 10: f for f in range(FE // 512 - 1)} | {32: FE // 512 - 1}
NLVL = 7

KINDS = [("mkv", 8, 2048, True), ("a_in", 18, 2048, True), ("kc0", 4, 2048, False), ("vc0", 4, 2048, False),
         ("a_out", 8, 12 * P, True), ("wi", 22, 2048, True),
         ("wo", 16, FT // 2 * P, True), ("b_in", 6, 2048, True), ("pool", 1, 2048, False),
         ("kc1", 4, 2048, False), ("vc1", 4, 2048, False), ("b_out", 8, 12 * P, True)]
DENSE = [(kind, i) for kind, n, _, _ in KINDS for i in range(n)]
ND = len(DENSE)
AT = {c: n for n, c in enumerate(DENSE)}
WIDTH = {kind: w for kind, _, w, _ in KINDS}
SPLIT = {kind: x for kind, _, _, x in KINDS}
HALVED = [n for n, (kind, _) in enumerate(DENSE) if SPLIT[kind]]
TURN = {n: q for q, n in enumerate(HALVED)}
RUN = {n: ("mkv", "a_in").count(k) or 2 * ("a_out", "wi", "wo", "b_in").count(k) or 3 for n, (k, _) in enumerate(DENSE)}
CHUNKS = {"aout": "a_out", "wo": "wo", "bout": "b_out"}

CIDENT, CTRI, CSTRI, CNEG, CLVL = 0, P, 2 * P, 3 * P, 4 * P
CIOTA = CLVL + NLVL * P
CTIE = CIOTA + P
CINV = CTIE + E * E
CN = CINV + 4 * 16
GA1, GA2, GB1, GB2, GFIN, GM0, GM1, GPS = (8 * i for i in range(8))
GON = 64
GTAP = 65
GALOG = GTAP + CT * CW
GDT = GALOG + H
GN = GDT + H


def build(nc, ins, outs):
    ctx = ExitStack()
    with ctx:
        def sb(name, n, dt=F32):
            return ctx.enter_context(nc.sbuf_tensor(name, [P, n], dt))

        def sem(name):
            return ctx.enter_context(nc.semaphore(name))

        consts = sb("consts", CN)
        gains = sb("gains", GN)
        wba = sb("wba", KD * 16)
        router = sb("router", KD * E)
        ones = sb("ones", P)
        epsc = sb("epsc", 1)
        pick = sb("pick", 31)
        small = sb("small", 840)
        nsteps_i = sb("nsteps_i", 1, I32)
        hbuf = sb("hbuf", KD * T)
        ubuf = sb("ubuf", KD * T)
        base = (nc.sbuf_base + 63) // 64 * 64
        sb("weights", WREG + 32)

        def at(name, off, n, dt):
            return nc.alloc_sbuf_tensor_at(name, [P, n], dt, offset=base + 4 * off)

        ring = at("ring", 0, WREG, F32)
        whi = [at(f"whi{i}", 2 * i * XCH, XCH, F32R) for i in range(XSET)]
        wlo = [at(f"wlo{i}", (2 * i + 1) * XCH, XCH, F32R) for i in range(XSET)]
        assert 2 * XSET * XCH <= ARENA
        draw = [ring[:, i * DCH:(i + 1) * DCH] for i in range(DRAW)]
        dhi = [at(f"dhi{i}", DRAW * DCH + 2 * i * DCH, DCH, F32R) for i in range(DSET)]
        dlo = [at(f"dlo{i}", DRAW * DCH + (2 * i + 1) * DCH, DCH, F32R) for i in range(DSET)]
        raw = at("raw", 2 * XSET * XCH, XRAW * XCH, F32)
        tail = (2 * XSET + XRAW) * XCH
        PP = [ctx.enter_context(nc.psum_tensor(f"PP{i}", [P, 1024], F32)) for i in range(4)]

        def bank(b):
            return PP[b // 2][:, (b % 2) * 512:(b % 2) * 512 + 512]

        ident = consts[:, CIDENT:CIDENT + P]
        tri = consts[:, CTRI:CTRI + P]
        stri = consts[:, CSTRI:CSTRI + P]
        neg = consts[:, CNEG:CNEG + P]
        iota = consts[:, CIOTA:CIOTA + P]
        h = hbuf[:, :].rearrange("p (k t) -> p k t", k=KD)
        u = ubuf[:, :].rearrange("p (k t) -> p k t", k=KD)

        def cut(buf, at, n):
            return buf[:, at:at + n]

        arena = ARENA
        pre = cut(ring, arena, CT * PRE).rearrange("p (m c) -> p m c", m=CT)
        act = cut(ring, arena + CT * PRE, CT * ACTW).rearrange("p (m c) -> p m c", m=CT)
        z = cut(ring, arena + CT * (PRE + ACTW), H * T).rearrange("p (m c) -> p m c", m=H)
        assert CT * (PRE + ACTW) + H * T <= WREG - ARENA
        state = ring[:, DRAW * DCH:DRAW * DCH + DBH * P]
        assert DBH * P == DSET * 2 * DCH
        memh = [at(f"memh{i}", arena + 4096 * i, 2048, F32R) for i in range(2)]
        meml = [at(f"meml{i}", arena + 4096 * i + 2048, 2048, F32R) for i in range(2)]
        cath = [at("cath0", arena, 12 * T, F32R)]
        catl = [at("catl0", arena + 12 * T, 12 * T, F32R)]
        hidh = at("hidh", arena, FT * T, F32R)
        hidl = at("hidl", arena + FT * T, FT * T, F32R)
        uh = [None, at("uh1", arena + 2 * FT * T, KD * T, F32R)]
        ul = [None, at("ul1", arena + 2 * FT * T + KD * T, KD * T, F32R)]
        assert 2 * FT * T + 2 * KD * T <= WREG - ARENA
        DTb, MTb, MLb, Xb, PTb, Sb = (cut(ring, arena + 1024 * i, 1024) for i in range(6))
        GEN = 1056 + 3168 + 4 * 1024 + 648 + 8100
        gbase = (nc.sbuf_base + 63) // 64 * 64
        sb("activations", GEN + 32)

        def gat_(name, off, n, dt=F32):
            return nc.alloc_sbuf_tensor_at(name, [P, n], dt, offset=gbase + 4 * off)

        gen = gat_("gen", 0, GEN)
        uh[0], ul[0] = gat_("uh0", 1056, KD * T, F32R), gat_("ul0", 8968 + 4688, KD * T, F32R)
        uh.append(gat_("uh2", 1056, KD * T, F32R))
        ul.append(gat_("ul2", 1056 + KD * T, KD * T, F32R))
        cath.append(gat_("cath1", 4224, 12 * T, F32R))
        catl.append(gat_("catl1", 8968, 12 * T, F32R))
        cq = cut(gen, 0, XH * T).rearrange("p (m c) -> p m c", m=XH)
        cat = cut(gen, 1056, 12 * T).rearrange("p (m c) -> p m c", m=12)
        mk = [cut(gen, 4224 + 2048 * i, 1024) for i in range(2)]
        mv = [cut(gen, 5248 + 2048 * i, 1024) for i in range(2)]
        convio = cut(gen, 8320, 648)
        SC = 8968
        SCN = GEN - SC
        memT = cut(gen, 1056, KD * NM).rearrange("p (k t) -> p k t", k=KD)
        sq = cut(gen, SC, KD * T)
        rt = cut(gen, SC + 2112, 264)
        rs = cut(gen, SC + 2376, 264)
        memn = [cut(gen, SC + 2640 + 2048 * i, 2048).rearrange("p (k t) -> p k t", k=KD) for i in range(2)]
        assert 2640 + 4096 <= SCN
        sqq = cut(gen, SC, 2 * H * ACTW)
        l2root = cut(gen, SC + 2 * H * ACTW, ACTW)
        l2inv = cut(gen, SC + (2 * H + 1) * ACTW, ACTW)
        Pr_of = [cut(gen, SC, 2048), cut(gen, 4224, 2048)]
        PrT = cut(gen, SC + 2048, 2048)
        P32 = cut(gen, SC + 64, 256)
        O32 = cut(gen, SC + 320, P)
        q_diag = cut(gen, SC + 6400, BH * BH)
        p_diag = PrT[:, 0:MT * BH * BH]
        kq_diag = cut(gen, 4224, 2 * DBH * 16)
        Tb, Ub, vtok, ktail = (cut(gen, SC + 1024 * i, 1024) for i in range(4))
        DS = SC + 4096
        kq = cut(gen, DS, 128).rearrange("p (n c) -> p n c", c=2)
        v64 = cut(gen, DS + 128, 64)
        kqd = cut(gen, DS + 192, 64)
        t64 = cut(gen, DS + 256, 64)
        u64 = cut(gen, DS + 320, 64)
        qku = cut(gen, DS + 384, 64)
        krow = cut(gen, DS + 448, 128)
        kqrow = cut(gen, DS + 704, 512)
        urow = cut(gen, DS + 576, 128)
        ublk = [cut(gen, DS + 704 + 512 * i, 512) for i in range(2)]
        sil = [cut(gen, SC + 2640 + 264 * i, 264) for i in range(2)]
        hidf = [cut(gen, SC + 264 * i, 264) for i in range(2)]
        pin = cut(gen, SC, KD * PCOL).rearrange("p (m c) -> p m c", m=KD)
        psm = cut(gen, SC + KD * PCOL, KD * PCOL).rearrange("p (m c) -> p m c", m=KD)
        poolbuf = cut(gen, SC + KD * PCOL, KD * NS * PW)
        assert 2 * KD * PCOL <= SCN
        pst = cut(ring, tail, 8 * 135)
        pd = cut(gen, 1056, KD * T).rearrange("p (m c) -> p m c", m=KD)
        pfix = cut(small, 512, 128)

        xtok = cut(gen, 0, 3 * D).rearrange("p (t c) -> p t c", t=3)
        hTh = gat_("hTh", 3072, KE * C, F32R)
        hTl = gat_("hTl", 3072 + KE * C, KE * C, F32R)
        xsh = gat_("xsh", 10240, KD * C, F32R)
        xsl = gat_("xsl", 11264, KD * C, F32R)
        yslot = cut(gen, 12288, D)
        disp = cut(gen, 13312, 384).rearrange("p (t c) -> p t c", t=3)
        dispg = cut(gen, 13696, 384).rearrange("p (t c) -> p t c", t=3)
        comb = cut(gen, 14080, T)
        esil = [cut(ubuf, 512 * i, 512) for i in range(2)]
        hslot = [cut(ubuf, 1024 + 512 * i, 512) for i in range(2)]
        rout = cut(ring, tail, 3 * E)
        rtmp = cut(ring, tail + 32, 3 * E * E)
        rtm2 = cut(ring, tail + 224, 3 * E * E)
        rr = [cut(ring, tail + 416 + 24 * i, 24) for i in range(8)]
        NSTX = (ROUNDS + 1) * E
        posx = cut(ring, tail + 608, NSTX * 3).rearrange("p (s t) -> p s t", t=3)
        gatex = cut(ring, tail + 608 + NSTX * 3, NSTX * 3).rearrange("p (s t) -> p s t", t=3)
        cnt8 = cut(ring, tail + 608 + 6 * NSTX, 16)
        fsq = cut(gen, 14400, KD * T)
        frt = cut(gen, 16512, 264)
        frs = cut(gen, 16776, 264)

        gba = cut(small, 0, 48).rearrange("p (t c) -> p t c", t=3)
        gx, gax, ge, gl, gg, gb = (cut(small, 48 + 24 * i, 24).rearrange("p (t c) -> p t c", t=3)
                                   for i in range(6))
        gea = cut(small, 192, 8)
        gd = cut(small, 200, 128)
        cG, cnG, cdl, ceG, ctail, ceGl, cbeG = (cut(small, 328 + 16 * i, 16) for i in range(7))
        sgb = cut(small, 440, 128)
        amx = cut(small, 568, 8)
        anm = cut(small, 576, 8)
        asum = cut(small, 584, 8)
        ars = cut(small, 592, 8)
        sgt = cut(small, 600, 128)
        cgt = cut(small, 728, 32)

        raw_loaded = [sem(f"raw_loaded{i}") for i in range(XRAW)]
        slot_loaded = [sem(f"slot_loaded{i}") for i in range(DRAW)]
        names = {}

        def s(name):
            if name not in names:
                names[name] = sem(name)
            return names[name]

        block = ctx.enter_context(nc.Block())

        def read_by(n):
            kind, i = DENSE[n]
            return {"mkv": ("mkv_mm", 2 * (i + 1)), "a_in": ("ain_mm", 2 * (i + 1)),
                    "kc0": ("cache_mm", i + 1), "vc0": ("cache_mm", i + 5),
                    "a_out": ("aout_mm", i + 1), "wi": ("wi_mm", i + 1), "wo": ("wo_mm", i + 1),
                    "b_in": ("bin_mm", 2 * (i + 1)), "pool": ("pm_mm", 8),
                    "kc1": ("cache_mm", i + 9), "vc1": ("cache_mm", i + 13), "b_out": ("bout_mm", i + 1)}[kind]

        def arrived(eng, n):
            eng.wait_ge(slot_loaded[n % DRAW], 16 * (n // DRAW + 1))
            return draw[n % DRAW][:, 0:WIDTH[DENSE[n][0]]]

        def halves(n):
            q, w = TURN[n], WIDTH[DENSE[n][0]]
            return dhi[q % DSET][:, 0:w], dlo[q % DSET][:, 0:w]

        def dense_high(a, n):
            x, q = arrived(a, n), TURN[n]
            if q >= DSET:
                name, count = read_by(HALVED[q - DSET])
                a.wait_ge(s(name), count)
            a.activation(halves(n)[0], x, ACT.Copy).then_inc(s("d_hi"), 1)

        def dense_low(v, n):
            v.wait_ge(s("d_hi"), TURN[n] + 1)
            high, low = halves(n)
            v.tensor_tensor(low, draw[n % DRAW][:, 0:WIDTH[DENSE[n][0]]], high.bitcast(F32), ALU.subtract)\
                .then_inc(s("d_lo"), 1)

        wi_e = ins["wi_e"].rearrange("e (k p) n -> e p k n", p=P)
        wo_e = ins["wo_e"].rearrange("e (k p) n -> e p k n", p=P)

        def expert_source(e, c):
            if c < NUP:
                col = (c // 2 % 2) * FE + (c // 4) * 512
                k = 4 * (c % 2)
                return wi_e[bass.ds(e, 1), :, k:k + 4, col:col + 512].rearrange("e p k n -> p (e k) n")
            k = 2 * (c - NUP)
            return wo_e[bass.ds(e, 1), :, k:k + 2, :].rearrange("e p k n -> p (e k) n")

        def as_chunk(buf, c):
            return buf.rearrange("p (k n) -> p k n", n=512 if c < NUP else D)

        def raw_of(c):
            return cut(raw, (c % XRAW) * XCH, XCH)

        def new_state(v, g):
            v.wait_ge(s("sd_outer"), g + 1)
            for x in range(4):
                sl = state[:, (4 * g + x) * P:(4 * g + x + 1) * P]
                ins_ = v.scalar_tensor_tensor(out=sl, in0=sl, scalar=sgb[:, 4 * g + x:4 * g + x + 1],
                                              in1=bank(2 + g % 2)[:, x * P:(x + 1) * P], op0=ALU.mult, op1=ALU.add)
            ins_.then_inc(s("state_new"), 1)

        @block.sync
        def _(sp):
            sp.dma_start(memT, ins["mem"].rearrange("p (k t) -> p k t", k=KD)).then_inc(s("mem_loaded"), 16)
            sp.dma_start(gains[:, :], ins["gains"]).then_inc(s("gains_loaded"), 16)
            for n, (kind, i) in enumerate(DENSE):
                if n == 2:
                    sp.dma_start(hbuf[:, :], ins["x"]).then_inc(s("x_loaded"), 16)
                    sp.dma_start(consts[:, :], ins["consts"]).then_inc(s("consts_loaded"), 16)
                    sp.dma_start(router[:, :], ins["router"]).then_inc(s("consts_loaded"), 16)
                    sp.dma_start(wba[:, :], ins["wba"]).then_inc(s("consts_loaded"), 16)
                if n == 2:
                    sp.dma_start(convio[:, 0:576], ins["convbuf"]).then_inc(s("convbuf_loaded"), 16)
                if (kind, i) == ("kc0", 0):
                    sp.wait_ge(s("ain_mm"), 36)
                    for x in range(4):
                        sl = slice(x * DCH, (x + 1) * DCH)
                        sp.dma_start(state[:, sl], ins["state"][x]).then_inc(s("state_loaded"), 16)
                if n >= DRAW:
                    old = n - DRAW
                    name, count = ("d_lo", TURN[old] + 1) if SPLIT[DENSE[old][0]] else read_by(old)
                    sp.wait_ge(s(name), count)
                sp.dma_start(draw[n % DRAW][:, 0:WIDTH[kind]], ins[kind][i]).then_inc(slot_loaded[n % DRAW], 16)

            def load(e, c, before):
                before()
                sp.dma_start(as_chunk(raw_of(c), c), expert_source(e, c)).then_inc(raw_loaded[c % XRAW], 16)

            def step(e, after, st):
                for c in range(XSET, PERX):
                    load(e, c, lambda: sp.wait_ge(s("w_lo"), st * PERX + (c - XRAW + 1)))
                for c in range(XSET):
                    load(after, c, lambda: sp.wait_ge(s("w_lo"), st * PERX + (PERX + c - XRAW + 1)))

            sp.wait_ge(s("wo_mm"), KD)
            for c in range(PERX + XSET):
                load(c // PERX, c % PERX, lambda: sp.wait_ge(s("w_lo"), c - XRAW + 1) if c >= XRAW else None)
            with sp.Fori(1, E - 1) as e:
                step(e, e + 1, e)
            step(E - 1, 0, E - 1)
            sp.wait_ge(s("steps_known"), 1)
            n_rounds = sp.value_load(nsteps_i[0:1, 0:1], min_val=1, max_val=ROUNDS)
            with sp.If(n_rounds > 1):
                with sp.Fori(1, n_rounds) as r:
                    with sp.Fori(0, E - 1) as e:
                        step(e, e + 1, r * E + e)
                    step(E - 1, 0, r * E + (E - 1))
            sp.wait_ge(s("kv_stored"), 64)
            sp.wait_ge(s("S_stored"), 16)
            sp.wait_ge(s("state_stored0"), 32)
            sp.wait_ge(s("state_stored1"), 32)
            sp.wait_ge(s("outputs_stored"), 48)

        @block.gpsimd
        def _(pool):
            pool.memset(ones[:, :], 1.0).then_inc(s("ones_set"), 1)
            pool.memset(epsc[:, :], EPS).then_inc(s("ones_set"), 1)
            pool.memset(pick[:, 0:15], 0.0).then_inc(s("ones_set"), 1)
            pool.memset(pick[:, 16:31], 0.0).then_inc(s("ones_set"), 1)
            pool.memset(pick[:, 15:16], 1.0).then_inc(s("ones_set"), 1)

            def store(dst, src):
                pool.dma_start(dst, src).then_inc(s("outputs_stored"), 16)

            pool.wait_ge(s("mem_kv"), 16)
            for l in range(2):
                pool.dma_start(outs["mk"][l], mk[l]).then_inc(s("kv_stored"), 16)
                pool.dma_start(outs["mv"][l], mv[l]).then_inc(s("kv_stored"), 16)
            pool.wait_ge(s("conv_state"), 2)
            store(outs["conv"], convio)
            pool.wait_ge(s("ain_mm"), 36)
            pool.memset(q_diag, 0.0).then_inc(s("diag_zero"), 1)
            pool.wait_ge(s("att_o"), 1)
            pool.memset(p_diag, 0.0).then_inc(s("diag_zero"), 1)
            pool.wait_ge(s("kv_stored"), 64)
            pool.memset(kq_diag, 0.0).then_inc(s("diag_zero"), 1)
            pool.wait_ge(s("S_done"), 2)
            pool.dma_start(outs["S"], Sb).then_inc(s("S_stored"), 16)
            for i in range(4):
                pool.wait_ge(s("state_new"), 4 * (i + 1))
                pool.dma_start(outs["state"][i], state[:, i * DCH:(i + 1) * DCH]).then_inc(s(f"state_stored{i // 2}"), 16)
            pool.wait_ge(s("norm_u"), 32)
            pool.dma_start(poolbuf, ins["poolbuf"]).then_inc(s("poolbuf_loaded"), 16)
            pool.wait_ge(s("pool_state"), 2)
            store(outs["pool"], pst)
            pool.wait_ge(s("att_o"), 3)
            pool.memset(p_diag, 0.0).then_inc(s("diag_zero"), 1)
            pool.wait_ge(s("norm_u"), 56)
            store(outs["y"], ubuf[:, :])

        @block.scalar
        def _(a):
            own = [0]

            def link(ins_):
                own[0] += 1
                ins_.then_inc(s("act_own"), 1)
                a.wait_ge(s("act_own"), own[0])

            def norm(i, src, n, ready, scale, eps_in=epsc, sqb=None, rtb=None):
                sqb = sq if sqb is None else sqb
                rtb = rt if rtb is None else rtb
                for k in range(KD):
                    ready(k)
                    a.activation(sqb[:, k * n:(k + 1) * n], src[:, k, :], ACT.Square).then_inc(s("norm_sq"), 1)
                a.wait_ge(s("norm_ss"), i + 1)
                a.activation(rtb[:, 0:n], bank(0)[:, 0:n], ACT.Sqrt, bias=epsc[:, 0:1], scale=scale)\
                    .then_inc(s("norm_rt"), 1)

            a.wait_ge(s("ones_set"), 2)
            a.wait_ge(s("gains_loaded"), 16)

            def high(dst, src, n, tiles, ready):
                for k in tiles:
                    ready(k)
                    a.activation(dst[:, k * n:(k + 1) * n], src[:, k, :], ACT.Copy).then_inc(s("m_hi"), 1)

            def next_high(n):
                q = TURN[n] + DSET
                if q < len(HALVED) and RUN[HALVED[q]] == RUN[n]:
                    dense_high(a, HALVED[q])

            def root(i, n):
                a.wait_ge(s("norm_ss"), i + 1)
                a.activation(rt[:, 0:n], bank(0)[:, 0:n], ACT.Sqrt, bias=epsc[:, 0:1], scale=1.0 / D).then_inc(s("norm_rt"), 1)

            for k in range(KD):
                a.wait_ge(s("mem_loaded"), 16)
                a.activation(sq[:, k * NM:(k + 1) * NM], memT[:, k, :], ACT.Square).then_inc(s("norm_sq"), 1)
            dense_high(a, 0)
            root(0, NM)
            high(memh[0], memn[0], NM, range(KD), lambda k: a.wait_ge(s("norm_u"), k + 1))
            dense_high(a, 1)
            high(memh[1], memn[1], NM, range(KD), lambda k: a.wait_ge(s("norm_u"), KD + k + 1))

            for g in range(16):
                l, i = g // 8, g % 8
                a.wait_ge(s("mkv_mm"), g + 1)
                if i < 4:
                    a.activation(mk[l][:, i * NM:(i + 1) * NM], bank(i)[:, 0:NM], ACT.Copy).then_inc(s("mem_kv"), 1)
                else:
                    half, x = (i - 4) // 2, i % 2
                    a.activation(mv[l][:, x * 512 + half * 256:x * 512 + half * 256 + 256], bank(i)[:, 0:256], ACT.Copy)\
                        .then_inc(s("mem_kv"), 1)
                if g == 3:
                    for k in range(KD):
                        a.wait_ge(s("x_loaded"), 16)
                        a.activation(sq[:, k * T:(k + 1) * T], h[:, k, :], ACT.Square).then_inc(s("norm_sq"), 1)
                if g == 5:
                    a.wait_ge(s("norm_rs"), 1)
                    root(1, T)
                if g == 9:
                    high(uh[0], u, T, range(KD), lambda k: a.wait_ge(s("norm_u"), 2 * KD + k + 1))
                if i % 2:
                    next_high(g // 2)

            a.wait_ge(s("ba_mm"), 1)
            a.wait_ge(s("gba_zero"), 1)
            a.activation(gba[:, 0:2, :], bank(1)[:, 0:32].rearrange("p (t c) -> p t c", t=2), ACT.Copy).then_inc(s("gba_out"), 1)
            a.activation(gba[0:NS, 2, :], bank(1)[0:NS, 32:48], ACT.Copy).then_inc(s("gba_out"), 1)
            a.wait_ge(s("gba_out"), 2)
            a.activation(gb, gba[:, :, 0:8], ACT.Exp, scale=-1.0).then_inc(s("gate_exp"), 1)
            a.activation(gea, gains[:, GALOG:GALOG + H], ACT.Exp).then_inc(s("gate_exp"), 1)
            a.wait_ge(s("gate_ax"), 1)
            link(a.activation(ge, gax, ACT.Exp, scale=-1.0))
            a.activation(gl, ge, ACT.Ln, bias=ones[:, 0:1]).then_inc(s("gate_exp"), 1)

            a.wait_ge(s("convbuf_loaded"), 16)
            smp = pre[:, :, CW - 1 + SEQ:PRE].rearrange("p m (b j) -> p m b j", j=CW)
            for b in range(NS):
                cb = convio[:, 0:576].rearrange("p (m b j) -> p m b j", m=CT, b=NS)
                a.activation(smp[:, :, b, 0:CW - 1], cb[:, :, b, :], ACT.Copy).then_inc(s("conv_rows"), 1)

            def silu_of(m):
                a.wait_ge(s("conv_done"), m + 1)
                a.activation(act[:, m, :], act[:, m, :], ACT.Silu).then_inc(s("conv_silu"), 1)

            for t in range(36):
                a.wait_ge(s("ain_mm"), t + 1)
                if t % 2:
                    next_high(AT["a_in", t // 2])
                src = bank(t % 8)
                if t < CT:
                    a.activation(pre[:, t, CW - 1:CW - 1 + SEQ], src[:, 0:SEQ], ACT.Copy)
                    a.activation(smp[:, t, :, CW - 1], src[:, SEQ:T], ACT.Copy).then_inc(s("ain_out"), 1)
                elif t < 32:
                    a.activation(z[:, t - CT, :], src[:, 0:T], ACT.Silu).then_inc(s("ain_out"), 1)
                else:
                    a.activation(cq[:, t - 32, :], src[:, 0:T], ACT.Copy).then_inc(s("ain_out"), 1)
                if 8 <= t < 32:
                    silu_of(t - 8)
                if 0 <= t - 9 < 2 * H:
                    a.wait_ge(s("conv_silu"), t - 8)
                    a.activation(sqq[:, (t - 9) * ACTW:(t - 8) * ACTW], act[:, t - 9, :], ACT.Square).then_inc(s("l2_sq"), 1)

            a.wait_ge(s("l2_mm"), 1)
            a.activation(l2root[0:2 * H, :], bank(4)[0:2 * H, 0:ACTW], ACT.Sqrt, bias=epsc[0:2 * H, 0:1]).then_inc(s("head_rt"), 1)

            a.wait_ge(s("coef_dif"), 1)
            for dst, src in ((ceG, cG), (ctail, cdl), (ceGl, cgt[:, 0:16]), (sgb[:, 0:64], sgt[:, 0:64])):
                a.activation(dst, src, ACT.Exp).then_inc(s("coef_exp"), 1)

            def attention(l, between=lambda: None):
                Pr = Pr_of[l]
                a.wait_ge(s("diag_zero"), 1)
                a.wait_ge(s("bin_out" if l else "ain_out"), 12 if l else 36)
                a.activation(q_diag[:, 0:BH * BH:BH + 1].rearrange("p (b x) -> p b x", x=XH),
                             cq[:, :, SEQ:T].rearrange("p x b -> p b x"), ACT.Copy).then_inc(s("sat_in"), 1)
                for t in range(2):
                    a.wait_ge(s("att_max"), 3 * l + t + 1)
                    for x in range(XH):
                        a.activation(Pr[:, t * 1024 + x * NM:t * 1024 + (x + 1) * NM], PP[t][:, x * NM:(x + 1) * NM], ACT.Exp,
                                     bias=anm[:, t * 4 + x:t * 4 + x + 1], scale=P ** -0.5,
                                     accum_out=asum[:, t * 4 + x:t * 4 + x + 1]).then_inc(s("att_exp"), 1)
                between()
                v = PrT.rearrange("p (n t c) -> p n t c", t=2, c=P)
                for t in range(2):
                    a.wait_ge(s("att_tr"), 3 * l + t + 1)
                    a.activation(v[:, :, t, :], PP[2 + t][:, :].rearrange("p (n c) -> p n c", c=P), ACT.Copy).then_inc(s("att_pt"), 1)
                a.wait_ge(s("att_o"), 2 * l + 1)
                a.activation(cat[:, H:H + XH, 0:SEQ], PP[0][:, :].rearrange("p (m c) -> p m c", m=XH), ACT.Copy).then_inc(s("att_cat"), 1)
                a.wait_ge(s("att_max"), 3 * l + 3)
                a.activation(P32[0:BH, :], bank(1)[0:BH, 0:NM], ACT.Exp, bias=anm[0:BH, 0:1], scale=P ** -0.5,
                             accum_out=asum[0:BH, 0:1]).then_inc(s("att_exp"), 1)
                a.wait_ge(s("att_tr"), 3 * l + 3)
                a.wait_ge(s("diag_zero"), 2 * l + 2)
                a.activation(p_diag.rearrange("p (m f) -> p m f", m=MT)[:, :, 0:BH * BH:BH + 1],
                             bank(2)[:, 0:MT * BH].rearrange("p (m n) -> p m n", m=MT), ACT.Copy).then_inc(s("sat_in"), 1)
                a.wait_ge(s("cache_mm"), 8 * l + 8)
                a.activation(O32[0:BH, :], bank(3)[0:BH, 0:P], ACT.Copy).then_inc(s("sat_in"), 1)
                a.wait_ge(s("att_o"), 2 * l + 2)
                a.activation(cat[:, H:H + XH, SEQ:T].rearrange("p x b -> p b x"),
                             bank(0)[:, 0:BH].rearrange("p (b x) -> p b x", x=XH), ACT.Copy).then_inc(s("att_cat"), 1)

            attention(0)

            for c in range(NCH):
                a.wait_ge(s("dl_neg"), c + 1)
                for x in range(H):
                    a.activation(DTb[:, x * P:(x + 1) * P], MLb[:, x * P:(x + 1) * P], ACT.Exp,
                                 bias=cnG[:, c * H + x:c * H + x + 1]).then_inc(s("dl_dt"), 1)
                a.activation(Xb, PP[0][:, :], ACT.Exp).then_inc(s("dl_eg"), 1)
                for lv in range(1, NLVL + 1):
                    if lv < NLVL:
                        for g in range(2):
                            a.wait_ge(s("dl_tt"), (c * (NLVL - 1) + lv - 1) * 2 + g + 1)
                            a.activation(Tb[:, g * 512:(g + 1) * 512], bank(g), ACT.Copy).then_inc(s("dl_t"), 1)
                        for g in range(2):
                            a.wait_ge(s("dl_xx"), (c * (NLVL - 1) + lv - 1) * 2 + g + 1)
                            a.activation(Xb[:, g * 512:(g + 1) * 512], bank(2 + g), ACT.Copy).then_inc(s("dl_x"), 1)
                a.wait_ge(s("dl_uu"), c + 1)
                a.activation(Tb, PP[1][:, :], ACT.Copy).then_inc(s("dl_u"), 1)
                a.wait_ge(s("dl_o"), c + 1)
                a.activation(cat[:, 0:H, c * P:(c + 1) * P], PP[2][:, :].rearrange("p (m c) -> p m c", m=H), ACT.Copy)\
                    .then_inc(s("dl_cat"), 1)

            a.wait_ge(s("sd_mm"), 1)
            a.activation(kqrow[0:32, :], bank(0)[0:32, :], ACT.Copy).then_inc(s("sd_row"), 1)
            a.wait_ge(s("sd_rows"), 1)
            a.activation(krow[0:DBH, :], bank(4)[0:DBH, 0:P], ACT.Copy).then_inc(s("sd_row"), 1)
            a.wait_ge(s("sd_rows"), 2)
            a.activation(urow[0:DBH, :], bank(5)[0:DBH, 0:P], ACT.Copy).then_inc(s("sd_row"), 1)

            a.wait_ge(s("dl_cat"), NCH)
            a.wait_ge(s("sd_cat"), 1)
            for x in range(H):
                a.activation(sq[:, x * T:(x + 1) * T], cat[:, x, :], ACT.Square).then_inc(s("on_sq"), 1)
            a.wait_ge(s("on_mm"), 1)
            a.activation(rt[0:H, :], bank(0)[0:H, 0:T], ACT.Sqrt, bias=epsc[0:H, 0:1], scale=1.0 / P).then_inc(s("head_rt"), 1)
            a.wait_ge(s("att_cat"), 2)
            high(cath[0], cat, T, range(H, H + XH), lambda k: None)
            a.wait_ge(s("state_stored0"), 32)
            dense_high(a, AT["a_out", 0])
            high(cath[0], cat, T, range(H), lambda k: a.wait_ge(s("on_done"), k + 1))
            a.wait_ge(s("state_stored1"), 32)
            dense_high(a, AT["a_out", 1])

            def residual_norm(i, name, last):
                for t in range(KD + 1):
                    if t < KD:
                        for n in last(t):
                            next_high(n)
                    if t:
                        a.wait_ge(s(f"{name}_h"), t)
                        a.activation(sq[:, (t - 1) * T:t * T], h[:, t - 1, :], ACT.Square).then_inc(s("norm_sq"), 1)
                a.wait_ge(s("norm_ss"), i + 1)
                a.activation(rt[:, 0:T], bank(0)[:, 0:T], ACT.Sqrt, bias=epsc[:, 0:1], scale=1.0 / D).then_inc(s("norm_rt"), 1)

            residual_norm(2, "aout", lambda t: [AT["a_out", t]])
            high(uh[1], u, T, range(KD), lambda k: a.wait_ge(s("norm_u"), 3 * KD + k + 1))
            for f in range(FT):
                a.wait_ge(s("wi_mm"), f + 1)
                if f >= 2:
                    a.wait_ge(s("wi_prod"), f - 1)
                a.activation(sil[f % 2], bank(2 * (f % 4))[:, 0:T], ACT.Silu).then_inc(s("wi_sil"), 1)
                next_high(AT["wi", f])
                a.wait_ge(s("wi_prod"), f + 1)
                a.activation(hidh[:, f * T:(f + 1) * T], hidf[f % 2], ACT.Copy).then_inc(s("hid_hi"), 1)
            residual_norm(3, "wo", lambda t: [AT["wo", 2 * t], AT["wo", 2 * t + 1]])
            high(uh[2], u, T, range(KD), lambda k: a.wait_ge(s("norm_u"), 4 * KD + k + 1))

            psm_in = pin[:, :, PW + SEQ:PCOL].rearrange("p m (b j) -> p m b j", j=PW + 1)
            a.wait_ge(s("norm_u"), 40)
            a.wait_ge(s("pin_zero"), 1)
            a.wait_ge(s("poolbuf_loaded"), 16)
            a.wait_ge(s("pin_zero"), 2)
            for t in range(12):
                a.wait_ge(s("bin_mm"), t + 1)
                if t % 2:
                    next_high(AT["b_in", t // 2])
                if t < 8:
                    a.activation(pin[:, t, PW:PW + SEQ], bank(t % 8)[:, 0:SEQ], ACT.Copy)
                    a.activation(psm_in[:, t, :, PW], bank(t % 8)[:, SEQ:T], ACT.Copy).then_inc(s("bin_out"), 1)
                else:
                    a.activation(cq[:, t - 8, :], bank(t % 8)[:, 0:T], ACT.Copy).then_inc(s("bin_out"), 1)
            def pooled():
                a.wait_ge(s("pm_mm"), 8)
                for t in range(8):
                    a.activation(cat[:, t, :], bank(t)[:, 0:T], ACT.Copy, scale=gains[:, GPS + t:GPS + t + 1])\
                        .then_inc(s("pm_cat"), 1)

            attention(1, pooled)
            a.wait_ge(s("pm_cat"), 8)
            a.wait_ge(s("att_cat"), 4)
            a.wait_ge(s("outputs_stored"), 32)
            high(cath[1], cat, T, range(12), lambda k: None)
            for i in range(DSET):
                dense_high(a, AT["b_out", i])
            for t in range(KD - DSET):
                next_high(AT["b_out", t])
            norm(4, h, T, lambda k: a.wait_ge(s("bout_h"), k + 1), 1.0 / D, sqb=fsq, rtb=frt)

            a.wait_ge(s("outputs_stored"), 32)
            def halve(c, st, again=0):
                a.wait_ge(raw_loaded[c % XRAW], st * (16 * PERX // XRAW) + (16 * (PERX // XRAW * again + c // XRAW + 1)))
                q = c + PERX * again - XSET
                if q >= 0:
                    name, n = ("up_mm", NUP) if q < NUP else ("down_mm", NDOWN)
                    a.wait_ge(s(name), st * n + ((q if q < NUP else q - NUP) + 1))
                a.activation(whi[c % XSET][:, :], raw_of(c), ACT.Copy).then_inc(s("w_hi"), 1)

            a.wait_ge(s("bout_mm"), KD)
            for c in range(XSET):
                halve(c, 0)
            a.wait_ge(s("rt_mm"), 1)
            a.wait_ge(s("rout_zero"), 1)
            a.activation(rout[:, 0:16], bank(0)[:, 0:16], ACT.Copy).then_inc(s("rt_out"), 1)
            a.activation(rout[0:NS, 16:24], bank(0)[0:NS, 16:24], ACT.Copy).then_inc(s("rt_out"), 1)
            for t in range(3):
                n = P if t < 2 else NS
                a.wait_ge(s("xt_mm"), t + 1)
                a.activation(xtok[0:n, t, :], PP[1 + t][0:n, :], ACT.Copy).then_inc(s("xt_out"), 1)
            a.wait_ge(s("rt_sub"), 1)
            a.activation(rr[1], rr[1], ACT.Exp).then_inc(s("rt_exp"), 1)

            def slots():
                a.activation(xsh[:, :], PP[1][:, :], ACT.Copy).then_inc(s("xs_hi"), 1)

            a.wait_ge(s("gat_mm"), 1)
            slots()

            a.wait_ge(s("steps_known"), 1)
            n_rounds = a.value_load(nsteps_i[0:1, 0:1], min_val=1, max_val=ROUNDS)
            with a.Fori(0, n_rounds * E) as st:
                for c in range(XSET, PERX):
                    halve(c, st)
                    if c % 4 == 0 and c // 4 - 1 < FCN:
                        f = c // 4 - 1
                        a.wait_ge(s("up_mm"), st * NUP + (4 * f + 2))
                        if f >= 2:
                            a.wait_ge(s("up_h"), st * FCN + (f - 1))
                        a.activation(esil[f % 2], bank(2 * (f % 2))[:, :], ACT.Silu).then_inc(s("up_sil"), 1)
                    if c in TURNED:
                        f = TURNED[c]
                        a.wait_ge(s("ht_mm"), st * FCN + (f + 1))
                        a.activation(hTh[:, 4 * f * C:4 * (f + 1) * C], bank(4 + f % 2), ACT.Copy).then_inc(s("ht_hi"), 1)
                    if c == NUP + 3:
                        a.wait_ge(s("gat_mm"), st + 2)
                        slots()
                halve(0, st, 1)
                halve(1, st, 1)
                a.wait_ge(s("down_mm"), st * NDOWN + NDOWN)
                a.activation(yslot, PP[3][:, :], ACT.Copy).then_inc(s("y_out"), 1)
                halve(2, st, 1)

            a.wait_ge(s("comb_h"), n_rounds * E * KD + KD)
            norm(5, h, T, lambda k: None, 1.0 / D, sqb=fsq, rtb=frt)

        @block.vector
        def _(v):
            own = [0]

            def link(ins_):
                own[0] += 1
                ins_.then_inc(s("dve_own"), 1)
                v.wait_ge(s("dve_own"), own[0])

            m_lo = [0]

            def low(dst, high_, src, n, k):
                m_lo[0] += 1
                v.wait_ge(s("m_hi"), m_lo[0])
                v.tensor_tensor(dst[:, k * n:(k + 1) * n], src[:, k, :], high_[:, k * n:(k + 1) * n].bitcast(F32), ALU.subtract)\
                    .then_inc(s("m_lo"), 1)

            def next_low(n):
                q = TURN[n] + DSET
                if q < len(HALVED) and RUN[HALVED[q]] == RUN[n]:
                    dense_low(v, HALVED[q])

            def norm(i, src, n, dsts, rtb=None, rsb=None, halves_=None):
                rtb = rt if rtb is None else rtb
                rsb = rs if rsb is None else rsb
                v.wait_ge(s("norm_rt"), i + 1)
                if i:
                    v.wait_ge(s("norm_u"), (i + 1) * KD)
                v.reciprocal(rsb[:, 0:n], rtb[:, 0:n]).then_inc(s("norm_rs"), 1)
                v.wait_ge(s("norm_rs"), i + 1)
                for dst, g in dsts:
                    for k in range(KD + 2):
                        if k < KD:
                            v.scalar_tensor_tensor(out=dst[:, k, :], in0=src[:, k, :], scalar=gains[:, g + k:g + k + 1],
                                                   in1=rsb[:, 0:n], op0=ALU.mult, op1=ALU.mult).then_inc(s("norm_u"), 1)
                        if k >= 2 and halves_:
                            low(halves_[1], halves_[0], dst, n, k - 2)

            v.memset(gba, 0.0).then_inc(s("gba_zero"), 1)
            v.wait_ge(s("gains_loaded"), 16)
            v.wait_ge(s("mem_loaded"), 16)
            dense_low(v, 0)
            norm(0, memT, NM, [(memn[0], GM0)])
            for k in range(KD):
                low(meml[0], memh[0], memn[0], NM, k)
            dense_low(v, 1)
            for k in range(KD):
                v.scalar_tensor_tensor(out=memn[1][:, k, :], in0=memT[:, k, :], scalar=gains[:, GM1 + k:GM1 + k + 1],
                                       in1=rs[:, 0:NM], op0=ALU.mult, op1=ALU.mult).then_inc(s("norm_u"), 1)
            for k in range(KD):
                low(meml[1], memh[1], memn[1], NM, k)
            for i in range(8):
                if i == 3:
                    v.wait_ge(s("consts_loaded"), 48)
                    v.wait_ge(s("x_loaded"), 16)
                    norm(1, h, T, [(u, GA1)])
                if i == 5:
                    for k in range(KD):
                        low(ul[0], uh[0], u, T, k)
                next_low(i)

            v.wait_ge(s("gba_out"), 2)
            dt_b = gains[:, GDT:GDT + H].unsqueeze(1).to_broadcast([P, 3, H])
            link(v.tensor_tensor(gx, gba[:, :, 8:16], dt_b, ALU.add))
            v.scalar_tensor_tensor(out=gax, in0=gx, scalar=-1.0, in1=gx, op0=ALU.mult, op1=ALU.max).then_inc(s("gate_ax"), 1)
            v.wait_ge(s("gate_exp"), 1)
            link(v.tensor_scalar(gb, gb, 1.0, None, ALU.add))
            link(v.reciprocal(gb, gb))
            v.wait_ge(s("gate_exp"), 3)
            link(v.scalar_tensor_tensor(out=gl, in0=gx, scalar=0.0, in1=gl, op0=ALU.max, op1=ALU.add))
            v.wait_ge(s("gate_exp"), 2)
            link(v.scalar_tensor_tensor(out=gg, in0=gl, scalar=-1.0, in1=gea.unsqueeze(1).to_broadcast([P, 3, H]),
                                        op0=ALU.mult, op1=ALU.mult))
            dg8 = ident[0:NS, 0:NS].unsqueeze(2).to_broadcast([NS, NS, H])
            for i, val in enumerate((gg, gb)):
                v.tensor_tensor(gd[0:NS, 64 * i:64 * i + 64].rearrange("p (b x) -> p b x", x=H),
                                val[0:NS, 2, :].unsqueeze(1).to_broadcast([NS, NS, H]), dg8, ALU.mult)\
                    .then_inc(s("gate_done"), 1)

            v.wait_ge(s("mkv_mm"), 16)
            v.memset(pre[:, :, 0:CW - 1], 0.0).then_inc(s("pre_zero"), 1)
            v.wait_ge(s("conv_rows"), NS)
            v.wait_ge(s("pre_zero"), 1)
            for c in range(18):
                next_low(AT["a_in", c])
                g = c - 1
                if not 0 <= g < CT // 2:
                    continue
                v.wait_ge(s("ain_out"), 2 * g + 2)
                for j in range(CW):
                    for m in range(2 * g, 2 * g + 2):
                        tap = gains[:, GTAP + m * CW + j:GTAP + m * CW + j + 1]
                        if j:
                            v.wait_ge(s("conv_tap"), 6 * g + 2 * (j - 1) + m - 2 * g + 1)
                        ins_ = v.tensor_scalar(act[:, m, :], pre[:, m, 0:ACTW], tap, None, ALU.mult) if j == 0 else \
                            v.scalar_tensor_tensor(out=act[:, m, :], in0=pre[:, m, j:j + ACTW], scalar=tap,
                                                   in1=act[:, m, :], op0=ALU.mult, op1=ALU.add)
                        ins_.then_inc(s("conv_tap") if j < CW - 1 else s("conv_done"), 1)
            cio = convio.rearrange("p (m c) -> p m c", m=CT)
            smp = pre[:, :, CW - 1 + SEQ:PRE].rearrange("p m (b j) -> p m b j", j=CW)
            v.tensor_copy(cio[:, :, 0:3], pre[:, :, SEQ:SEQ + 3]).then_inc(s("conv_state"), 1)
            for b in range(NS):
                ins_ = v.tensor_copy(cio[:, :, 3 + 3 * b:6 + 3 * b], smp[:, :, b, 1:CW])
            ins_.then_inc(s("conv_state"), 1)

            v.wait_ge(s("head_rt"), 1)
            v.reciprocal(l2inv[0:2 * H, :], l2root[0:2 * H, :]).then_inc(s("head_inv"), 1)

            def l2_scale():
                for x in range(2 * H):
                    v.wait_ge(s("l2_mm"), x + 2)
                    v.scalar_tensor_tensor(out=act[:, x, :], in0=act[:, x, :], scalar=P ** -0.5 if x < H else 1.0,
                                           in1=bank(4 + x % 4)[:, 0:ACTW], op0=ALU.mult, op1=ALU.mult).then_inc(s("l2_done"), 1)

            v.wait_ge(s("coef_mm"), 1)
            link(v.tensor_copy(cG, bank(5)[:, 0:16]))
            v.tensor_copy(cgt[:, 0:16], bank(5)[:, 16:32])
            link(v.tensor_copy(sgt, bank(5)[:, 32:160]))
            v.tensor_scalar(cnG, cG, -1.0, None, ALU.mult)
            v.tensor_copy(sgb[:, 64:128], sgt[:, 64:128])
            link(v.tensor_tensor(cdl, cgt[:, 0:16], cG, ALU.subtract))
            v.tensor_copy(cgt[:, 16:32], cG).then_inc(s("coef_dif"), 1)
            v.wait_ge(s("coef_exp"), 4)
            gbp = gb[:, 0:2, :].rearrange("p t c -> p (t c)")
            v.tensor_tensor(cbeG, ceG, gbp, ALU.mult).then_inc(s("coef_beg"), 1)

            def attention(l, between=lambda: None):
                Pr = Pr_of[l]
                for t in range(2):
                    v.wait_ge(s("att_mm"), 2 * l + t + 1)
                    link(v.reduce_max(amx[:, 4 * t:4 * t + 4], PP[t][:, :].rearrange("p (m c) -> p m c", m=XH), AX))
                    v.tensor_scalar(anm[:, 4 * t:4 * t + 4], amx[:, 4 * t:4 * t + 4], -(P ** -0.5), None, ALU.mult)\
                        .then_inc(s("att_max"), 1)
                between()
                for t in range(2):
                    v.wait_ge(s("att_exp"), 9 * l + 4 * t + 4)
                    link(v.reciprocal(ars[:, 4 * t:4 * t + 4], asum[:, 4 * t:4 * t + 4]))
                    pt = Pr[:, 1024 * t:1024 * (t + 1)].rearrange("p (m c) -> p m c", m=XH)
                    v.tensor_tensor(pt, pt, ars[:, 4 * t:4 * t + 4].unsqueeze(2).to_broadcast([P, XH, NM]), ALU.mult)\
                        .then_inc(s("att_p"), 1)
                v.wait_ge(s("cache_mm"), 8 * l + 4)
                link(v.reduce_max(amx[0:BH, 0:1], bank(1)[0:BH, 0:NM], AX))
                v.tensor_scalar(anm[0:BH, 0:1], amx[0:BH, 0:1], -(P ** -0.5), None, ALU.mult).then_inc(s("att_max"), 1)
                v.wait_ge(s("att_exp"), 9 * l + 9)
                link(v.reciprocal(ars[0:BH, 0:1], asum[0:BH, 0:1]))
                v.tensor_scalar(P32[0:BH, :], P32[0:BH, :], ars[0:BH, 0:1], None, ALU.mult).then_inc(s("att_p"), 1)

            attention(0, l2_scale)

            def per_head(c, coef):
                return coef[:, c * H:(c + 1) * H].unsqueeze(2).to_broadcast([P, H, P])

            def heads(b):
                return b.rearrange("p (m c) -> p m c", m=H)

            for c in range(NCH):
                cols = slice(c * P, (c + 1) * P)
                v.wait_ge(s("conv_state"), 2)
                v.wait_ge(s("dl_grow"), c + 1)
                v.tensor_tensor(heads(MLb), heads(PP[0][:, :]), neg.unsqueeze(1).to_broadcast([P, H, P]), ALU.add)\
                    .then_inc(s("dl_neg"), 1)
                v.wait_ge(s("dl_dt"), H * (c + 1))
                v.wait_ge(s("dl_kk"), 2 * c + 1)
                v.tensor_tensor(PTb, PP[1][:, :], DTb, ALU.mult).then_inc(s("dl_pt"), 1)
                v.wait_ge(s("dl_kk"), 2 * c + 2)
                link(v.tensor_tensor(MTb, PP[2][:, :], DTb, ALU.mult))
                v.wait_ge(s("dl_brow"), c + 1)
                link(v.tensor_tensor(MTb, MTb, PP[3][:, :], ALU.mult))
                v.wait_ge(s("dl_eg"), c + 1)
                v.tensor_tensor(act[:, 0:H, cols], act[:, 0:H, cols], heads(Xb), ALU.mult).then_inc(s("dl_qd"), 1)
                v.wait_ge(s("dl_tok"), 2 * c + 1)
                v.tensor_tensor(heads(vtok), heads(PP[1][:, :]), per_head(c, gbp), ALU.mult).then_inc(s("dl_v"), 1)
                v.wait_ge(s("dl_tok"), 2 * c + 2)
                v.tensor_tensor(heads(ktail), heads(PP[2][:, :]), per_head(c, ctail), ALU.mult).then_inc(s("dl_kt"), 1)

                for lv in range(NLVL):
                    mask = consts[:, CLVL + lv * P:CLVL + (lv + 1) * P].unsqueeze(1).to_broadcast([P, H, P])
                    if lv >= 2:
                        v.wait_ge(s("dl_xx"), (c * (NLVL - 1) + lv - 1) * 2)
                    if lv:
                        v.wait_ge(s("dl_um"), 2 * (c * NLVL + lv))
                    v.tensor_tensor(heads(MLb), heads(MTb), mask, ALU.mult).then_inc(s("dl_ml"), 1)
                    if lv == 0:
                        v.wait_ge(s("dl_ml"), c * NLVL + 1)
                        for g in range(2):
                            v.tensor_tensor(heads(Ub)[:, 4 * g:4 * g + 4, :], ident.unsqueeze(1).to_broadcast([P, 4, P]),
                                            heads(MLb)[:, 4 * g:4 * g + 4, :], ALU.subtract).then_inc(s("dl_um"), 1)
                        continue
                    for g in range(2):
                        v.wait_ge(s("dl_du"), (c * (NLVL - 1) + lv - 1) * 2 + g + 1)
                        v.tensor_tensor(Ub[:, g * 512:(g + 1) * 512], Ub[:, g * 512:(g + 1) * 512], bank(4 + g), ALU.subtract)\
                            .then_inc(s("dl_um"), 1)
                if c:
                    v.wait_ge(s("dl_ks"), 1)
                    link(v.tensor_tensor(heads(Xb), heads(PP[0][:, :]), per_head(c, cbeG), ALU.mult))
                    v.tensor_tensor(Xb, vtok, Xb, ALU.subtract).then_inc(s("dl_r"), 1)
                v.wait_ge(s("dl_ds"), c + 1)
                if c == 0:
                    v.tensor_copy(Sb, PP[3][:, :]).then_inc(s("S_done"), 1)
                else:
                    v.wait_ge(s("S_done"), 1)
                    v.wait_ge(s("dl_o"), c + 1)
                    link(v.tensor_tensor(heads(Sb), heads(Sb), per_head(c, ceGl), ALU.mult))
                    v.tensor_tensor(Sb, Sb, PP[3][:, :], ALU.add).then_inc(s("S_done"), 1)

            def cols64(m0):
                return act[:, m0:m0 + H, S0:S0 + CW * (NS - 1) + 1:CW].rearrange("p x b -> p b x")

            def as_bx(b):
                return b.rearrange("p (b x) -> p b x", x=H)

            v.wait_ge(s("dl_ds"), NCH)
            v.tensor_copy(kq[:, :, 0].rearrange("p (b x) -> p b x", x=H), cols64(8))
            v.tensor_copy(kq[:, :, 1].rearrange("p (b x) -> p b x", x=H), cols64(0))
            link(v.tensor_copy(as_bx(v64), cols64(16)))
            v.wait_ge(s("diag_zero"), 3)
            for c in range(2):
                v.tensor_copy(kq_diag.rearrange("p (g f) -> p g f", g=4)[:, :, c:512:34],
                              kq[:, :, c].rearrange("p (g j) -> p g j", g=4))
            link(v.tensor_copy(t64, kq[:, :, 0]))
            v.tensor_tensor(kqd, t64, kq[:, :, 1], ALU.mult).then_inc(s("sd_cols"), 1)
            v.wait_ge(s("sd_mm"), 2)
            rk = bank(2)[:, 0:128].rearrange("p (n c) -> p n c", c=2)
            egs, bs = sgb[:, 0:64], sgb[:, 64:128]
            v.wait_ge(s("sd_rows"), 1)
            link(v.tensor_tensor(t64, rk[:, :, 0], egs, ALU.mult))
            link(v.tensor_tensor(u64, v64, t64, ALU.subtract))
            link(v.tensor_tensor(u64, u64, bs, ALU.mult))
            v.tensor_tensor(qku, rk[:, :, 1], egs, ALU.mult).then_inc(s("sd_u"), 1)
            v.wait_ge(s("sd_u"), 1)
            link(v.tensor_tensor(t64, bank(1)[:, 0:64], u64, ALU.mult))
            v.tensor_tensor(cat[:, 0:H, SEQ:T].rearrange("p x b -> p b x"), as_bx(t64), as_bx(qku), ALU.add)\
                .then_inc(s("sd_cat"), 1)
            v.wait_ge(s("sd_row"), 3)
            for g in range(16):
                if g >= 2:
                    v.wait_ge(s("sd_outer"), g - 1)
                v.tensor_tensor(ublk[g % 2][0:DBH, :].rearrange("p (n c) -> p n c", c=P),
                                urow[0:DBH, :].unsqueeze(1).to_broadcast([DBH, 4, P]),
                                ident[0:DBH, 4 * g:4 * g + 4].unsqueeze(2).to_broadcast([DBH, 4, P]), ALU.mult)\
                    .then_inc(s("sd_blk"), 1)
                if g >= 1:
                    new_state(v, g - 1)
                if g == 2:
                    v.wait_ge(s("head_rt"), 2)
                    v.reciprocal(rs[0:H, :], rt[0:H, :]).then_inc(s("head_inv"), 1)
                if g < H:
                    v.wait_ge(s("on_sq"), g + 1)
                    v.scalar_tensor_tensor(out=cat[:, g, :], in0=z[:, g, :], scalar=gains[:, GON:GON + 1], in1=cat[:, g, :],
                                           op0=ALU.mult, op1=ALU.mult).then_inc(s("on_z"), 1)
                x = g - 5
                if 0 <= x < H:
                    v.wait_ge(s("on_z"), x + 1)
                    v.wait_ge(s("on_mm"), x + 2)
                    v.tensor_tensor(cat[:, x, :], cat[:, x, :], bank(4 + x % 4)[:, 0:T], ALU.mult).then_inc(s("on_done"), 1)
            new_state(v, 15)
            dense_low(v, AT["a_out", 0])
            v.wait_ge(s("S_stored"), 16)
            for k in range(H, H + XH):
                low(catl[0], cath[0], cat, T, k)
            for k in range(H):
                low(catl[0], cath[0], cat, T, k)
            dense_low(v, AT["a_out", 1])

            def residual(name, chunks):
                for t in range(KD):
                    for n in range(chunks * t, chunks * (t + 1) - 1):
                        next_low(AT[CHUNKS[name], n])
                    v.wait_ge(s(f"{name}_mm"), chunks * (t + 1))
                    v.tensor_tensor(h[:, t, :], h[:, t, :], bank(t)[:, 0:T], ALU.add).then_inc(s(f"{name}_h"), 1)
                    next_low(AT[CHUNKS[name], chunks * (t + 1) - 1])

            residual("aout", 1)
            norm(2, h, T, [(u, GA2)], halves_=(uh[1], ul[1]))
            for f in range(FT):
                v.wait_ge(s("wi_sil"), f + 1)
                if f >= 2:
                    v.wait_ge(s("hid_hi"), f - 1)
                    v.wait_ge(s("hid_lo"), f - 1)
                v.tensor_tensor(hidf[f % 2], sil[f % 2], bank(2 * (f % 4) + 1)[:, 0:T], ALU.mult).then_inc(s("wi_prod"), 1)
                next_low(AT["wi", f])
                v.wait_ge(s("hid_hi"), f + 1)
                sl = slice(f * T, (f + 1) * T)
                v.tensor_tensor(hidl[:, sl], hidf[f % 2], hidh[:, sl].bitcast(F32), ALU.subtract).then_inc(s("hid_lo"), 1)
            residual("wo", 2)
            norm(3, h, T, [(u, GB1)], halves_=(uh[2], ul[2]))

            v.wait_ge(s("norm_u"), 40)
            v.memset(pin[:, :, 0:PW], 0.0).then_inc(s("pin_zero"), 1)
            v.wait_ge(s("poolbuf_loaded"), 16)
            psv = pin[:, :, PW + SEQ:PCOL].rearrange("p m (b j) -> p m b j", j=PW + 1)
            pbv = poolbuf.rearrange("p (m b j) -> p m b j", m=KD, b=NS)
            for b in range(NS):
                ins_ = v.tensor_copy(psv[:, :, b, 0:PW], pbv[:, :, b, :])
            ins_.then_inc(s("pin_zero"), 1)
            for i in range(6):
                next_low(AT["b_in", i])
            v.wait_ge(s("bin_out"), 8)
            v.wait_ge(s("pin_zero"), 2)
            pstv = pst.rearrange("p (m c) -> p m c", m=KD)
            v.tensor_copy(pstv[:, :, 0:PW], pin[:, :, SEQ:SEQ + PW]).then_inc(s("pool_state"), 1)
            for b in range(NS):
                ins_ = v.tensor_copy(pstv[:, :, PW + PW * b:PW + PW * (b + 1)], psv[:, :, b, 1:PW + 1])
            ins_.then_inc(s("pool_state"), 1)
            v.tensor_copy(u[:, :, 0:SEQ], pin[:, :, PW:PW + SEQ])
            link(v.tensor_copy(u[:, :, SEQ:T], psv[:, :, :, PW]))
            link(v.tensor_tensor(psm[:, :, 1:], pin[:, :, 1:], pin[:, :, 0:PCOL - 1], ALU.add))
            v.wait_ge(s("bin_mm"), 12)

            def pooling():
                for g in range(4):
                    w = 2 << g
                    m0 = 2 * g
                    sh = w // 2
                    if g % 2 == 0:
                        dst, frm = psm, pin
                    else:
                        dst, frm = pin, psm
                    lo = 2 * sh - 1
                    if g:
                        link(v.tensor_tensor(dst[:, m0:, lo:], frm[:, m0:, lo:], frm[:, m0:, lo - sh:PCOL - sh], ALU.add))
                    v.scalar_tensor_tensor(out=pd[:, m0:m0 + 2, 0:SEQ], in0=dst[:, m0:m0 + 2, PW:PW + SEQ], scalar=1.0 / w,
                                           in1=u[:, m0:m0 + 2, 0:SEQ], op0=ALU.mult, op1=ALU.subtract)
                    dsv = dst[:, :, PW + SEQ:PCOL].rearrange("p m (b j) -> p m b j", j=PW + 1)
                    link(v.scalar_tensor_tensor(out=pd[:, m0:m0 + 2, SEQ:T], in0=dsv[:, m0:m0 + 2, :, PW], scalar=1.0 / w,
                                                in1=u[:, m0:m0 + 2, SEQ:T], op0=ALU.mult, op1=ALU.subtract))
                    inv = consts[:, CINV + 16 * g:CINV + 16 * g + 16].unsqueeze(1).to_broadcast([P, 2, 16])
                    fx = pfix[:, 0:32].rearrange("p (m c) -> p m c", m=2)
                    link(v.tensor_tensor(fx, dst[:, m0:m0 + 2, PW:PW + 16], inv, ALU.mult))
                    ins_ = v.tensor_tensor(pd[:, m0:m0 + 2, 0:16], fx, u[:, m0:m0 + 2, 0:16], ALU.subtract)
                    ins_.then_inc(s("pool_d"), 1)
                    v.wait_ge(s("pool_d"), g + 1)

            attention(1, pooling)
            for k in range(12):
                low(catl[1], cath[1], cat, T, k)
            for i in range(DSET):
                dense_low(v, AT["b_out", i])
            residual("bout", 1)
            norm(4, h, T, [(u, GB2)], rtb=frt, rsb=frs)

            def halve(c, want):
                v.wait_ge(s("w_hi"), want)
                v.tensor_tensor(wlo[c % XSET][:, :], raw_of(c), whi[c % XSET][:, :].bitcast(F32), ALU.subtract)\
                    .then_inc(s("w_lo"), 1)

            v.memset(rout, 0.0).then_inc(s("rout_zero"), 1)
            for c in range(XSET):
                halve(c, c + 1)
            v.wait_ge(s("rt_out"), 2)
            lg = rout.rearrange("p (t e) -> p t e", t=3)
            rank, sel, gat, mx, pos = rr[0], rr[2], rr[3], rr[4], rr[5]
            mine = lg.unsqueeze(3).to_broadcast([P, 3, E, E])
            other = lg.unsqueeze(2).to_broadcast([P, 3, E, E])
            o1, o2 = (x.rearrange("p (t a b) -> p t a b", t=3, a=E) for x in (rtmp, rtm2))
            tie = consts[:, CTIE:CTIE + 64].rearrange("p (a b) -> p a b", a=E).unsqueeze(1).to_broadcast([P, 3, E, E])
            v.tensor_tensor(o1, other, mine, ALU.is_gt)
            link(v.tensor_tensor(o2, other, mine, ALU.is_equal))
            link(v.tensor_tensor(o2, o2, tie, ALU.mult))
            v.reduce_max(mx[:, 0:3], lg, AX)
            link(v.tensor_tensor(o1, o1, o2, ALU.add))
            link(v.reduce_sum(rank.rearrange("p (t e) -> p t e", t=3), o1, AX))
            v.tensor_tensor(rr[1].rearrange("p (t e) -> p t e", t=3), lg, mx[:, 0:3].unsqueeze(2).to_broadcast([P, 3, E]),
                            ALU.subtract)
            v.tensor_scalar(sel, rank, 1.5, None, ALU.is_lt).then_inc(s("rt_sub"), 1)
            v.wait_ge(s("rt_sub"), 1)
            v.wait_ge(s("rt_exp"), 1)
            link(v.tensor_tensor(gat, rr[1], sel, ALU.mult))
            link(v.reduce_sum(mx[:, 0:3], gat.rearrange("p (t e) -> p t e", t=3), AX))
            link(v.reciprocal(mx[:, 0:3], mx[:, 0:3]))
            link(v.tensor_tensor(gat.rearrange("p (t e) -> p t e", t=3), gat.rearrange("p (t e) -> p t e", t=3),
                                 mx[:, 0:3].unsqueeze(2).to_broadcast([P, 3, E]), ALU.mult))
            def dispatch(dst, at):
                for t in range(3):
                    n = P if t < 2 else NS
                    v.tensor_scalar(dst[0:n, t, :], iota[0:n, :], posx[0:n, at, t:t + 1] if isinstance(at, int) else
                                    posx[0:n, bass.ds(at, 1), t:t + 1].rearrange("p a b -> p (a b)"), None, ALU.is_equal)\
                        .then_inc(s("disp"), 1)

            v.wait_ge(s("pos_mm"), 1)
            link(v.tensor_copy(pos, bank(0)[:, 0:24]))
            link(v.tensor_copy(cnt8[:, 0:8], bank(0)[:, 24:32]))
            link(v.tensor_scalar(rr[6], sel, 1e4, -1e4, ALU.mult, ALU.add))
            link(v.tensor_tensor(pos, pos, rr[6], ALU.add))
            for r in range(ROUNDS + 1):
                ins_ = v.tensor_scalar(posx[:, r * E:(r + 1) * E, :].rearrange("p e t -> p t e"),
                                       pos.rearrange("p (t e) -> p t e", t=3), -float(r * C), None, ALU.add)
                if r == 0:
                    link(ins_)
                    dispatch(disp, 0)
                link(v.tensor_copy(gatex[:, r * E:(r + 1) * E, :].rearrange("p e t -> p t e"),
                                   gat.rearrange("p (t e) -> p t e", t=3)))
            link(v.reduce_max(cnt8[:, 8:9], cnt8[:, 0:8], AX))
            link(v.memset(cnt8[:, 9:10], 1.0))
            for r in range(1, ROUNDS):
                link(v.scalar_tensor_tensor(out=cnt8[:, 9:10], in0=cnt8[:, 8:9], scalar=float(r * C), in1=cnt8[:, 9:10],
                                            op0=ALU.is_gt, op1=ALU.add))
            v.tensor_copy(nsteps_i[:, :], cnt8[:, 9:10]).then_inc(s("steps_known"), 1)

            def slots(want):
                v.wait_ge(s("xs_hi"), want)
                v.tensor_tensor(xsl[:, :], PP[1][:, :], xsh[:, :].bitcast(F32), ALU.subtract).then_inc(s("xs_lo"), 1)

            v.memset(comb, 0.0).then_inc(s("comb_out"), 1)
            v.memset(yslot, 0.0).then_inc(s("y_out"), 1)
            slots(1)
            v.wait_ge(s("steps_known"), 1)
            n_rounds = v.value_load(nsteps_i[0:1, 0:1], min_val=1, max_val=ROUNDS)

            def add_back(before):
                for t in range(KD):
                    v.wait_ge(s("cmb_mm"), before + (t + 1))
                    v.tensor_tensor(h[:, t, :], h[:, t, :], bank(2 + t % 4)[:, 0:T], ALU.add).then_inc(s("comb_h"), 1)

            with v.Fori(0, n_rounds * E) as st:
                v.wait_ge(s("disp"), st * 3 + 3)
                for t in range(3):
                    n = P if t < 2 else NS
                    v.tensor_scalar(dispg[0:n, t, :], disp[0:n, t, :],
                                    gatex[0:n, bass.ds(st, 1), t:t + 1].rearrange("p a b -> p (a b)"), None, ALU.mult)\
                        .then_inc(s("dispg"), 1)
                v.wait_ge(s("gat_mm"), st + 1)
                v.wait_ge(s("dispg"), st * 3 + 3)
                dispatch(disp, st + 1)
                for c in range(XSET, PERX):
                    halve(c, st * PERX + (c + 1))
                    if c == XSET:
                        add_back(st * KD)
                    if c % 4 == 2 and 0 <= c // 4 - 1 < FCN:
                        f = c // 4 - 1
                        v.wait_ge(s("up_sil"), st * FCN + (f + 1))
                        v.wait_ge(s("up_mm"), st * NUP + (4 * f + 4))
                        if f >= 2:
                            v.wait_ge(s("ht_mm"), st * FCN + (f - 1))
                        v.tensor_tensor(hslot[f % 2], esil[f % 2], bank(2 * (f % 2) + 1)[:, :], ALU.mult)\
                            .then_inc(s("up_h"), 1)
                    if c in TURNED:
                        f = TURNED[c]
                        v.wait_ge(s("ht_hi"), st * FCN + (f + 1))
                        sl = slice(4 * f * C, 4 * (f + 1) * C)
                        v.tensor_tensor(hTl[:, sl], bank(4 + f % 2), hTh[:, sl].bitcast(F32), ALU.subtract)\
                            .then_inc(s("ht_lo"), 1)
                    if c == NUP + 3:
                        slots(st + 2)
                    if c == NUP + 7:
                        v.wait_ge(s("cmb_tr"), st + 1)
                        v.tensor_copy(comb, bank(5)[:, 0:T]).then_inc(s("comb_out"), 1)
                for c in range(XSET):
                    halve(c, st * PERX + (PERX + c + 1))
            add_back(n_rounds * E * KD)
            norm(5, h, T, [(u, GFIN)], rtb=frt, rsb=frs)

        @block.tensor
        def _(t_):
            pe = t_

            def norm(i, n, sqb=None):
                sqb = sq if sqb is None else sqb
                pe.wait_ge(s("ones_set"), 1)
                for k in range(KD):
                    pe.wait_ge(s("norm_sq"), KD * i + k + 1)
                    mm = pe.matmul(bank(0)[:, 0:n], ones[:, :], sqb[:, k * n:(k + 1) * n], start=(k == 0), stop=(k == KD - 1))
                mm.then_inc(s("norm_ss"), 1)

            def split_product(out, lhs, rhs, first, last):
                for i, (l, r) in enumerate(((0, 0), (0, 1), (1, 0))):
                    mm = pe.matmul(out, lhs[l], rhs[r], start=first and i == 0, stop=last and i == 2)
                return mm

            def weights(n, nk):
                pe.wait_ge(s("d_lo"), TURN[n] + 1)
                return [x.rearrange("p (k c) -> p k c", k=nk) for x in halves(n)]

            def tile(out, w, col, moving, n, ks, first=True, last=True, ready=None):
                for i, (kw, km) in enumerate(ks):
                    if ready is not None:
                        pe.wait_ge(s("m_lo"), ready(i))
                    mm = split_product(out, [x[:, kw, col:col + P] for x in w],
                                       [x[:, km * n:(km + 1) * n] for x in moving],
                                       first and i == 0, last and i == len(ks) - 1)
                return mm

            norm(0, NM)
            pe.wait_ge(s("norm_rt"), 1)
            square = [(k, k) for k in range(KD)]
            for g in range(16):
                l, i = g // 8, g % 8
                w = weights(g // 2, KD)
                if g == 5:
                    pe.wait_ge(s("mem_kv"), 1)
                    norm(1, T)
                if g == 8:
                    pe.wait_ge(s("norm_rt"), 2)
                if g >= 8:
                    pe.wait_ge(s("mem_kv"), g - 7)
                if g == 8:
                    pe.wait_ge(s("m_lo"), 2 * KD)
                if i < 4:
                    mm = tile(bank(i)[:, 0:NM], w, (i % 2) * P, (memh[l], meml[l]), NM, square,
                              ready=(lambda k: k + 1) if g == 0 else None)
                else:
                    x = i % 2
                    for k in range(KD):
                        mm = split_product(bank(i)[:, 0:256], [y[:, k * NM + x * P:k * NM + (x + 1) * P] for y in (memh[l], meml[l])],
                                           [y[:, k, :] for y in w], k == 0, k == KD - 1)
                mm.then_inc(s("mkv_mm"), 1)
            pe.wait_ge(s("mem_kv"), 16)
            pe.wait_ge(s("consts_loaded"), 48)
            pe.wait_ge(s("norm_u"), 3 * KD)
            wb = wba[:, :].rearrange("p (k c) -> p k c", k=KD)
            for t in range(3):
                n = P if t < 2 else NS
                for k in range(KD):
                    mm = pe.matmul(bank(1)[0:n, 16 * t:16 * t + 16], u[:, k, t * P:t * P + n], wb[:, k, :],
                                   start=(k == 0), stop=(k == KD - 1))
            mm.then_inc(s("ba_mm"), 1)
            pe.wait_ge(s("gba_out"), 2)
            pe.wait_ge(s("m_lo"), 3 * KD)
            for t in range(36):
                w = weights(AT["a_in", t // 2], KD)
                if t >= 8:
                    pe.wait_ge(s("ain_out"), t - 7)
                tile(bank(t % 8)[:, 0:T], w, (t % 2) * P, (uh[0], ul[0]), T, square).then_inc(s("ain_mm"), 1)
            pe.wait_ge(s("ain_out"), 36)
            pe.wait_ge(s("l2_sq"), 2 * H)
            pe.wait_ge(s("ones_set"), 5)
            for x in range(2 * H):
                mm = pe.matmul(bank(4)[0:2 * H, 0:ACTW], pick[:, 15 - x:31 - x], sqq[:, x * ACTW:(x + 1) * ACTW],
                               start=(x == 0), stop=(x == 2 * H - 1))
            mm.then_inc(s("l2_mm"), 1)
            pe.wait_ge(s("consts_loaded"), 48)
            pe.wait_ge(s("gate_done"), 2)
            gp = gg[:, 0:2, :].rearrange("p t c -> p (t c)")
            pe.matmul(bank(5)[:, 0:16], tri, gp, start=True, stop=True)
            pe.matmul(bank(5)[:, 16:32], ones[:, :], gp, start=True, stop=True)
            pe.matmul(bank(5)[:, 32:160], ones[0:NS, :], gd[0:NS, :], start=True, stop=True).then_inc(s("coef_mm"), 1)

            def row_to_all(out, rows, x, n):
                return pe.matmul(out, ident[0:n, x:x + 1].to_broadcast([n, P]), rows[0:n, :], start=True, stop=True)

            def l2_rows():
                pe.wait_ge(s("head_inv"), 1)
                pe.wait_ge(s("coef_dif"), 1)
                for x in range(2 * H):
                    if x >= 4:
                        pe.wait_ge(s("l2_done"), x - 3)
                    row_to_all(bank(4 + x % 4)[:, 0:ACTW], l2inv, x, 2 * H).then_inc(s("l2_mm"), 1)
                pe.wait_ge(s("l2_done"), 2 * H)

            def attention(l, between=lambda: None):
                Pr = Pr_of[l]
                for t in range(2):
                    for x in range(XH):
                        mm = pe.matmul(PP[t][:, x * NM:(x + 1) * NM], cq[:, x, t * P:(t + 1) * P],
                                       mk[l][:, x * NM:(x + 1) * NM], start=True, stop=True)
                    mm.then_inc(s("att_mm"), 1)
                between()
                for t in range(2):
                    pe.wait_ge(s("att_p"), 3 * l + t + 1)
                    for n in range(XH * MT):
                        mm = pe.transpose(PP[2 + t][:, n * P:(n + 1) * P], Pr[:, t * 1024 + n * P:t * 1024 + (n + 1) * P], ident)
                    mm.then_inc(s("att_tr"), 1)
                pe.wait_ge(s("att_pt"), 2 * l + 2)
                for x in range(XH):
                    for m in range(MT):
                        mm = pe.matmul(PP[0][:, x * SEQ:(x + 1) * SEQ], mv[l][:, m * 512 + x * P:m * 512 + (x + 1) * P],
                                       PrT[:, (x * MT + m) * SEQ:(x * MT + m + 1) * SEQ], start=(m == 0), stop=(m == MT - 1))
                mm.then_inc(s("att_o"), 1)
                pe.wait_ge(s("att_cat"), 2 * l + 1)
                kd, vd = f"kc{l}", f"vc{l}"
                pe.wait_ge(s("sat_in"), 3 * l + 1)
                for n in range(BH):
                    w = arrived(pe, AT[kd, n // 8]) if n % 8 == 0 else w
                    mm = pe.matmul(bank(1)[0:BH, 0:NM], q_diag[:, n * BH:(n + 1) * BH], w[:, (n % 8) * NM:(n % 8 + 1) * NM],
                                   start=(n == 0), stop=(n == BH - 1))
                    if n % 8 == 7:
                        mm.then_inc(s("cache_mm"), 1)
                pe.wait_ge(s("att_p"), 3 * l + 3)
                for m in range(MT):
                    mm = pe.transpose(bank(2)[:, m * BH:(m + 1) * BH], P32[0:BH, m * P:(m + 1) * P], ident[0:BH, 0:BH])
                mm.then_inc(s("att_tr"), 1)
                pe.wait_ge(s("sat_in"), 3 * l + 2)
                for n in range(BH):
                    b, x = n // XH, n % XH
                    w = arrived(pe, AT[vd, b // 2]) if n % 8 == 0 else w
                    for m in range(MT):
                        col = ((b % 2) * MT + m) * 512 + x * P
                        mm = pe.matmul(bank(3)[0:BH, 0:P], p_diag[:, (m * BH + n) * BH:(m * BH + n + 1) * BH],
                                       w[:, col:col + P], start=(n == 0 and m == 0), stop=(n == BH - 1 and m == MT - 1))
                    if n % 8 == 7:
                        mm.then_inc(s("cache_mm"), 1)
                pe.wait_ge(s("sat_in"), 3 * l + 3)
                pe.transpose(bank(0)[:, 0:BH], O32[0:BH, :], ident[0:BH, 0:BH]).then_inc(s("att_o"), 1)

            attention(0, l2_rows)

            for c in range(NCH):
                cols = slice(c * P, (c + 1) * P)
                pe.wait_ge(s("att_cat"), 2)
                if c:
                    pe.wait_ge(s("dl_cat"), c)
                    pe.wait_ge(s("S_done"), c)
                for x in range(H):
                    gcol = gg[:, c, x:x + 1].to_broadcast([P, P])
                    mm = pe.matmul(PP[0][:, x * P:(x + 1) * P], gcol, tri, start=True, stop=True)
                mm.then_inc(s("dl_grow"), 1)
                for w_, (m0, m1) in enumerate(((8, 0), (8, 8))):
                    for x in range(H):
                        mm = pe.matmul(PP[1 + w_][:, x * P:(x + 1) * P], act[:, m0 + x, cols], act[:, m1 + x, cols],
                                       start=True, stop=True)
                    mm.then_inc(s("dl_kk"), 1)
                for x in range(H):
                    mm = pe.matmul(PP[3][:, x * P:(x + 1) * P], gb[:, c, x:x + 1].to_broadcast([P, P]), ident,
                                   start=True, stop=True)
                mm.then_inc(s("dl_brow"), 1)
                if c == 0:
                    pe.wait_ge(s("conv_silu"), 24)
                pe.wait_ge(s("dl_pt"), c + 1)
                for x in range(H):
                    mm = pe.transpose(PP[1][:, x * P:(x + 1) * P], act[:, 16 + x, cols], ident)
                mm.then_inc(s("dl_tok"), 1)
                pe.wait_ge(s("dl_qd"), c + 1)
                for x in range(H):
                    mm = pe.transpose(PP[2][:, x * P:(x + 1) * P], act[:, 8 + x, cols], ident)
                mm.then_inc(s("dl_tok"), 1)
                pe.wait_ge(s("dl_kt"), c + 1)
                for lv in range(1, NLVL):
                    n0 = (c * (NLVL - 1) + lv - 1) * 2
                    u0 = (c * NLVL + lv) * 2
                    for g in range(2):
                        pe.wait_ge(s("dl_um"), u0 - 2 + g + 1)
                        if n0 + g >= 2:
                            pe.wait_ge(s("dl_t"), n0 + g - 1)
                        for x in range(4 * g, 4 * g + 4):
                            mm = pe.transpose(PP[0][:, x * P:(x + 1) * P], Ub[:, x * P:(x + 1) * P], ident)
                        mm.then_inc(s("dl_tt"), 1)
                    pe.wait_ge(s("dl_ml"), c * NLVL + lv + 1)
                    for g in range(2):
                        pe.wait_ge(s("dl_t"), n0 + g + 1)
                        if n0 + g >= 2:
                            pe.wait_ge(s("dl_x"), n0 + g - 1)
                        for x in range(4 * g, 4 * g + 4):
                            mm = pe.matmul(PP[1][:, x * P:(x + 1) * P], MLb[:, x * P:(x + 1) * P], Tb[:, x * P:(x + 1) * P],
                                           start=True, stop=True)
                        mm.then_inc(s("dl_xx"), 1)
                    for g in range(2):
                        pe.wait_ge(s("dl_x"), n0 + g + 1)
                        for x in range(4 * g, 4 * g + 4):
                            mm = pe.matmul(PP[2][:, x * P:(x + 1) * P], Xb[:, x * P:(x + 1) * P], Ub[:, x * P:(x + 1) * P],
                                           start=True, stop=True)
                        mm.then_inc(s("dl_du"), 1)
                pe.wait_ge(s("dl_um"), (c + 1) * NLVL * 2)
                R = vtok
                if c:
                    for x in range(H):
                        mm = pe.matmul(PP[0][:, x * P:(x + 1) * P], act[:, 8 + x, cols], Sb[:, x * P:(x + 1) * P],
                                       start=True, stop=True)
                    mm.then_inc(s("dl_ks"), 1)
                    pe.wait_ge(s("dl_r"), 1)
                    R = Xb
                for x in range(H):
                    mm = pe.matmul(PP[1][:, x * P:(x + 1) * P], Ub[:, x * P:(x + 1) * P], R[:, x * P:(x + 1) * P],
                                   start=True, stop=True)
                mm.then_inc(s("dl_uu"), 1)
                pe.wait_ge(s("dl_u"), c + 1)
                uu = Tb
                for x in range(H):
                    if c:
                        pe.matmul(PP[2][:, x * P:(x + 1) * P], Sb[:, x * P:(x + 1) * P], act[:, x, cols], start=True, stop=False)
                    mm = pe.matmul(PP[2][:, x * P:(x + 1) * P], uu[:, x * P:(x + 1) * P], PTb[:, x * P:(x + 1) * P],
                                   start=(c == 0), stop=True)
                mm.then_inc(s("dl_o"), 1)
                for x in range(H):
                    mm = pe.matmul(PP[3][:, x * P:(x + 1) * P], ktail[:, x * P:(x + 1) * P], uu[:, x * P:(x + 1) * P],
                                   start=True, stop=True)
                mm.then_inc(s("dl_ds"), 1)

            pe.wait_ge(s("dl_cat"), NCH)
            pe.wait_ge(s("S_done"), NCH)
            pe.wait_ge(s("sd_cols"), 1)
            pe.wait_ge(s("state_loaded"), 64)
            for n in range(DBH):
                g = n // 16
                mm = pe.matmul(bank(0)[0:32, g * P:(g + 1) * P], kq_diag[:, 32 * n:32 * (n + 1)], state[:, n * P:(n + 1) * P],
                               start=(n % 16 == 0), stop=(n % 16 == 15))
            mm.then_inc(s("sd_mm"), 1)
            pe.matmul(bank(1)[:, 0:64], ones[:, :], kqd, start=True, stop=True)
            pe.transpose(bank(4)[0:DBH, 0:P], t64, ident).then_inc(s("sd_rows"), 1)
            pe.wait_ge(s("sd_row"), 1)
            for g in range(4):
                mm = pe.transpose(bank(2)[:, g * 32:(g + 1) * 32], kqrow[0:32, g * P:(g + 1) * P], ident[0:32, 0:32])
            mm.then_inc(s("sd_mm"), 1)
            pe.wait_ge(s("sd_u"), 1)
            pe.transpose(bank(5)[0:DBH, 0:P], u64, ident).then_inc(s("sd_rows"), 1)
            pe.wait_ge(s("sd_row"), 3)
            for g in range(16):
                pe.wait_ge(s("sd_blk"), g + 1)
                if g >= 2:
                    pe.wait_ge(s("state_new"), g - 1)
                pe.matmul(bank(2 + g % 2), krow[0:DBH, :], ublk[g % 2][0:DBH, :], start=True, stop=True)\
                    .then_inc(s("sd_outer"), 1)
                if g == 1:
                    for x in range(H):
                        pe.wait_ge(s("on_sq"), x + 1)
                        mm = pe.matmul(bank(0)[0:H, 0:T], pick[:, 15 - x:15 - x + H], sq[:, x * T:(x + 1) * T],
                                       start=(x == 0), stop=(x == H - 1))
                    mm.then_inc(s("on_mm"), 1)
                x = g - 3
                if 0 <= x < H:
                    pe.wait_ge(s("head_inv"), 2)
                    if x >= 4:
                        pe.wait_ge(s("on_done"), x - 3)
                    row_to_all(bank(4 + x % 4)[:, 0:T], rs, x, H).then_inc(s("on_mm"), 1)
            pe.wait_ge(s("state_new"), 16)
            pe.wait_ge(s("on_done"), H)

            order = [(k, k) for k in (*range(H, H + XH), *range(H))]
            base_a = 3 * KD
            for t in range(KD):
                w = weights(AT["a_out", t], 12)
                tile(bank(t)[:, 0:T], w, 0, (cath[0], catl[0]), T, order,
                     ready=(lambda i: base_a + i + 1) if t == 0 else None).then_inc(s("aout_mm"), 1)
            pe.wait_ge(s("aout_h"), KD)
            norm(2, T)
            base_f = base_a + 12
            for f in range(FT):
                w = [x.rearrange("p k (g c) -> p k g c", g=2) for x in weights(AT["wi", f], KD)]
                if f >= 4:
                    pe.wait_ge(s("wi_prod"), f - 3)
                if f == 0:
                    pe.wait_ge(s("norm_rt"), 3)
                for g in range(2):
                    mm = tile(bank(2 * (f % 4) + g)[:, 0:T], [x[:, :, g, :] for x in w], 0, (uh[1], ul[1]), T, square,
                              ready=(lambda i: base_f + i + 1) if f == 0 and g == 0 else None)
                mm.then_inc(s("wi_mm"), 1)
            pe.wait_ge(s("wi_prod"), FT)
            for t in range(KD):
                for half in range(2):
                    w = weights(AT["wo", 2 * t + half], FT // 2)
                    ks = [(k, half * (FT // 2) + k) for k in range(FT // 2)]
                    for i, (kw, km) in enumerate(ks):
                        if t == 0:
                            pe.wait_ge(s("hid_lo"), km + 1)
                        mm = split_product(bank(t)[:, 0:T], [x[:, kw, :] for x in w],
                                           [x[:, km * T:(km + 1) * T] for x in (hidh, hidl)], km == 0, km == FT - 1)
                    mm.then_inc(s("wo_mm"), 1)
            pe.wait_ge(s("wo_h"), KD)
            norm(3, T)
            base_b = base_f + KD
            for t in range(12):
                w = weights(AT["b_in", t // 2], KD)
                if t >= 8:
                    pe.wait_ge(s("bin_out"), t - 7)
                if t == 0:
                    pe.wait_ge(s("norm_rt"), 4)
                tile(bank(t % 8)[:, 0:T], w, (t % 2) * P, (uh[2], ul[2]), T, square,
                     ready=(lambda i: base_b + i + 1) if t == 0 else None).then_inc(s("bin_mm"), 1)
            pe.wait_ge(s("bin_out"), 12)
            def pooled():
                pe.wait_ge(s("att_exp"), 9 + 2 * XH)
                w = arrived(pe, AT["pool", 0]).rearrange("p (g k c) -> p g k c", g=4, k=2)
                for t in range(8):
                    pe.wait_ge(s("pool_d"), t // 2 + 1)
                    for k in range(2):
                        mm = pe.matmul(bank(t)[:, 0:T], w[:, t // 2, k, (t % 2) * P:(t % 2 + 1) * P],
                                       pd[:, (t // 2) * 2 + k, :], start=(k == 0), stop=(k == 1))
                    mm.then_inc(s("pm_mm"), 1)
                pe.wait_ge(s("pm_cat"), 8)

            attention(1, pooled)
            pe.wait_ge(s("att_cat"), 4)
            base_o = base_b + KD
            for t in range(KD):
                w = weights(AT["b_out", t], 12)
                tile(bank(t)[:, 0:T], w, 0, (cath[1], catl[1]), T, [(k, k) for k in range(12)],
                     ready=(lambda i: base_o + i + 1) if t == 0 else None).then_inc(s("bout_mm"), 1)
            pe.wait_ge(s("bout_h"), KD)
            norm(4, T, sqb=fsq)
            rw = router[:, :].rearrange("p (k c) -> p k c", k=KD)
            for t in range(3):
                n = P if t < 2 else NS
                for k in range(KD):
                    if t == 0:
                        pe.wait_ge(s("norm_u"), 5 * KD + k + 1)
                        if k == 0:
                            pe.wait_ge(s("norm_rt"), 5)
                    mm = pe.matmul(bank(0)[0:n, E * t:E * t + E], u[:, k, t * P:t * P + n], rw[:, k, :],
                                   start=(k == 0), stop=(k == KD - 1))
            mm.then_inc(s("rt_mm"), 1)
            for t in range(3):
                n = P if t < 2 else NS
                for k in range(KD):
                    mm = pe.transpose(PP[1 + t][0:n, k * P:(k + 1) * P], u[:, k, t * P:t * P + n], ident)
                mm.then_inc(s("xt_mm"), 1)
            pe.wait_ge(s("rt_sub"), 1)
            sel = rr[2]
            pe.matmul(bank(0)[:, 0:8], stri, sel[:, 0:8], start=True, stop=True)
            pe.matmul(bank(0)[:, 8:16], stri, sel[:, 8:16], start=True, stop=False)
            pe.matmul(bank(0)[:, 8:16], ones[:, :], sel[:, 0:8], start=False, stop=True)
            pe.matmul(bank(0)[:, 16:24], stri, sel[:, 16:24], start=True, stop=False)
            pe.matmul(bank(0)[:, 16:24], ones[:, :], sel[:, 0:8], start=False, stop=False)
            pe.matmul(bank(0)[:, 16:24], ones[:, :], sel[:, 8:16], start=False, stop=True)
            pe.matmul(bank(0)[:, 24:32], ones[:, :], sel[:, 0:8], start=True, stop=False)
            pe.matmul(bank(0)[:, 24:32], ones[:, :], sel[:, 8:16], start=False, stop=False)
            pe.matmul(bank(0)[:, 24:32], ones[0:NS, :], sel[0:NS, 16:24], start=False, stop=True).then_inc(s("pos_mm"), 1)

            def gather():
                for k in range(KD):
                    for t in range(3):
                        n = P if t < 2 else NS
                        mm = pe.matmul(PP[1][:, k * C:(k + 1) * C], xtok[0:n, t, k * P:(k + 1) * P], disp[0:n, t, :],
                                       start=(t == 0), stop=(t == 2))
                mm.then_inc(s("gat_mm"), 1)

            pe.wait_ge(s("xt_out"), 3)
            pe.wait_ge(s("disp"), 3)
            gather()
            pe.wait_ge(s("steps_known"), 1)
            n_rounds = pe.value_load(nsteps_i[0:1, 0:1], min_val=1, max_val=ROUNDS)

            def combine(before, tiles):
                for t in tiles:
                    if t >= 4:
                        pe.wait_ge(s("comb_h"), before + (t - 3))
                    pe.matmul(bank(2 + t % 4)[:, 0:T], yslot[:, t * P:(t + 1) * P], comb, start=True, stop=True)\
                        .then_inc(s("cmb_mm"), 1)

            with pe.Fori(0, n_rounds * E) as st:
                def up(c):
                    f, g = c // 4, c // 2 % 2
                    pe.wait_ge(s("w_lo"), st * PERX + (c + 1))
                    w = [as_chunk(x[c % XSET][:, :], c) for x in (whi, wlo)]
                    for k in range(4):
                        kk = (c % 2) * 4 + k
                        mm = split_product(bank(2 * (f % 2) + g), [x[:, kk * C:(kk + 1) * C] for x in (xsh, xsl)],
                                           [x[:, k, :] for x in w], kk == 0, kk == KD - 1)
                    mm.then_inc(s("up_mm"), 1)

                def turn(f):
                    pe.wait_ge(s("up_h"), st * FCN + (f + 1))
                    if f >= 2:
                        pe.wait_ge(s("ht_lo"), st * FCN + (f - 1))
                    for x in range(4):
                        mm = pe.transpose(bank(4 + f % 2)[:, x * C:(x + 1) * C], hslot[f % 2][:, x * P:(x + 1) * P], ident)
                    mm.then_inc(s("ht_mm"), 1)

                pe.wait_ge(s("xs_lo"), st + 1)
                for c in range(NUP):
                    if c % 4 == 0 and c >= 8:
                        pe.wait_ge(s("up_h"), st * FCN + (c // 4 - 1))
                    if c == 4:
                        pe.wait_ge(s("comb_h"), st * KD + KD)
                    up(c)
                    if c == 1:
                        pe.wait_ge(s("y_out"), st + 1)
                        pe.wait_ge(s("comb_out"), st + 1)
                        combine(st * KD, range(4))
                    if c == 2:
                        combine(st * KD, range(4, KD))
                    if c % 4 == 3 and c > 3:
                        turn(c // 4 - 1)
                pe.wait_ge(s("disp"), st * 3 + 6)
                pe.wait_ge(s("up_h"), st * FCN + (FCN - 1))
                gather()
                turn(FCN - 1)
                for j in range(NDOWN):
                    c = NUP + j
                    pe.wait_ge(s("w_lo"), st * PERX + (c + 1))
                    pe.wait_ge(s("ht_lo"), st * FCN + (j // 2 + 1))
                    w = [as_chunk(x[c % XSET][:, :], c) for x in (whi, wlo)]
                    for k in range(2):
                        kk = 2 * j + k
                        for g in range(2):
                            mm = split_product(bank(6 + g), [x[:, kk * C:(kk + 1) * C] for x in (hTh, hTl)],
                                               [x[:, k, g * 512:(g + 1) * 512] for x in w], kk == 0, kk == KE - 1)
                    mm.then_inc(s("down_mm"), 1)
                    if j == 4:
                        pe.wait_ge(s("dispg"), st * 3 + 3)
                        pe.wait_ge(s("up_h"), st * FCN + FCN)
                        pe.wait_ge(s("ht_lo"), st * FCN + (FCN - 1))
                        for t in range(3):
                            n = P if t < 2 else NS
                            mm = pe.transpose(bank(5)[:, t * P:t * P + n], dispg[0:n, t, :], ident[0:n, 0:n])
                        mm.then_inc(s("cmb_tr"), 1)
            pe.wait_ge(s("y_out"), n_rounds * E + 1)
            pe.wait_ge(s("comb_out"), n_rounds * E + 1)
            pe.wait_ge(s("xs_lo"), n_rounds * E + 1)
            combine(n_rounds * E * KD, range(KD))
            pe.wait_ge(s("comb_h"), n_rounds * E * KD + KD)
            norm(5, T, sqb=fsq)


def kernel(**inputs):
    import concourse.bacc as bacc
    from concourse.bass_utils import run_bass_kernel_spmd

    f = {k: np.asarray(v) for k, v in inputs.items()}

    def fm(x):
        t, d = x.shape
        return x.T.reshape(d // P, P, t).transpose(1, 0, 2).reshape(P, -1)

    def tiles(w, per):
        k, n = w.shape
        return w.reshape(k // P, P, n // per, per).transpose(2, 1, 0, 3).reshape(n // per, P, -1)

    def col(g):
        return g.reshape(-1, P).T

    def rows(g):
        return np.broadcast_to(g.reshape(1, -1), (P, g.size))

    w_in = f["a_w_in"][0]
    split = CT * P + H * P
    ff = f["a_ffn_wi"][0]
    ffa = ff.reshape(KD, P, 2, FT, P).transpose(3, 1, 0, 2, 4).reshape(FT, P, -1)
    kc = f["cache_mem_k"]
    vc = f["cache_mem_v"]
    i = np.arange(P)
    J, I = i[:, None], i[None, :]
    lvl = [((I >> (l + 1)) == (J >> (l + 1))) & (((I >> l) & 1) == 1) & (((J >> l) & 1) == 0) for l in range(NLVL)]
    tie = (np.arange(E)[None, :] < np.arange(E)[:, None]).reshape(1, -1)
    cinv = np.stack([1.0 / np.minimum(np.arange(16) + 1, 2 << g) for g in range(4)]).reshape(1, -1)
    consts = np.concatenate([J == I, J <= I, J < I, np.where(J <= I, 0.0, -1e30)] + lvl
                            + [np.broadcast_to(I, (P, P)), np.broadcast_to(tie, (P, E * E)),
                               np.broadcast_to(cinv, (P, 64))], axis=1).astype(np.float32)
    gains = np.concatenate([col(f["a_norm1"]), col(f["a_norm2"]), col(f["b_norm1"]), col(f["b_norm2"]),
                            col(f["final_norm"]), col(f["m_norm"][0]), col(f["m_norm"][1]), col(f["b_pool_scale"]),
                            col(f["a_o_norm"]),
                            f["a_conv_w"][0].reshape(CW, CT, P).transpose(2, 1, 0).reshape(P, -1),
                            rows(f["a_a_log"]), rows(f["a_dt_bias"])], axis=1)
    arrays = {
        "x": fm(np.concatenate([f["x_prompt"][0], f["x_sample"][:, 0]], axis=0)),
        "mem": fm(f["mem_prompt"][0]),
        "gains": gains,
        "consts": consts,
        "wba": w_in[:, split:split + 16].reshape(KD, P, 16).transpose(1, 0, 2).reshape(P, -1),
        "router": f["b_router"][0].reshape(KD, P, E).transpose(1, 0, 2).reshape(P, -1),
        "convbuf": f["state_dn_conv"][0].reshape(NS, CW - 1, CT, P).transpose(3, 2, 0, 1).reshape(P, -1),
        "poolbuf": f["state_pool"][0].reshape(NS, PW, KD, P).transpose(3, 2, 0, 1).reshape(P, -1),
        "a_in": tiles(np.concatenate([w_in[:, :split], w_in[:, split + 16:]], axis=1), 256),
        "mkv": np.concatenate([tiles(f[n][l], 256) for l in range(2) for n in ("m_w_k", "m_w_v")]),
        "state": f["state_dn"][0].reshape(4, 16, P, P).transpose(0, 2, 1, 3).reshape(4, P, -1),
        "a_out": tiles(f["a_w_out"][0], P),
        "wi": ffa,
        "wo": f["a_ffn_wo"][0].reshape(2, FT // 2, P, KD, P).transpose(3, 0, 2, 1, 4).reshape(2 * KD, P, -1),
        "b_in": tiles(f["b_w_in"][0], 256),
        "pool": f["b_pool_w"].reshape(1, 4, 2, P, 256).transpose(0, 3, 1, 2, 4).reshape(1, P, -1),
        "b_out": tiles(f["b_w_out"][0], P),
        "wi_e": f["b_moe_wi"][0],
        "wo_e": f["b_moe_wo"][0],
    }
    for l in range(2):
        arrays[f"kc{l}"] = kc[l].reshape(4, 2, NM, XH, P).transpose(0, 4, 1, 3, 2).reshape(4, P, -1)
        arrays[f"vc{l}"] = vc[l].reshape(4, 2, MT, P, XH * P).transpose(0, 3, 1, 2, 4).reshape(4, P, -1)
    shapes = {"y": (P, KD * T), "S": (P, 1024), "conv": (P, 648), "pool": (P, 8 * 135), "mk": (2, P, 1024),
              "mv": (2, P, 1024), "state": (4, P, DCH)}
    nc = bacc.Bacc("TRN2", target_bir_lowering=False, num_devices=1)
    ins = {}
    sent = {}
    for name, a in arrays.items():
        a = np.ascontiguousarray(a)
        sent[f"in_{name}"] = a
        ins[name] = nc.dram_tensor(f"in_{name}", a.shape, F32, kind="ExternalInput").ap()
    outs = {n: nc.dram_tensor(f"out_{n}", sh, F32, kind="ExternalOutput").ap() for n, sh in shapes.items()}
    build(nc, ins, outs)
    r = run_bass_kernel_spmd(nc, [sent], core_ids=[0])
    o = {n: r.results[0][f"out_{n}"] for n in shapes}

    y = o["y"].reshape(P, KD, T).transpose(2, 1, 0).reshape(T, D)
    S = o["S"].reshape(P, H, P).transpose(1, 0, 2)[None, None]
    cv = o["conv"].reshape(P, CT, 27).transpose(2, 1, 0).reshape(27, CT * P)
    pl = o["pool"].reshape(P, KD, 135).transpose(2, 1, 0).reshape(135, D)
    mk = o["mk"].reshape(2, P, XH, NM).transpose(0, 3, 2, 1)[:, None]
    mv = o["mv"].reshape(2, P, MT, XH, P).transpose(0, 2, 1, 3, 4).reshape(2, 1, NM, XH, P)
    st = o["state"].reshape(4, P, 16, P).transpose(0, 2, 1, 3).reshape(1, NS, H, P, P)
    c = np.ascontiguousarray
    return (c(y[None, :SEQ]), c(y[SEQ:, None]), c(S), c(cv[None, None, :3]), c(pl[None, None, :PW]), c(mk), c(mv), c(st),
            c(cv[3:].reshape(1, NS, CW - 1, CT * P)), c(pl[PW:].reshape(1, NS, PW, D)))
```
